# Optimizing a Trainium2 kernel written in Bass

```python
import jax, jax.numpy as jnp
from jax import lax
import numpy as np

D_MODEL = 1024
BATCH = 1
SEQ = 1024
DEPTH = 1
DEC_BATCH = 1
DEC_SEQ = 32
PAST_LEN = 256

CHUNK = 64
QBLK = 128
H_A = 4
HD_A = 64
W_A = H_A * HD_A
H_I = 4
D_I = 32
TOPK_MAX = 256
H_B = 4
DK_B = 48
DV_B = 96
W_B = H_B * DV_B
GATE_RANK = 16
GLA_TAU = 16.0
H_C = 4
HD_C = 96
W_C = H_C * HD_C
CONV_W = 4
D_MIX = W_A + W_B + W_C
N_EXPERTS = 16
N_GROUPS = 4
EXPERTS_PER_GROUP = N_EXPERTS // N_GROUPS
TOP_K_EXPERTS = 2
D_EXPERT = 256
ALPHA = float((2 * DEPTH) ** 0.25)
BETA = float((8 * DEPTH) ** -0.25)
LN_EPS = 1e-5
_IN_SIZES = (W_A, W_A, W_A, H_I * D_I, D_I, H_I, H_B * DK_B, H_B * DK_B, W_B, W_B, GATE_RANK, W_C, W_C, W_C)
P_IN = sum(_IN_SIZES)
_IN_SPLITS = tuple(int(s) for s in np.cumsum(_IN_SIZES)[:-1])
F32 = jnp.float32

kernel_name = 'hybrid_dsa_gla_mlstm_moe_stream_step'

def layer_norm(x, g, b):
    xf = x.astype(F32)
    mu = jnp.mean(xf, axis=-1, keepdims=True)
    var = jnp.mean(jnp.square(xf - mu), axis=-1, keepdims=True)
    return ((xf - mu) * lax.rsqrt(var + LN_EPS) * g.astype(F32) + b.astype(F32)).astype(x.dtype)

def head_rms_norm(h, g):
    hf = h.astype(F32)
    hf = hf * lax.rsqrt(jnp.mean(hf * hf, axis=-1, keepdims=True) + LN_EPS)
    return hf.reshape(*h.shape[:-2], -1) * g.astype(F32)

def causal_dwconv(xc, w, b):
    out = lax.conv_general_dilated(xc, w.astype(xc.dtype)[:, None, :], window_strides=(1,), padding='VALID',
                                   dimension_numbers=('NWC', 'WIO', 'NWC'), feature_group_count=xc.shape[-1])
    return out + b.astype(out.dtype)

def _to_chunks(a, nc):
    return a.reshape(a.shape[0], nc, CHUNK, *a.shape[2:]).swapaxes(0, 1)

def _from_chunks(a):
    return a.swapaxes(0, 1).reshape(a.shape[1], a.shape[0] * a.shape[2], *a.shape[3:])

def _dsa_attend(q, qi, wi, qpos, k, v, ki, topk):
    S = k.shape[1]
    qchunk = qpos // CHUNK
    admissible = (jnp.arange(S)[None, :] // CHUNK) <= qchunk[:, None]
    rel = jax.nn.relu(jnp.einsum('bthd,bsd->bths', qi.astype(F32), ki.astype(F32)) * D_I ** -0.5)
    iscore = jnp.einsum('bth,bths->bts', wi.astype(F32) * H_I ** -0.5, rel)
    iscore = jnp.where(admissible[None], iscore, -jnp.inf)
    _, sel = lax.top_k(iscore, topk)
    valid = (sel // CHUNK) <= qchunk[None, :, None]
    gather = jax.vmap(lambda a, i: a[i])
    kg = gather(k, sel).astype(F32)
    vg = gather(v, sel).astype(F32)
    logits = jnp.einsum('bthd,btjhd->bthj', q.astype(F32), kg) * HD_A ** -0.5
    logits = jnp.where(valid[:, :, None, :], logits, -jnp.inf)
    p = jax.nn.softmax(logits, axis=-1)
    return jnp.einsum('bthj,btjhd->bthd', p, vg)

def dsa_prompt(q, qi, wi, k, v, ki):
    B, S = q.shape[:2]
    topk = min(TOPK_MAX, S // 4)
    def blk(i):
        sl = lambda a: lax.dynamic_slice_in_dim(a, i * QBLK, QBLK, axis=1)
        return _dsa_attend(sl(q), sl(qi), sl(wi), i * QBLK + jnp.arange(QBLK), k, v, ki, topk)
    out = lax.map(blk, jnp.arange(S // QBLK))
    return _from_chunks_q(out)

def _from_chunks_q(a):
    return a.swapaxes(0, 1).reshape(a.shape[1], a.shape[0] * a.shape[2], *a.shape[3:])

def dsa_sample(q, qi, wi, k, v, ki, ck, cv, cki):
    P, T = ck.shape[1], q.shape[1]
    kk = jnp.concatenate([ck.astype(F32), k.astype(F32)], axis=1)
    vv = jnp.concatenate([cv.astype(F32), v.astype(F32)], axis=1)
    kki = jnp.concatenate([cki.astype(F32), ki.astype(F32)], axis=1)
    topk = min(TOPK_MAX, (P + T) // 4)
    return _dsa_attend(q, qi, wi, P + jnp.arange(T), kk, vv, kki, topk)

def gla_chunk(q, k, v, lg, S0):
    L = q.shape[1]
    S0 = S0.astype(F32)
    b = jnp.cumsum(lg, axis=1)
    causal = jnp.tril(jnp.ones((L, L), bool))
    dec = jnp.exp(jnp.where(causal[None, :, :, None, None], b[:, :, None] - b[:, None, :], -jnp.inf))
    att = jnp.einsum('bthc,bshc,btshc->bhts', q, k, dec)
    o = jnp.einsum('bhts,bshv->bthv', att, v) + jnp.einsum('bthc,bhcv->bthv', q * jnp.exp(b), S0)
    bL = b[:, -1]
    S1 = jnp.exp(bL)[..., None] * S0 + jnp.einsum('bshc,bshv->bhcv', k * jnp.exp(bL[:, None] - b), v)
    return o, S1

def gla_prompt(q, k, v, lg):
    B, S = q.shape[:2]
    nc = S // CHUNK
    def step(St, inp):
        o, S1 = gla_chunk(*inp, St)
        return S1, o
    S_fin, o = lax.scan(step, jnp.zeros((B, H_B, DK_B, DV_B), F32),
                        (_to_chunks(q, nc), _to_chunks(k, nc), _to_chunks(v, nc), _to_chunks(lg, nc)))
    return _from_chunks(o), S_fin

def mlstm_chunk(q, k, v, ig, lf, C0, n0, m0):
    L = q.shape[1]
    C0, n0, m0 = C0.astype(F32), n0.astype(F32), m0.astype(F32)
    Fc = jnp.cumsum(lf, axis=1)
    a = Fc + m0[:, None]
    causal = jnp.tril(jnp.ones((L, L), bool))
    Dm = jnp.where(causal[None, :, :, None], Fc[:, :, None] - Fc[:, None, :] + ig[:, None, :], -jnp.inf)
    m = jnp.maximum(a, jnp.max(Dm, axis=2))
    w_in = jnp.exp(Dm - m[:, :, None])
    w_st = jnp.exp(a - m)
    qk = jnp.einsum('bthd,bshd->btsh', q, k) * w_in
    num = jnp.einsum('btsh,bshe->bthe', qk, v) + w_st[..., None] * jnp.einsum('bthd,bhde->bthe', q, C0)
    den = jnp.sum(qk, axis=2) + w_st * jnp.einsum('bthd,bhd->bth', q, n0)
    h = num / jnp.maximum(jnp.abs(den), jnp.exp(-m))[..., None]
    mL = m[:, -1]
    wL = jnp.exp(Dm[:, -1] - mL[:, None])
    gL = jnp.exp(a[:, -1] - mL)
    C1 = gL[..., None, None] * C0 + jnp.einsum('bsh,bshd,bshe->bhde', wL, k, v)
    n1 = gL[..., None] * n0 + jnp.einsum('bsh,bshd->bhd', wL, k)
    return h, C1, n1, mL

def mlstm_prompt(q, k, v, ig, lf):
    B, S = q.shape[:2]
    nc = S // CHUNK
    init = (jnp.zeros((B, H_C, HD_C, HD_C), F32), jnp.zeros((B, H_C, HD_C), F32), jnp.zeros((B, H_C), F32))
    def step(carry, inp):
        h, C1, n1, m1 = mlstm_chunk(*inp, *carry)
        return (C1, n1, m1), h
    (C, n, m), h = lax.scan(step, init, (_to_chunks(q, nc), _to_chunks(k, nc), _to_chunks(v, nc),
                                          _to_chunks(ig, nc), _to_chunks(lf, nc)))
    return _from_chunks(h), C, n, m

def token_mixer(x, w_in, w_gla_a2, b_gla_a, g_gla, conv_w, conv_b, w_mq, w_mk, w_if, b_if, g_mlstm, w_out, past):
    B, T, _ = x.shape
    (qa, ka, va, qi, ki, wi, qb, kb, vb, rb, glr, cc, vc, oc) = jnp.split(x @ w_in, _IN_SPLITS, axis=-1)
    heads = lambda a, h: a.reshape(B, T, h, -1)
    qa, ka, va, qi = heads(qa, H_A), heads(ka, H_A), heads(va, H_A), heads(qi, H_I)
    lg = (jax.nn.log_sigmoid((glr @ w_gla_a2 + b_gla_a).astype(F32)) / GLA_TAU).reshape(B, T, H_B, DK_B)
    qb = heads(qb, H_B).astype(F32) * DK_B ** -0.5
    kb = heads(kb, H_B).astype(F32)
    vb = heads(vb, H_B).astype(F32)
    if past is None:
        buf = jnp.zeros((B, CONV_W - 1, W_C), cc.dtype)
    else:
        ck, cv, cki, s_gla, c_m, n_m, m_m, buf = past
    xc = jnp.concatenate([buf.astype(cc.dtype), cc], axis=1)
    conv_new = xc[:, -(CONV_W - 1):]
    u = jax.nn.silu(causal_dwconv(xc, conv_w, conv_b).astype(F32)).reshape(B, T, H_C, HD_C)
    qc = jnp.einsum('bthd,hde->bthe', u, w_mq.astype(F32))
    kc = jnp.einsum('bthd,hde->bthe', u, w_mk.astype(F32)) * HD_C ** -0.5
    vch = heads(vc, H_C).astype(F32)
    gates = jnp.concatenate([qc.reshape(B, T, W_C), kc.reshape(B, T, W_C), vch.reshape(B, T, W_C)], axis=-1) \
        @ w_if.astype(F32) + b_if.astype(F32)
    ig = gates[..., :H_C]
    lf = jax.nn.log_sigmoid(gates[..., H_C:])
    if past is None:
        ya = dsa_prompt(qa, qi, wi, ka, va, ki)
        ob, s_new = gla_prompt(qb, kb, vb, lg)
        hc, c_new, n_new, m_new = mlstm_prompt(qc, kc, vch, ig, lf)
    else:
        ya = dsa_sample(qa, qi, wi, ka, va, ki, ck, cv, cki)
        ob, s_new = gla_chunk(qb, kb, vb, lg, s_gla)
        hc, c_new, n_new, m_new = mlstm_chunk(qc, kc, vch, ig, lf, c_m, n_m, m_m)
    yb = head_rms_norm(ob, g_gla) * jax.nn.silu(rb.astype(F32))
    yc = head_rms_norm(jax.nn.sigmoid(oc.astype(F32)).reshape(B, T, H_C, HD_C) * hc, g_mlstm)
    y = jnp.concatenate([ya.reshape(B, T, W_A), yb, yc], axis=-1) @ w_out.astype(F32)
    return y.astype(x.dtype), (ka, va, ki, s_new, c_new, n_new, m_new, conv_new)

def moe(x, w_router, b_router, w_gate, w_up, w_down):
    B, T, D = x.shape
    xf = x.reshape(B * T, D)
    s = jax.nn.sigmoid((xf @ w_router).astype(F32))
    sel = s + b_router.astype(F32)
    gscore = jnp.sum(lax.top_k(sel.reshape(-1, N_GROUPS, EXPERTS_PER_GROUP), TOP_K_EXPERTS)[0], axis=-1)
    gbest = jnp.argmax(gscore, axis=-1)
    in_group = (jnp.arange(N_EXPERTS) // EXPERTS_PER_GROUP)[None, :] == gbest[:, None]
    _, eidx = lax.top_k(jnp.where(in_group, sel, -jnp.inf), TOP_K_EXPERTS)
    wsel = jnp.take_along_axis(s, eidx, axis=-1)
    wsel = wsel / jnp.sum(wsel, axis=-1, keepdims=True)
    gate = jnp.einsum('nk,nke->ne', wsel, jax.nn.one_hot(eidx, N_EXPERTS, dtype=F32))
    out = jnp.zeros((B * T, D), F32)
    for e in range(N_EXPERTS):
        h = jax.nn.silu(xf @ w_gate[e]) * (xf @ w_up[e])
        out = out + gate[:, e:e + 1] * (h @ w_down[e]).astype(F32)
    return out.reshape(B, T, D).astype(x.dtype)

def trunk_layer(x, lw, fw, past):
    y, st = token_mixer(x, *lw, past)
    ln1_g, ln1_b, w_router, b_router, wg, wu, wd, ln2_g, ln2_b = fw
    x = layer_norm(ALPHA * x + y, ln1_g, ln1_b)
    x = layer_norm(ALPHA * x + moe(x, w_router, b_router, wg, wu, wd), ln2_g, ln2_b)
    return x, st

def setup_inputs(seed: int = 0) -> dict:
    key = jax.random.key(seed)
    ks = iter(jax.random.split(key, 40))
    nrm = lambda shape, scale: jax.random.normal(next(ks), shape, F32) * scale
    b_if = jnp.concatenate([nrm((DEPTH, H_C), 0.1),
                            jnp.linspace(3.0, 6.0, H_C, dtype=F32)[None] + nrm((DEPTH, H_C), 0.1)], axis=-1)
    return {
        'x_prompt': nrm((BATCH, SEQ, D_MODEL), 1.0),
        'x_sample': nrm((DEC_BATCH, DEC_SEQ, D_MODEL), 1.0),
        'cache_k': nrm((DEPTH, DEC_BATCH, PAST_LEN, H_A, HD_A), 1.0),
        'cache_v': nrm((DEPTH, DEC_BATCH, PAST_LEN, H_A, HD_A), 1.0),
        'cache_kidx': nrm((DEPTH, DEC_BATCH, PAST_LEN, D_I), 1.0),
        'state_gla': nrm((DEPTH, DEC_BATCH, H_B, DK_B, DV_B), 0.5),
        'state_mlstm_C': nrm((DEPTH, DEC_BATCH, H_C, HD_C, HD_C), 0.5),
        'state_mlstm_n': nrm((DEPTH, DEC_BATCH, H_C, HD_C), 0.5),
        'state_mlstm_m': nrm((DEPTH, DEC_BATCH, H_C), 0.5),
        'state_conv': nrm((DEPTH, DEC_BATCH, CONV_W - 1, W_C), 1.0),
        'ln0_g': 1.0 + nrm((D_MODEL,), 0.02),
        'ln0_b': nrm((D_MODEL,), 0.02),
        'w_in': nrm((DEPTH, D_MODEL, P_IN), D_MODEL ** -0.5),
        'w_gla_a2': nrm((DEPTH, GATE_RANK, H_B * DK_B), GATE_RANK ** -0.5),
        'b_gla_a': nrm((DEPTH, H_B * DK_B), 0.1),
        'g_gla': 1.0 + nrm((DEPTH, W_B), 0.02),
        'conv_w': nrm((DEPTH, CONV_W, W_C), CONV_W ** -0.5),
        'conv_b': nrm((DEPTH, W_C), 0.02),
        'w_mq': nrm((DEPTH, H_C, HD_C, HD_C), HD_C ** -0.5),
        'w_mk': nrm((DEPTH, H_C, HD_C, HD_C), HD_C ** -0.5),
        'w_if': nrm((DEPTH, 3 * W_C, 2 * H_C), 0.1 * (3 * W_C) ** -0.5),
        'b_if': b_if,
        'g_mlstm': 1.0 + nrm((DEPTH, W_C), 0.02),
        'w_out': nrm((DEPTH, D_MIX, D_MODEL), BETA * D_MIX ** -0.5),
        'ln1_g': 1.0 + nrm((DEPTH, D_MODEL), 0.02),
        'ln1_b': nrm((DEPTH, D_MODEL), 0.02),
        'w_router': nrm((D_MODEL, N_EXPERTS), D_MODEL ** -0.5),
        'b_router': nrm((N_EXPERTS,), 0.01),
        'w_exp_gate': nrm((DEPTH, N_EXPERTS, D_MODEL, D_EXPERT), D_MODEL ** -0.5),
        'w_exp_up': nrm((DEPTH, N_EXPERTS, D_MODEL, D_EXPERT), D_MODEL ** -0.5),
        'w_exp_down': nrm((DEPTH, N_EXPERTS, D_EXPERT, D_MODEL), BETA * D_EXPERT ** -0.5),
        'ln2_g': 1.0 + nrm((DEPTH, D_MODEL), 0.02),
        'ln2_b': nrm((DEPTH, D_MODEL), 0.02),
    }

def reference(x_prompt, x_sample, cache_k, cache_v, cache_kidx, state_gla, state_mlstm_C, state_mlstm_n,
              state_mlstm_m, state_conv, ln0_g, ln0_b, w_in, w_gla_a2, b_gla_a, g_gla, conv_w, conv_b, w_mq, w_mk,
              w_if, b_if, g_mlstm, w_out, ln1_g, ln1_b, w_router, b_router, w_exp_gate, w_exp_up, w_exp_down,
              ln2_g, ln2_b):
    xp = layer_norm(x_prompt, ln0_g, ln0_b)
    xs = layer_norm(x_sample, ln0_g, ln0_b)
    sp, ss = [], []
    for l in range(DEPTH):
        lw = (w_in[l], w_gla_a2[l], b_gla_a[l], g_gla[l], conv_w[l], conv_b[l], w_mq[l], w_mk[l],
              w_if[l], b_if[l], g_mlstm[l], w_out[l])
        fw = (ln1_g[l], ln1_b[l], w_router, b_router, w_exp_gate[l], w_exp_up[l], w_exp_down[l], ln2_g[l], ln2_b[l])
        xp, st_p = trunk_layer(xp, lw, fw, None)
        past = (cache_k[l], cache_v[l], cache_kidx[l], state_gla[l], state_mlstm_C[l], state_mlstm_n[l],
                state_mlstm_m[l], state_conv[l])
        xs, st_s = trunk_layer(xs, lw, fw, past)
        sp.append(st_p)
        ss.append(st_s)
    stk = lambda sts, i: jnp.stack([s[i] for s in sts])
    return (xp, xs,
            stk(sp, 0), stk(sp, 1), stk(sp, 2), stk(sp, 3), stk(sp, 4), stk(sp, 5), stk(sp, 6), stk(sp, 7),
            stk(ss, 0), stk(ss, 1), stk(ss, 2), stk(ss, 3), stk(ss, 4), stk(ss, 5), stk(ss, 6), stk(ss, 7))


_drawn_inputs = setup_inputs


def setup_inputs(seed=0):
    import zlib

    import numpy as np

    out = dict(_drawn_inputs(seed))
    spreads = {}
    factors = {'g_gla': 11.092, 'g_mlstm': 3.96, 'ln2_g': 7.52, 'ln2_b': 7.793}
    for name, (base, spread) in spreads.items():
        noise = np.random.default_rng([zlib.crc32(name.encode()), seed]).standard_normal(out[name].shape)
        drawn = base * np.exp(spread * noise) if base else spread * noise
        out[name] = __import__('jax').numpy.asarray(drawn.astype(out[name].dtype))
    for name, factor in factors.items():
        out[name] = (out[name] * factor).astype(out[name].dtype)
    return out
```

```python
import concourse.bass as bass
from concourse import mybir
from contextlib import ExitStack
import math

F32 = mybir.dt.float32
U32 = mybir.dt.uint32
I32 = mybir.dt.int32
ALU = mybir.AluOpType
ACT = mybir.ActivationFunctionType
AX = mybir.AxisListType

D = 1024
KD = D // 128
SEQ, SMP, PAST = 1024, 32, 256
NPT = SEQ // 128
NT = NPT + 1
CHUNK = 64
H = 4
HA, WA = 64, 256
DI = 32
TOPK_P = min(256, SEQ // 4)
TOPK_S = min(256, (PAST + SMP) // 4)
DK, DV, WB = 48, 96, 384
RANK, TAU = 16, 16.0
HC, WC, CW = 96, 384, 4
P_IN = 3 * WA + H * DI + DI + H + 2 * H * DK + 2 * WB + RANK + 3 * WC
NE, NG, EPG, FF = 16, 4, 4, 256
ALPHA = 2.0 ** 0.25
EPS = 1e-5
CAP = 160
TOKENS = SEQ + SMP
MORE = -(-(TOKENS - CAP) // 128)
SLOTS = CAP + 128 * MORE
CB = CAP - 128
NW = 4
NEG = -1.0e30
OUTSIDE = -3.0e38

CUTS = [0, 512, 932, 1316, 1700, 2100, 2484, 2868, P_IN]
NCUT = len(CUTS) - 1
WCUT = max(b - a for a, b in zip(CUTS, CUTS[1:]))


def tokens(t):
    return 128 if t < NPT else SMP


def keys(t):
    return 128 * (t + 1) if t < NPT else PAST + SMP


def selects(t):
    return keys(t) > (TOPK_P if t < NPT else TOPK_S)


def score_units(t):
    if not selects(t):
        return []
    return [(h, a, min(512, keys(t) - a)) for a in range(0, keys(t), 512) for h in range(H)]


def units_before(t):
    return sum(len(score_units(u)) for u in range(t))


def key_blocks(t):
    return -(-keys(t) // 128)


def block_groups(t):
    return [(b, min(4, key_blocks(t) - b)) for b in range(0, key_blocks(t), 4)]


def groups_before(t):
    return sum(len(block_groups(u)) for u in range(t)) * H


def semaphores(nc, ctx):
    sems = {}

    def S(name):
        if name not in sems:
            sems[name] = nc.alloc_semaphore(name)
        return sems[name]

    def give_back():
        nc.clear_and_free_semaphores(list(sems.values()))
        nc.all_engine_barrier()

    ctx.callback(give_back)

    return S


def build(nc, a, o):
    ctx = ExitStack()
    with ctx:
        x1_d = nc.dram_tensor("x1_rows", [TOKENS, D], F32, kind="Internal").ap()
        slot_d = nc.dram_tensor("slot_tokens", [NE * SLOTS, 1], I32, kind="Internal").ap()
        eo_d = nc.dram_tensor("expert_rows", [NE * CAP, D], F32, kind="Internal").ap()
        em_d = nc.dram_tensor("expert_rows_more", [NE * 128 * MORE, D], F32, kind="Internal").ap()

        def keep(name, shape, dt=F32):
            return ctx.enter_context(nc.sbuf_tensor(name, shape, dt))

        ident = keep("ident", [128, 128])
        expert = keep("expert", [128, NT, 2])
        before = keep("before", [128, NT, 2])
        gatew = keep("gatew", [128, NT, 2])
        ps = [ctx.enter_context(nc.psum_tensor(f"bank_pair{i}", [128, 1024], F32)) for i in range(4)]
        ones = keep("ones", [128, 128])
        chosen_sum = keep("chosen_sum", [128, NE])
        trunk(nc, a, o, ident, ones, chosen_sum, expert, before, gatew, ps, x1_d, slot_d)
        experts(nc, a, o, ident, ones, chosen_sum, expert, before, gatew, ps, x1_d, slot_d, eo_d, em_d)


def trunk(nc, a, o, ident, ones, chosen_sum, expert, before, gatew, ps, x1_d, slot_d):
    ctx = ExitStack()
    S = semaphores(nc, ctx)
    with ctx:
        def sb(name, shape, dt=F32):
            return ctx.enter_context(nc.sbuf_tensor(name, shape, dt))

        upper = sb("upper", [128, 128])
        upper_x = sb("upper_x", [128, 128])
        mid_p = sb("mid_p", [128, 128])
        mid_s = sb("mid_s", [SMP, SMP])
        half_p = sb("half_p", [128, 2])
        half_s = sb("half_s", [SMP, 2])
        minmask = sb("minmask", [128, 128])
        iota16 = sb("iota16", [128, NE])
        group16 = sb("group16", [128, NE])
        tok_id = sb("tok_id", [128, NT], I32)
        zeros_i = sb("zeros_i", [128, NE * SLOTS // 128], I32)
        w_out = sb("w_out", [128, KD, D])
        win = sb("win", [128, 2, KD, WCUT])
        ln0g, ln0b = sb("ln0g", [128, D]), sb("ln0b", [128, D])
        ln1g, ln1b = sb("ln1g", [128, D]), sb("ln1b", [128, D])
        ggla, gml = sb("ggla", [128, WB]), sb("gml", [128, WC])
        a2b = sb("a2b", [RANK + 1, H * DK])
        cw, cb = sb("cw", [HC, H, CW]), sb("cb", [HC, H])
        wmq, wmk = sb("wmq", [HC, H, HC]), sb("wmk", [HC, H, HC])
        wif = sb("wif", [HC, 3 * H, 2 * H])
        bif = sb("bif", [128, 2 * H])
        wr, br = sb("wr", [128, KD, NE]), sb("br", [128, NE])
        x0 = sb("x0", [128, 2, D])
        xT = sb("xT", [128, KD, 128])
        yT = xT
        zqk = sb("zqk", [128, 2 * WA])
        zix = sb("zix", [128, 2 * H * DI + H])
        zg = sb("zg", [128, 2, H, 64])
        zv = sb("zv", [128, WB])
        zr = sb("zr", [128, WB + RANK + 1])
        zc = sb("zc", [128, WC])
        zm = sb("zm", [128, H, HC + 1])
        zo = sb("zo", [128, WC])
        kT = sb("kT", [128, 2, SEQ])
        kiT = sb("kiT", [128, SEQ])
        va = sb("va", [128, NT, WA])
        kTs = sb("kTs", [128, 2, PAST + SMP])
        kiTs = sb("kiTs", [128, PAST + SMP])
        cach = sb("cach", [128, 2, WA + H * DI])
        vc = sb("vc", [128, 2, WA])
        qT = sb("qT", [128, 2, 2, 128])
        qiT = sb("qiT", [128, 128])
        score = sb("score", [128, 2, SEQ])
        rel = sb("rel", [128, 2, 512])
        top8 = sb("top8", [128, 8])
        lm = sb("lm", [128, SEQ])
        pT = rel[:].rearrange("p a (b n) -> p a b n", b=4)
        y = sb("y", [128, D])
        x1 = lm
        small = sb("small", [128, 384])
        glrT = sb("glrT", [RANK + 1, 128])
        lg = sb("lg", [128, H, 64])
        gtmp = sb("gtmp", [128, 2, H * DK])
        dec = sb("dec", [128, 2, H * 64])
        ecol = sb("ecol", [128, 2, 2])
        qk = sb("qk", [128, 2, H, 64])
        qkT = sb("qkT", [128, 4, 128])
        att = sb("att", [128, H, 128])
        gS = {g: sb(f"gS_{g}", [128, 2, DV]) for g in "ps"}
        gS2 = sb("gS2", [128, 2, DV])
        ccx = sb("ccx", [HC, H, CW - 1 + 128])
        xconv = att[0:HC]
        uT = sb("uT", [HC, H, 128])
        qcT, kcT = sb("qcT", [HC, H, 128]), sb("kcT", [HC, H, 128])
        kc = sb("kc", [128, H, HC])
        mi = sb("mi", [128, H, 128])
        mm = sb("mm", [128, H, 128])
        mw = sb("mw", [128, H, 128])
        mp = sb("mp", [128, H, 128])
        cS = {g: sb(f"cS_{g}", [HC, H, HC + 1]) for g in "ps"}
        m0 = {g: sb(f"m0_{g}", [128, H]) for g in "ps"}
        eg, eo = sb("eg", [128, WB]), sb("eo", [128, WC])
        scv = sb("scv", [HC, H, CW - 1])
        pexp = sb("pexp", [128, 4])
        idx8 = sb("idx8", [128, 8], U32)
        slots_i = sb("slots_i", [128, NT, 2], I32)

        Z = [ps[0][:, 0:512], ps[0][:, 512:1024]]
        T = [ps[1][:, 0:512], ps[1][:, 512:1024]]
        SC = ps[2]
        M = ps[3][:, 0:512]
        O = ps[3][:, 512:1024]
        gt = lambda i, n=4: small[:, i:i + n]

        block = ctx.enter_context(nc.Block())

        N_VEC = 22
        N_STATE = 1 + H + 2 + H

        def state_stores(sp, done, g):
            q = S(f"state_stored_{g}")
            sp.wait_ge(S("gla_state"), done)
            for h in range(H):
                sp.dma_start(o[f"gla_{g}"][0, 0, h], gS[g][64 * (h % 2):64 * (h % 2) + DK, h // 2, :]).then_inc(q, 16)
            sp.wait_ge(S("mlstm_state"), done)
            sp.dma_start(o[f"mC_{g}"][0, 0].rearrange("h d e -> d h e"), cS[g][:, :, 0:HC]).then_inc(q, 16)
            with nc.allow_non_contiguous_dma("a column of the state"):
                sp.dma_start(o[f"mn_{g}"][0, 0].rearrange("h d -> d h"), cS[g][:, :, HC]).then_inc(q, 16)
            sp.dma_start(o[f"mm_{g}"][0, 0:1], m0[g][0:1, :]).then_inc(q, 16)

        @block.sync
        def _(sp):
            def stores(t):
                n = tokens(t)
                kout, vout, iout, cout = (o["k_p"], o["v_p"], o["kidx_p"], o["conv_p"]) if t < NPT else (
                    o["k_s"], o["v_s"], o["kidx_s"], o["conv_s"])
                r0 = 128 * t if t < NPT else 0
                sp.wait_ge(S("z_copied"), NCUT * t + 2)
                sp.dma_start(kout[0, 0, r0:r0 + n].rearrange("s h d -> s (h d)"), zqk[0:n, WA:2 * WA]).then_inc(S("kv_stored"), 16)
                sp.dma_start(vout[0, 0, r0:r0 + n].rearrange("s h d -> s (h d)"), va[0:n, t, :]).then_inc(S("kv_stored"), 16)
                sp.dma_start(iout[0, 0, r0:r0 + n], zix[0:n, H * DI:H * DI + DI]).then_inc(S("kv_stored"), 16)
                if t >= NPT - 1:
                    sp.wait_ge(S("z_copied"), NCUT * t + 6)
                    sp.dma_start(cout[0, 0], zc[n - 3:n, :]).then_inc(S("conv_stored"), 16)

            for t in range(NT):
                n = tokens(t)
                if t >= 2:
                    sp.wait_ge(S("residual_done"), 2 * (t - 1))
                src = a["x_prompt"][0, 128 * t:128 * t + n] if t < NPT else a["x_sample"][0]
                sp.dma_start(x0[0:n, t % 2, :], src).then_inc(S("x_loaded"), 16)
                if t == 0:
                    sp.dma_start(ln0g[:], a["ln0_g"].partition_broadcast(128)).then_inc(S("ln0_loaded"), 16)
                    sp.dma_start(ln0b[:], a["ln0_b"].partition_broadcast(128)).then_inc(S("ln0_loaded"), 16)
                for j in range(NCUT):
                    i = NCUT * t + j
                    if i >= 2:
                        sp.wait_ge(S("z_done"), i - 1)
                    c0, c1 = CUTS[j], CUTS[j + 1]
                    sp.dma_start(win[:, i % 2, :, 0:c1 - c0],
                                 a["w_in"][0, :, c0:c1].rearrange("(k p) n -> p k n", p=128)).then_inc(S(f"win_loaded{i % 2}"), 16)
                stores(t)
                if t == 0:
                    sp.dma_start(w_out[:], a["w_out"][0].rearrange("(k p) n -> p k n", p=128)).then_inc(S("w_out_loaded"), 16)
            state_stores(sp, NPT, "p")
            state_stores(sp, NT, "s")
            sp.wait_ge(S("kv_stored"), 48 * NT)
            sp.wait_ge(S("conv_stored"), 32)
            sp.wait_ge(S("state_stored_p"), 16 * 7)
            sp.wait_ge(S("state_stored_s"), 16 * 7)

        grp = lambda t: "p" if t < NPT else "s"
        STAT0, MV0, RSTD0, NB0 = 0, 12, 14, 15
        STAT1, MV1, RSTD1, NB1 = 16, 28, 30, 31
        AMAX, ANEG, ASUM, AINV = 32, 36, 40, 44
        GMS, GRSTD = 52, 56
        GATES, LF, LNT, GI, DEN, EM, REC, MMS, MRSTD = 60, 68, 72, 76, 80, 84, 88, 92, 96
        RS, RSEL, RPAIR, RGS, RTOP, RF = 112, 128, 144, 168, 176, 184
        RIN, RSELM, RO, RSUM, RSCR = 192, 208, 224, 256, 272
        sm = lambda n, i, w=1: small[0:n, i:i + w]
        h4 = lambda bank, p, n: bank[0:p, :].rearrange("p (h n) -> p h n", h=H)[:, :, 0:n]

        @block.gpsimd
        def _(pool):
            G = nc.gpsimd
            n_step = [0]

            def step(ins):
                n_step[0] += 1
                ins.then_inc(S("pool_step"), 1)
                pool.wait_ge(S("pool_step"), n_step[0])

            def keep_where(out, base, pattern, mult, fill, op=ALU.is_ge):
                return G.affine_select(out=out, in_=out, compare_op=op, fill=fill, base=base,
                                       pattern=pattern, channel_multiplier=mult)

            G.memset(ident[:], 0.0)
            G.memset(ones[:], 1.0)
            G.memset(upper[:], 1.0)
            G.memset(upper_x[:], 1.0)
            G.memset(half_p[:], 1.0)
            G.memset(half_s[:], 1.0)
            step(G.memset(minmask[:], 0.0))
            keep_where(ident[:], 0, [[-1, 128]], 1, 1.0, ALU.not_equal)
            keep_where(upper[:], 0, [[1, 128]], -1, 0.0)
            keep_where(upper_x[:], -1, [[1, 128]], -1, 0.0)
            keep_where(minmask[:], 0, [[1, 128]], -1, NEG)
            for hf, L in ((half_p, 128), (half_s, SMP)):
                keep_where(hf[:, 0:1], L // 2 - 1, [[0, 1]], -1, 0.0)
                keep_where(hf[:, 1:2], -(L // 2), [[0, 1]], 1, 0.0)
            G.iota(tok_id[:], [[128, NT]], base=0, channel_multiplier=1)
            G.iota(iota16[:], [[1, NE]], base=0, channel_multiplier=0, allow_small_or_imprecise_dtypes=True)
            G.iota(group16[:], [[1, NG], [0, EPG]], base=0, channel_multiplier=0, allow_small_or_imprecise_dtypes=True)
            G.memset(pexp[:], -0.5)
            G.memset(zeros_i[:], 0)
            G.memset(zg[:], 0.0)
            G.memset(lg[:], 0.0)
            for g in "ps":
                G.memset(gS[g][:], 0.0)
            G.memset(cS["p"][:], 0.0)
            G.memset(m0["p"][:], 0.0)
            G.memset(ccx[:], 0.0)
            G.memset(zr[:, WB + RANK:], 1.0)
            G.memset(small[:], 0.0)
            for kept in (chosen_sum, expert, before, gatew):
                G.memset(kept[:], 0.0)
            step(G.memset(zm[:], 1.0))
            G.memset(small[:, RGS + 4:RGS + 8], NEG)
            G.tensor_scalar(mid_p[:], upper[:], half_p[:, 0:1], None, ALU.subtract)
            G.tensor_scalar(mid_s[:], upper[0:SMP, 0:SMP], half_s[:, 0:1], None, ALU.subtract).then_inc(S("consts"), 1)
            pool.wait_ge(S("consts"), 1)
            pool.dma_start(m0["s"][:], a["state_mlstm_m"][0, 0].partition_broadcast(128)).then_inc(S("states_loaded"), 16)
            for h in range(H):
                pool.dma_start(gS["s"][64 * (h % 2):64 * (h % 2) + DK, h // 2, :], a["state_gla"][0, 0, h]).then_inc(S("states_loaded"), 16)
            pool.dma_start(cS["s"][:, :, 0:HC], a["state_mlstm_C"][0, 0].rearrange("h d e -> d h e")).then_inc(S("states_loaded"), 16)
            with nc.allow_non_contiguous_dma("a column of the state"):
                pool.dma_start(cS["s"][:, :, HC], a["state_mlstm_n"][0, 0].rearrange("h d -> d h")).then_inc(S("states_loaded"), 16)
                for h in range(H):
                    pool.dma_start(scv[:, h, :], a["state_conv"][0, 0][:, HC * h:HC * h + HC].rearrange("j d -> d j")).then_inc(S("states_loaded"), 16)
            pool.dma_start(slot_d.rearrange("(p n) one -> p (n one)", p=128), zeros_i[:]).then_inc(S("slots_cleared"), 16)

            def norm_scale(n, mv, rstd, nb, out_sem):
                step(G.tensor_tensor(sm(n, rstd), sm(n, mv + 1), pexp[0:n, 0:1], ALU.pow))
                G.tensor_scalar(sm(n, nb), sm(n, mv), sm(n, rstd), -1.0, ALU.mult, ALU.mult).then_inc(S(out_sem), 1)

            def ln0(t):
                n = tokens(t)
                xt = x0[0:n, t % 2, :]
                pool.wait_ge(S("ln0_stats"), t + 1)
                norm_scale(n, MV0, RSTD0, NB0, "ln0_scale")
                pool.wait_ge(S("x_normed"), t + 1)
                if t == 0:
                    pool.wait_ge(S("ln0_loaded"), 32)
                step(G.tensor_tensor(xt, xt, ln0g[0:n], ALU.mult))
                G.tensor_tensor(xt, xt, ln0b[0:n], ALU.add).then_inc(S("x0_ready"), 1)

            def output(t):
                n = tokens(t)
                pool.wait_ge(S("ln1_stats"), t + 1)
                norm_scale(n, MV1, RSTD1, NB1, "ln1_scale")
                pool.wait_ge(S("x1_normed"), t + 1)
                step(G.tensor_tensor(x1[0:n], x1[0:n], ln1g[0:n], ALU.mult))
                G.tensor_tensor(x1[0:n], x1[0:n], ln1b[0:n], ALU.add).then_inc(S("x1_ready"), 1)
                pool.wait_ge(S("x1_ready"), t + 1)
                pool.dma_start(x1_d[128 * t:128 * t + n], x1[0:n]).then_inc(S("x1_stored"), 16)
                pool.wait_ge(S("slots_ready"), t + 1)
                if t == 0:
                    pool.wait_ge(S("slots_cleared"), 16)
                for k in range(2):
                    pool.indirect_dma_start(
                        out=slot_d, out_offset=bass.IndirectOffsetOnAxis(ap=slots_i[0:n, t, k:k + 1], axis=0),
                        in_=tok_id[0:n, t:t + 1], in_offset=None).then_inc(S("ids_stored"), 16)
                    pool.wait_ge(S("ids_stored"), 16 * (2 * t + k + 1))

            def recur(t):
                n = tokens(t)
                pool.wait_ge(S("eg_ready"), t + 1)
                step(G.tensor_tensor(eg[0:n], eg[0:n], zr[0:n, 0:WB], ALU.mult))
                G.tensor_tensor(eg[0:n], eg[0:n], ggla[0:n], ALU.mult).then_inc(S("eg_gained"), 1)
                pool.wait_ge(S("gla_ms"), t + 1)
                G.tensor_tensor(sm(n, GRSTD, H), sm(n, GMS, H), pexp[0:n, :], ALU.pow).then_inc(S("gla_scale"), 1)
                pool.wait_ge(S("yb_normed"), t + 1)
                pool.wait_ge(S("eg_gained"), t + 1)
                G.tensor_tensor(y[0:n, WA:WA + WB], y[0:n, WA:WA + WB], eg[0:n], ALU.mult).then_inc(S("yb_ready"), 1)
                pool.wait_ge(S("ml_ms"), t + 1)
                G.tensor_tensor(sm(n, MRSTD, H), sm(n, MMS, H), pexp[0:n, :], ALU.pow).then_inc(S("ml_scale"), 1)
                pool.wait_ge(S("yc_normed"), t + 1)
                G.tensor_tensor(y[0:n, WA + WB:], y[0:n, WA + WB:], gml[0:n], ALU.mult).then_inc(S("yc_ready"), 1)

            ln0(0)
            for t in range(NT + 1):
                if t >= 1:
                    if t == 1:
                        pool.wait_ge(S("vec_loaded"), 16 * N_VEC)
                    output(t - 1)
                if t < NT:
                    if t == 0:
                        pool.wait_ge(S("vec_loaded"), 16 * N_VEC)
                    recur(t)
                if t + 1 < NT:
                    ln0(t + 1)
            pool.wait_ge(S("x1_stored"), 16 * NT)
            pool.wait_ge(S("ids_stored"), 32 * NT)

        @block.scalar
        def _(act):
            A = nc.scalar
            n_step = [0]

            def step(ins):
                n_step[0] += 1
                ins.then_inc(S("act_step"), 1)
                act.wait_ge(S("act_step"), n_step[0])

            copy = lambda out, in_: A.activation(out, in_, ACT.Copy)
            bc = lambda v: v.partition_broadcast(128)
            small_loads = [
                (a2b[0:RANK, :], a["w_gla_a2"][0]), (a2b[RANK:RANK + 1, :], a["b_gla_a"]),
                (wmq[:], a["w_mq"][0].rearrange("h d e -> d h e")), (wmk[:], a["w_mk"][0].rearrange("h d e -> d h e")),
                (wif[:], a["w_if"][0].rearrange("(b d) g -> d b g", d=HC)), (bif[:], bc(a["b_if"][0])),
                (ggla[:], bc(a["g_gla"][0])), (gml[:], bc(a["g_mlstm"][0])),
                (ln1g[:], bc(a["ln1_g"][0])), (ln1b[:], bc(a["ln1_b"][0])),
                (wr[:], a["w_router"].rearrange("(k p) e -> p k e", p=128)), (br[:], bc(a["b_router"])),
                (cach[:, :, 0:WA], a["cache_k"][0, 0].rearrange("(b p) h d -> p b (h d)", p=128)),
                (vc[:], a["cache_v"][0, 0].rearrange("(b p) h d -> p b (h d)", p=128)),
            ]
            for h in range(H):
                small_loads.append((cw[:, h, :], a["conv_w"][0][:, HC * h:HC * h + HC].rearrange("j d -> d j")))
                small_loads.append((cach[:, :, WA + DI * h:WA + DI * h + DI], a["cache_kidx"][0, 0].rearrange("(b p) d -> p b d", p=128)))
            assert len(small_loads) == N_VEC
            with nc.allow_non_contiguous_dma("small vectors"):
                for dst, src in small_loads:
                    act.dma_start(dst, src).then_inc(S("vec_loaded"), 16)
                act.dma_start(cb[:], a["conv_b"][0].rearrange("(h d) -> d h", d=HC)).then_inc(S("cb_loaded"), 16)

            def project(t):
                n = tokens(t)
                xt = x0[0:n, t % 2, :]
                act.wait_ge(S("ln0_scale"), t + 1)
                A.activation(xt, xt, ACT.Identity, bias=sm(n, NB0), scale=sm(n, RSTD0)).then_inc(S("x_normed"), 1)
                if t >= 2:
                    act.wait_ge(S("route_ps"), t - 1)
                for g in range(2):
                    act.wait_ge(S("xT_ps"), 2 * t + g + 1)
                    copy(xT[:, 4 * g:4 * g + 4, 0:n], h4(T[g], 128, n)).then_inc(S("xT_ready"), 1)
                for j in range(NCUT):
                    i = NCUT * t + j
                    w = CUTS[j + 1] - CUTS[j]
                    zp = Z[i % 2][0:n, 0:w]
                    if t and j == 0:
                        act.wait_ge(S("kv_stored"), 48 * t)
                        act.wait_ge(S("yc_ready"), t)
                        act.wait_ge(S("ml_s_ps"), t)
                    if t >= NPT and j == 5:
                        act.wait_ge(S("conv_stored"), 16 * (t - NPT + 1))
                    act.wait_ge(S("z_done"), i + 1)
                    if j == 0:
                        last = copy(zqk[0:n], zp)
                    elif j == 1:
                        copy(va[0:n, t, :], zp[:, 0:WA])
                        copy(zix[0:n, 0:128], zp[:, WA:WA + 128])
                        copy(zix[0:n, 128:256].rearrange("p (h d) -> p h d", h=H),
                             zp[:, WA + 128:WA + 128 + DI].unsqueeze(1).to_broadcast([n, H, DI]))
                        last = copy(zix[0:n, 256:], zp[:, w - H:w])
                    elif j == 2:
                        last = copy(zg[0:n, :, :, 0:DK], zp.rearrange("p (a h d) -> p a h d", a=2, h=H))
                    elif j == 3:
                        last = copy(zv[0:n], zp)
                    elif j == 4:
                        last = copy(zr[0:n, 0:w], zp)
                    elif j == 5:
                        last = copy(zc[0:n], zp)
                    elif j == 6:
                        last = copy(zm[0:n, :, 0:HC], zp.rearrange("p (h d) -> p h d", h=H))
                    else:
                        last = copy(zo[0:n], zp)
                    last.then_inc(S("z_copied"), 1)
                    if j == 3:
                        act.wait_ge(S("aT_ps"), 2 * t + 1)
                        kdst, kidst, r0 = (kT, kiT, 128 * t) if t < NPT else (kTs, kiTs, PAST)
                        copy(qT[:, t % 2, :, 0:n], h4(T[0], 128, n)[:, 0:2])
                        copy(kdst[:, :, r0:r0 + n], h4(T[0], 128, n)[:, 2:4]).then_inc(S("aT_ready"), 1)
                        act.wait_ge(S("aT_ps"), 2 * t + 2)
                        copy(qiT[:, 0:n], T[1][:, 0:n])
                        copy(kidst[:, r0:r0 + n], T[1][:, 128:128 + n]).then_inc(S("aT_ready"), 1)
                if t == NPT:
                    for b in range(2):
                        act.wait_ge(S("cacheT_ps"), b + 1)
                        copy(kTs[:, :, 128 * b:128 * b + 128], h4(T[b], 128, 128)[:, 0:2])
                        copy(kiTs[:, 128 * b:128 * b + 128], T[b][:, 256:384]).then_inc(S("cacheT_ready"), 1)
                u0 = units_before(t)
                for v, (h, k0, w) in enumerate(score_units(t)):
                    act.wait_ge(S("iscore_ps"), u0 + v + 1)
                    if u0 + v >= 2:
                        act.wait_ge(S("rel_used"), u0 + v - 1)
                    if v == 0 and t >= 2:
                        act.wait_ge(S("pv_done"), groups_before(t - 1))
                    A.activation(rel[0:n, (u0 + v) % 2, 0:w], SC[0:n, 512 * ((u0 + v) % 2):512 * ((u0 + v) % 2) + w],
                                 ACT.Relu, scale=DI ** -0.5).then_inc(S("rel_ready"), 1)

            def output(t):
                n, K = tokens(t), keys(t)
                gb, ng = groups_before(t), len(block_groups(t))
                if units_before(min(t + 2, NT)):
                    act.wait_ge(S("rel_used"), units_before(min(t + 2, NT)))
                for h in range(H):
                    act.wait_ge(S("lm_ready"), H * t + h + 1)
                    A.activation(lm[0:n, 0:K], lm[0:n, 0:K], ACT.Exp, bias=sm(n, ANEG + h), scale=HA ** -0.5,
                                 accum_out=sm(n, ASUM + h)).then_inc(S("probs_ready"), 1)
                    for v, (b0, nb) in enumerate(block_groups(t)):
                        g = gb + ng * h + v
                        act.wait_ge(S("pT_ps"), g + 1)
                        if g >= 2:
                            act.wait_ge(S("pv_done"), g - 1)
                        full = [b for b in range(b0, b0 + nb) if K - 128 * b >= 128]
                        if full:
                            last = copy(pT[:, g % 2, 0:len(full), 0:n], h4(T[g % 2], 128, n)[:, 0:len(full)])
                        if len(full) < nb:
                            kb, b = K % 128, len(full)
                            last = copy(pT[0:kb, g % 2, b, 0:n], T[g % 2][0:kb, 128 * b:128 * b + n])
                        last.then_inc(S("pT_ready"), 1)
                for g in range(2):
                    act.wait_ge(S("yT_ps"), 2 * t + g + 1)
                    act.wait_ge(S("z_done"), NCUT * min(t + 2, NT))
                    copy(yT[:, 4 * g:4 * g + 4, 0:n], h4(T[g], 128, n)).then_inc(S("yT_ready"), 1)
                act.wait_ge(S("ln1_scale"), t + 1)
                A.activation(x1[0:n], x1[0:n], ACT.Identity, bias=sm(n, NB1), scale=sm(n, RSTD1)).then_inc(S("x1_normed"), 1)
                for g in range(2):
                    act.wait_ge(S("x1T_ps"), 2 * t + g + 1)
                    if g == 0:
                        act.wait_ge(S("wo_ps"), 2 * t + 2)
                    copy(yT[:, 4 * g:4 * g + 4, 0:n], h4(T[g], 128, n)).then_inc(S("x1T_ready"), 1)
                act.wait_ge(S("route_ps"), t + 1)
                A.activation(sm(n, RS, NE), M[0:n, 0:NE], ACT.Exp, scale=-1.0).then_inc(S("route_exp"), 1)

            def recur(t):
                n = tokens(t)
                m0t = m0[grp(t)]
                act.wait_ge(S("z_copied"), NCUT * (t + 1))
                if t:
                    act.wait_ge(S("yb_ready"), t)
                    act.wait_ge(S("hs_ready"), t)
                A.activation(eg[0:n], zr[0:n, 0:WB], ACT.Exp, scale=-1.0)
                A.activation(eo[0:n], zo[0:n], ACT.Exp, scale=-1.0).then_inc(S("gate_exp"), 1)
                act.wait_ge(S("ccT_ps"), t + 1)
                act.wait_ge(S("carry_done"), t + 1)
                copy(ccx[:, :, CW - 1:CW - 1 + n], h4(T[1], HC, n)).then_inc(S("ccx_ready"), 1)
                act.wait_ge(S("glrT_ps"), t + 1)
                copy(glrT[:, 0:n], T[0][0:RANK + 1, 0:n]).then_inc(S("glrT_ready"), 1)
                act.wait_ge(S("vT_ps"), t + 1)
                copy(mp[0:HC, :, 0:n], h4(T[1], HC, n)).then_inc(S("vT_ready"), 1)
                act.wait_ge(S("lg_in"), t + 1)
                step(A.activation(gtmp[0:n, 0, :], gtmp[0:n, 0, :], ACT.Exp))
                A.activation(gtmp[0:n, 0, :], gtmp[0:n, 0, :], ACT.Ln, bias=1.0).then_inc(S("gla_ln"), 1)
                act.wait_ge(S("conv_done"), t + 1)
                A.activation(uT[:, :, 0:n], xconv[:, :, 0:n], ACT.Exp, scale=-1.0).then_inc(S("u_exp"), 1)
                act.wait_ge(S("cum_ps"), t + 1)
                A.activation(dec[0:n, 0, :], O[0:n, 0:256], ACT.Exp, scale=1 / TAU)
                A.activation(dec[0:n, 1, :], O[0:n, 0:256], ACT.Exp, scale=-1 / TAU)
                A.activation(ecol[:], O[:, 256:260].rearrange("p (a b) -> p a b", a=2), ACT.Exp, scale=1 / TAU).then_inc(S("dec_ready"), 1)
                act.wait_ge(S("qkT_ps"), t + 1)
                copy(qkT[:, :, 0:n], h4(T[0], 128, n)).then_inc(S("qkT_ready"), 1)
                act.wait_ge(S("qc_ps"), t + 1)
                copy(qcT[:, :, 0:n], h4(SC[:, 512:1024], HC, n)).then_inc(S("qc_ready"), 1)
                act.wait_ge(S("kcT_ps"), t + 1)
                A.mul(kcT[:, :, 0:n], h4(SC[:, 0:512], HC, n), HC ** -0.5).then_inc(S("kcT_ready"), 1)
                act.wait_ge(S("kc_ps"), t + 1)
                A.mul(kc[0:n], Z[0][0:n, 0:WC].rearrange("p (h d) -> p h d", h=H), HC ** -0.5).then_inc(S("kc_ready"), 1)
                act.wait_ge(S("ml_nabs"), t + 1)
                step(A.activation(sm(n, LNT, H), sm(n, LNT, H), ACT.Exp))
                A.activation(sm(n, LNT, H), sm(n, LNT, H), ACT.Ln, bias=1.0).then_inc(S("ml_ln"), 1)
                act.wait_ge(S("gla_o_ps"), t + 1)
                A.activation(gtmp[0:n].rearrange("p a b -> p (a b)"), O[0:n, 0:WB], ACT.Square).then_inc(S("gla_sq"), 1)
                act.wait_ge(S("rows_ps"), t + 1)
                copy(mi[:, :, 0:n], h4(T[1], 128, n)).then_inc(S("irow_ready"), 1)
                act.wait_ge(S("fm_ready"), t + 1)
                if t == NPT:
                    act.wait_ge(S("states_loaded"), 16 * N_STATE)
                for h in range(H):
                    last = A.activation(mi[:, h, 0:n], mw[:, h, 0:n], ACT.Exp, bias=m0t[:, h:h + 1])
                last.then_inc(S("wst_ready"), 1)
                act.wait_ge(S("mcol_ps"), t + 1)
                A.activation(sm(n, EM, H), Z[1][0:n, 16:20], ACT.Exp, scale=-1.0).then_inc(S("mcol_exp"), 1)
                act.wait_ge(S("arg_ready"), t + 1)
                A.activation(mw[0:n, :, 0:n], mw[0:n, :, 0:n], ACT.Exp).then_inc(S("w_ready"), 1)
                act.wait_ge(S("hs_ready"), t + 1)
                A.activation(gtmp[0:n].rearrange("p a b -> p (a b)"), y[0:n, WA + WB:], ACT.Square).then_inc(S("ml_sq"), 1)

            for t in range(NT + 1):
                if t < NT:
                    project(t)
                if t >= 1:
                    output(t - 1)
                if t < NT:
                    recur(t)

        @block.vector
        def _(dve):
            V = nc.vector
            n_step = [0]

            def step(ins):
                n_step[0] += 1
                ins.then_inc(S("dve_step"), 1)
                dve.wait_ge(S("dve_step"), n_step[0])

            def tell(ins, name, value):
                ins.then_inc(S(name), 1)
                dve.wait_ge(S(name), value)

            TT, TS, STT = V.tensor_tensor, V.tensor_scalar, V.scalar_tensor_tensor

            def stats(src, n, stat, mv, out_sem):
                V.bn_stats(sm(n, stat, 6), src[:, 0:512])
                step(V.bn_stats(sm(n, stat + 6, 6), src[:, 512:1024]))
                step(V.bn_aggr(sm(n, mv, 2), sm(n, stat, 12).rearrange("p (a b) -> p a b", a=2)))
                TS(sm(n, mv + 1), sm(n, mv + 1), EPS, None, ALU.add).then_inc(S(out_sem), 1)

            def ln0(t):
                n = tokens(t)
                if t == 0:
                    dve.wait_ge(S("consts"), 1)
                dve.wait_ge(S("x_loaded"), 16 * (t + 1))
                if t:
                    dve.wait_ge(S("x_normed"), t)
                stats(x0[0:n, t % 2, :], n, STAT0, MV0, "ln0_stats")

            def index(t):
                n = tokens(t)
                u0 = units_before(t)
                for v, (h, k0, w) in enumerate(score_units(t)):
                    dve.wait_ge(S("rel_ready"), u0 + v + 1)
                    wi = zix[0:n, 256 + h:257 + h]
                    r, s = rel[0:n, (u0 + v) % 2, 0:w], score[0:n, t % 2, k0:k0 + w]
                    if h == 0:
                        if t >= 2:
                            dve.wait_ge(S("lm_ready"), H * (t - 1))
                        ins = TS(s, r, wi, None, ALU.mult)
                    else:
                        ins = STT(out=s, in0=r, scalar=wi, in1=s, op0=ALU.mult, op1=ALU.add)
                    tell(ins, "rel_used", u0 + v + 1)

            def select(t):
                n, K = tokens(t), keys(t)
                s = score[0:n, t % 2, 0:K]
                if t < NPT:
                    corner = score[0:CHUNK, t % 2, K - CHUNK:K]
                if not selects(t):
                    if t < NPT:
                        step(V.memset(s, 0.0))
                        step(V.memset(corner, NEG))
                    return
                if t < NPT:
                    step(V.memset(corner, OUTSIDE))
                rounds = (TOPK_P if t < NPT else TOPK_S) // 8
                base = n_step[0]
                with V.Fori(0, rounds) as r:
                    V.max(top8[0:n], s).then_inc(S("dve_step"), 1)
                    dve.wait_ge(S("dve_step"), r * 2 + (base + 1))
                    dve.sem_inc(S("dve_passed"), 1)
                    V.match_replace(s, top8[0:n], s, NEG).then_inc(S("dve_step"), 1)
                    dve.wait_ge(S("dve_step"), r * 2 + (base + 2))
                n_step[0] += 2 * rounds
                step(TS(s, s, NEG, NEG, ALU.not_equal, ALU.mult))

            def output(t):
                n, K = tokens(t), keys(t)
                ng = len(block_groups(t))
                for h in range(H):
                    dve.wait_ge(S("logits_ps"), H * t + h + 1)
                    if t and h == 0:
                        dve.wait_ge(S("x1_stored"), 16 * t)
                        dve.wait_ge(S("x1T_ps"), 2 * t)
                    if h or t:
                        dve.wait_ge(S("pT_ps"), groups_before(t) + ng * h)
                    step(V.tensor_tensor_reduce(lm[0:n, 0:K], SC[0:n, 0:K], score[0:n, t % 2, 0:K], 1.0, -3.0e38,
                                                ALU.add, ALU.max, sm(n, AMAX + h)))
                    TS(sm(n, ANEG + h), sm(n, AMAX + h), -HA ** -0.5, None, ALU.mult).then_inc(S("lm_ready"), 1)
                dve.wait_ge(S("probs_ready"), H * (t + 1))
                step(V.reciprocal(sm(n, AINV, H), sm(n, ASUM, H)))
                dve.wait_ge(S("pv_done"), groups_before(t + 1))
                TT(y[0:n, 0:WA].rearrange("p (h d) -> p h d", h=H), M[0:n, 0:WA].rearrange("p (h d) -> p h d", h=H),
                   sm(n, AINV, H).unsqueeze(2).to_broadcast([n, H, HA]), ALU.mult).then_inc(S("ya_ready"), 1)
                for c in range(2):
                    dve.wait_ge(S("wo_ps"), 2 * t + c + 1)
                    cs = slice(512 * c, 512 * c + 512)
                    tell(STT(out=x1[0:n, cs], in0=x0[0:n, t % 2, cs], scalar=ALPHA, in1=Z[c][0:n, :],
                             op0=ALU.mult, op1=ALU.add), "residual_done", 2 * t + c + 1)
                stats(x1[0:n], n, STAT1, MV1, "ln1_stats")
                route(t)

            def route(t):
                n = tokens(t)
                s, sel = sm(n, RS, NE), sm(n, RSEL, NE)
                g4 = lambda v: v.rearrange("p (g e) -> p g e", g=NG)
                dve.wait_ge(S("route_exp"), t + 1)
                step(TS(s, s, 1.0, None, ALU.add))
                step(V.reciprocal(s, s))
                step(TT(sel, s, br[0:n], ALU.add))
                pair, at = sm(n, RPAIR, 24).rearrange("p (g e) -> p g e", g=NG), 0
                for d in (1, 2, 3):
                    TT(pair[:, :, at:at + 4 - d], g4(sel)[:, :, 0:4 - d], g4(sel)[:, :, d:4], ALU.add)
                    at += 4 - d
                step(V.memset(sm(n, RF), 0.0))
                step(V.tensor_reduce(sm(n, RGS, NG), pair, AX.X, ALU.max))
                step(V.max(sm(n, RTOP, 8), sm(n, RGS, 8)))
                step(V.max_index(idx8[0:n], sm(n, RTOP, 8), sm(n, RGS, 8)))
                step(V.tensor_copy(sm(n, RF), idx8[0:n, 0:1]))
                step(TS(sm(n, RIN, NE), group16[0:n], sm(n, RF), None, ALU.is_equal))
                step(TT(sm(n, RSELM, NE), sel, sm(n, RIN, NE), ALU.mult))
                step(TS(sm(n, RIN, NE), sm(n, RIN, NE), -NEG, NEG, ALU.mult, ALU.add))
                step(TT(sm(n, RSELM, NE), sm(n, RSELM, NE), sm(n, RIN, NE), ALU.add))
                step(V.max(sm(n, RTOP, 8), sm(n, RSELM, NE)))
                step(V.max_index(idx8[0:n], sm(n, RTOP, 8), sm(n, RSELM, NE)))
                step(V.tensor_copy(sm(n, RF, 2), idx8[0:n, 0:2]))
                for k in range(2):
                    step(TS(sm(n, RO + NE * k, NE), iota16[0:n], sm(n, RF + k), None, ALU.is_equal))
                    step(V.tensor_tensor_reduce(sm(n, RSCR, NE), sm(n, RO + NE * k, NE), s, 1.0, 0.0, ALU.mult, ALU.add,
                                                gatew[0:n, t, k:k + 1]))
                tell(TT(sm(n, RSUM, NE), sm(n, RO, NE), sm(n, RO + NE, NE), ALU.add), "chosen", t + 1)
                step(TT(sm(n, RF + 2), gatew[0:n, t, 0:1], gatew[0:n, t, 1:2], ALU.add))
                step(V.reciprocal(sm(n, RF + 3), sm(n, RF + 2)))
                step(TS(gatew[0:n, t, :], gatew[0:n, t, :], sm(n, RF + 3), None, ALU.mult))
                dve.wait_ge(S("pos_ps"), t + 1)
                for k in range(2):
                    step(V.tensor_tensor_reduce(sm(n, RSCR, NE), M[0:n, 16:32], sm(n, RO + NE * k, NE), 1.0, 0.0,
                                                ALU.mult, ALU.add, before[0:n, t, k:k + 1]))
                V.tensor_copy(expert[0:n, t, :], sm(n, RF, 2))
                step(STT(out=sm(n, RF + 6, 2), in0=sm(n, RF, 2), scalar=float(SLOTS), in1=before[0:n, t, :], op0=ALU.mult, op1=ALU.add))
                step(V.tensor_copy(slots_i[0:n, t, :], sm(n, RF + 6, 2)))
                TT(chosen_sum[0:n], chosen_sum[0:n], sm(n, RSUM, NE), ALU.add).then_inc(S("slots_ready"), 1)

            def recur(t):
                n = tokens(t)
                g = grp(t)
                hd = lambda v: v.rearrange("p (h d) -> p h d", h=H)
                wide = lambda v, w: v.unsqueeze(2).to_broadcast([v.shape[0], H, w])
                if t == 0:
                    dve.wait_ge(S("vec_loaded"), 16 * N_VEC)
                    dve.wait_ge(S("cb_loaded"), 16)
                if t == NPT:
                    dve.wait_ge(S("states_loaded"), 16 * N_STATE)
                    tell(V.tensor_copy(ccx[:, :, 0:CW - 1], scv[:]), "carry_done", t + 1)
                else:
                    tell(V.tensor_copy(ccx[:, :, 0:CW - 1], ccx[:, :, 128:128 + CW - 1]), "carry_done", t + 1)
                dve.wait_ge(S("lgpre_ps"), t + 1)
                step(TS(gtmp[0:n, 1, :], M[0:n, 0:H * DK], 0.0, None, ALU.min))
                STT(out=gtmp[0:n, 0, :], in0=gtmp[0:n, 1, :], scalar=2.0, in1=M[0:n, 0:H * DK], op0=ALU.mult,
                    op1=ALU.subtract).then_inc(S("lg_in"), 1)
                dve.wait_ge(S("ccx_ready"), t + 1)
                for j in range(CW):
                    for h in range(H):
                        if j == 0:
                            ins = TS(xconv[:, h, 0:n], ccx[:, h, 0:n], cw[:, h, 0:1], cb[:, h:h + 1], ALU.mult, ALU.add)
                        else:
                            ins = STT(out=xconv[:, h, 0:n], in0=ccx[:, h, j:j + n], scalar=cw[:, h, j:j + 1],
                                      in1=xconv[:, h, 0:n], op0=ALU.mult, op1=ALU.add)
                    if j < CW - 1:
                        step(ins)
                tell(ins, "conv_done", t + 1)
                dve.wait_ge(S("gate_exp"), t + 1)
                TS(eg[0:n], eg[0:n], 1.0, None, ALU.add)
                step(TS(eo[0:n], eo[0:n], 1.0, None, ALU.add))
                V.reciprocal(eg[0:n], eg[0:n]).then_inc(S("eg_ready"), 1)
                step(V.reciprocal(eo[0:n], eo[0:n]))
                dve.wait_ge(S("gla_ln"), t + 1)
                TT(lg[0:n, :, 0:DK], hd(gtmp[0:n, 1, :]), hd(gtmp[0:n, 0, :]), ALU.subtract).then_inc(S("lg_ready"), 1)
                dve.wait_ge(S("u_exp"), t + 1)
                step(TS(uT[:, :, 0:n], uT[:, :, 0:n], 1.0, None, ALU.add))
                step(V.reciprocal(uT[:, :, 0:n], uT[:, :, 0:n]))
                TT(uT[:, :, 0:n], uT[:, :, 0:n], xconv[:, :, 0:n], ALU.mult).then_inc(S("u_ready"), 1)
                dve.wait_ge(S("dec_ready"), t + 1)
                v4 = lambda v: v.rearrange("p (h d) -> p h d", h=H)
                STT(out=qk[0:n, 0], in0=zg[0:n, 0], scalar=DK ** -0.5, in1=v4(dec[0:n, 0, :]), op0=ALU.mult, op1=ALU.mult)
                TT(qk[0:n, 1], zg[0:n, 1], v4(dec[0:n, 1, :]), ALU.mult).then_inc(S("qk_ready"), 1)
                TT(gS2[:], gS[g][:], ecol[:, :, 0:1].to_broadcast([128, 2, DV]), ALU.mult).then_inc(S("gS2_ready"), 1)
                dve.wait_ge(S("att_ps"), t + 1)
                TT(att[0:n, :, 0:n], h4(M, n, n), upper[0:n, 0:n].unsqueeze(1).to_broadcast([n, H, n]), ALU.mult).then_inc(S("att_ready"), 1)
                dve.wait_ge(S("gates_ps"), t + 1)
                step(TT(sm(n, GATES, 8), Z[1][0:n, 0:8], bif[0:n], ALU.add))
                step(TS(sm(n, LF, H), sm(n, GATES + H, H), 0.0, None, ALU.min))
                STT(out=sm(n, LNT, H), in0=sm(n, LF, H), scalar=2.0, in1=sm(n, GATES + H, H), op0=ALU.mult,
                    op1=ALU.subtract).then_inc(S("ml_nabs"), 1)
                dve.wait_ge(S("ml_ln"), t + 1)
                TT(sm(n, LF, H), sm(n, LF, H), sm(n, LNT, H), ALU.subtract).then_inc(S("lf_ready"), 1)
                dve.wait_ge(S("gla_s_ps"), t + 1)
                gps = Z[1][:, 128:128 + 2 * DV].rearrange("p (a v) -> p a v", a=2)
                step(TT(gS[g][:], gps, gS2[:], ALU.add))
                TT(gS[g][:], gS[g][:], ecol[:, :, 1:2].to_broadcast([128, 2, DV]), ALU.mult).then_inc(S("gla_state"), 1)
                dve.wait_ge(S("gla_sq"), t + 1)
                step(V.tensor_reduce(sm(n, GMS, H), hd(gtmp[0:n].rearrange("p a b -> p (a b)")), AX.X, ALU.add))
                TS(sm(n, GMS, H), sm(n, GMS, H), 1.0 / DV, EPS, ALU.mult, ALU.add).then_inc(S("gla_ms"), 1)
                dve.wait_ge(S("irow_ready"), t + 1)
                TT(sm(n, GI, H), sm(n, GATES, H), Z[1][0:n, 8:12], ALU.subtract)
                for h in range(H):
                    ins = V.tensor_tensor_scan(mm[:, h, 0:n], h4(Z[0], 128, n)[:, h], mi[:, h, 0:n], m0[g][:, h:h + 1], ALU.add, ALU.max)
                tell(ins, "mm_ready", t + 1)
                tell(TT(mw[:, :, 0:n], h4(T[0], 128, n), mm[:, :, 0:n], ALU.subtract), "fm_ready", t + 1)
                dve.wait_ge(S("gla_scale"), t + 1)
                if t:
                    dve.wait_ge(S("yT_ps"), 2 * t)
                TT(hd(y[0:n, WA:WA + WB]), hd(O[0:n, 0:WB]), wide(sm(n, GRSTD, H), DV), ALU.mult).then_inc(S("yb_normed"), 1)
                dve.wait_ge(S("wst_ready"), t + 1)
                for h in range(H):
                    ins = STT(out=mw[0:n, h, 0:n], in0=mw[0:n, h, 0:n], scalar=sm(n, GI + h), in1=minmask[0:n, 0:n],
                              op0=ALU.add, op1=ALU.min)
                ins.then_inc(S("arg_ready"), 1)
                dve.wait_ge(S("qk2_ps"), t + 1)
                TT(qcT[:, :, 0:n], qcT[:, :, 0:n], mi[0:HC, :, 0:n], ALU.mult).then_inc(S("qs_ready"), 1)
                dve.wait_ge(S("w_ready"), t + 1)
                TT(mp[0:n, :, 0:n], mw[0:n, :, 0:n], h4(SC[:, 0:512], n, n), ALU.mult)
                TT(kc[0:n], kc[0:n], mw[0:n, :, n - 1:n].to_broadcast([n, H, HC]), ALU.mult).then_inc(S("p_ready"), 1)
                num = SC[0:n, 512:512 + H * (HC + 1)].rearrange("p (h d) -> p h d", h=H)
                dve.wait_ge(S("num_ps"), t + 1)
                dve.wait_ge(S("mcol_exp"), t + 1)
                step(TS(sm(n, DEN, H), num[:, :, HC], -1.0, None, ALU.mult))
                step(TT(sm(n, DEN, H), sm(n, DEN, H), num[:, :, HC], ALU.max))
                step(TT(sm(n, DEN, H), sm(n, DEN, H), sm(n, EM, H), ALU.max))
                step(V.reciprocal(sm(n, REC, H), sm(n, DEN, H)))
                step(TT(hd(y[0:n, WA + WB:]), num[:, :, 0:HC], wide(sm(n, REC, H), HC), ALU.mult))
                tell(TT(y[0:n, WA + WB:], y[0:n, WA + WB:], eo[0:n], ALU.mult), "hs_ready", t + 1)
                step(TT(cS[g][:], cS[g][:], mi[0:HC, :, n - 1:n].to_broadcast([HC, H, HC + 1]), ALU.mult))
                V.tensor_copy(m0[g][:], mm[:, :, n - 1])
                dve.wait_ge(S("ml_s_ps"), t + 1)
                TT(cS[g][:], cS[g][:], M[0:HC, 0:H * (HC + 1)].rearrange("p (h d) -> p h d", h=H), ALU.add).then_inc(S("mlstm_state"), 1)
                dve.wait_ge(S("ml_sq"), t + 1)
                step(V.tensor_reduce(sm(n, MMS, H), hd(gtmp[0:n].rearrange("p a b -> p (a b)")), AX.X, ALU.add))
                TS(sm(n, MMS, H), sm(n, MMS, H), 1.0 / HC, EPS, ALU.mult, ALU.add).then_inc(S("ml_ms"), 1)
                dve.wait_ge(S("ml_scale"), t + 1)
                TT(hd(y[0:n, WA + WB:]), hd(y[0:n, WA + WB:]), wide(sm(n, MRSTD, H), HC), ALU.mult).then_inc(S("yc_normed"), 1)

            ln0(0)
            for t in range(NT + 1):
                if t < NT:
                    index(t)
                if t >= 1:
                    output(t - 1)
                if t < NT:
                    recur(t)
                if t + 1 < NT:
                    ln0(t + 1)
                if t < NT:
                    select(t)

        @block.tensor
        def _(pe):
            E = nc.tensor
            mmul = E.matmul
            n_step = [0]

            def step(ins):
                n_step[0] += 1
                ins.then_inc(S("pe_step"), 1)
                pe.wait_ge(S("pe_step"), n_step[0])

            tr = lambda out, in_: E.transpose(out, in_, ident[0:in_.shape[0], 0:in_.shape[0]])

            def features(src, n, ready_sem, ready, free_sem, free, done_sem):
                pe.wait_ge(S(ready_sem), ready)
                for g in range(2):
                    if free:
                        pe.wait_ge(S(free_sem), free)
                    for k in range(4):
                        last = tr(T[g][:, 128 * k:128 * k + n], src[:, 512 * g + 128 * k:512 * g + 128 * k + 128])
                    last.then_inc(S(done_sem), 1)

            def project(t):
                n = tokens(t)
                if t == 0:
                    pe.wait_ge(S("consts"), 1)
                features(x0[0:n, t % 2, :], n, "x0_ready", t + 1, "fm_ready", t, "xT_ps")
                pe.wait_ge(S("xT_ready"), 2 * t + 2)
                for j in range(NCUT):
                    i = NCUT * t + j
                    w = CUTS[j + 1] - CUTS[j]
                    pe.wait_ge(S(f"win_loaded{i % 2}"), 16 * (i // 2 + 1))
                    if i >= 2:
                        pe.wait_ge(S("z_copied"), i - 1)
                    if t and j == 0:
                        pe.wait_ge(S("mm_ready"), t)
                    if t and j == 1:
                        pe.wait_ge(S("gla_state"), t)
                        pe.wait_ge(S("mcol_exp"), t)
                    for k in range(KD):
                        last = mmul(Z[i % 2][0:n, 0:w], xT[:, k, 0:n], win[:, i % 2, k, 0:w], start=(k == 0), stop=(k == KD - 1))
                    last.then_inc(S("z_done"), 1)
                    if j == 3:
                        pe.wait_ge(S("z_copied"), NCUT * t + 2)
                        for b in range(4):
                            last = tr(T[0][:, 128 * b:128 * b + n], zqk[0:n, 128 * b:128 * b + 128])
                        last.then_inc(S("aT_ps"), 1)
                        tr(T[1][:, 0:n], zix[0:n, 0:H * DI])
                        last = tr(T[1][:, 128:128 + n], zix[0:n, 128:256])
                        last.then_inc(S("aT_ps"), 1)
                if t == NPT:
                    pe.wait_ge(S("aT_ready"), 2 * t + 2)
                    for b in range(2):
                        for c in range(2):
                            tr(T[b][:, 128 * c:128 * c + 128], cach[:, b, 128 * c:128 * c + 128])
                        last = tr(T[b][:, 256:384], cach[:, b, WA:])
                        last.then_inc(S("cacheT_ps"), 1)
                u0 = units_before(t)
                if score_units(t):
                    pe.wait_ge(S("aT_ready"), 2 * t + 2)
                    pe.wait_ge(S("w_ready"), t)
                    pe.wait_ge(S("p_ready"), t)
                    pe.wait_ge(S("hs_ready"), t)
                if t == NPT:
                    pe.wait_ge(S("cacheT_ready"), 2)
                ki = kiT if t < NPT else kiTs
                for v, (h, k0, w) in enumerate(score_units(t)):
                    u = u0 + v
                    if u >= 2:
                        pe.wait_ge(S("rel_ready"), u - 1)
                    mmul(SC[0:n, 512 * (u % 2):512 * (u % 2) + w], qiT[DI * h:DI * h + DI, 0:n], ki[DI * h:DI * h + DI, k0:k0 + w],
                         start=True, stop=True).then_inc(S("iscore_ps"), 1)

            def output(t):
                n, K = tokens(t), keys(t)
                kt = kT if t < NPT else kTs
                gb, ng = groups_before(t), len(block_groups(t))

                def logits(h):
                    if h == 0:
                        if units_before(min(t + 2, NT)):
                            pe.wait_ge(S("rel_ready"), units_before(min(t + 2, NT)))
                        pe.wait_ge(S("aT_ready"), 2 * t + 2)
                        pe.wait_ge(S("p_ready"), t + 1)
                        pe.wait_ge(S("hs_ready"), t + 1)
                    if t or h:
                        pe.wait_ge(S("lm_ready"), H * t + h)
                    b = HA * (h % 2)
                    for c in range(0, K, 512):
                        w = min(512, K - c)
                        last = mmul(SC[0:n, c:c + w], qT[b:b + HA, t % 2, h // 2, 0:n], kt[b:b + HA, h // 2, c:c + w], start=True, stop=True)
                    last.then_inc(S("logits_ps"), 1)

                logits(0)
                if t == NPT - 1 or t == NT - 1:
                    pass
                for h in range(H):
                    if h + 1 < H:
                        logits(h + 1)
                    pe.wait_ge(S("probs_ready"), H * t + h + 1)
                    if h == 0:
                        pe.wait_ge(S("mlstm_state"), t + 1)
                        pe.wait_ge(S("aT_ready"), 2 * min(t + 2, NT))
                        if t >= NPT - 1:
                            pe.wait_ge(S("cacheT_ready"), 2)
                    for v, (b0, nb) in enumerate(block_groups(t)):
                        g = gb + ng * h + v
                        if g >= 2:
                            pe.wait_ge(S("pT_ready"), g - 1)
                        for b in range(b0, b0 + nb):
                            kb = min(128, K - 128 * b)
                            last = tr(T[g % 2][0:kb, 128 * (b - b0):128 * (b - b0) + n], lm[0:n, 128 * b:128 * b + kb])
                        last.then_inc(S("pT_ps"), 1)
                        pe.wait_ge(S("pT_ready"), g + 1)
                        for b in range(b0, b0 + nb):
                            kb = min(128, K - 128 * b)
                            vv = va[0:kb, b, :] if t < NPT else (vc[0:kb, b, :] if b < 2 else va[0:kb, t, :])
                            last = mmul(M[0:n, HA * h:HA * h + HA], pT[0:kb, g % 2, b - b0, 0:n], vv[:, HA * h:HA * h + HA],
                                        start=(b == 0), stop=(128 * b + kb == K))
                        last.then_inc(S("pv_done"), 1)
                pe.wait_ge(S("yb_ready"), t + 1)
                pe.wait_ge(S("yc_ready"), t + 1)
                pe.wait_ge(S("pT_ready"), gb + ng * H)
                features(y[0:n], n, "ya_ready", t + 1, "x1T_ready", 2 * t, "yT_ps")
                if t == 0:
                    pe.wait_ge(S("w_out_loaded"), 16)
                pe.wait_ge(S("yT_ready"), 2 * t + 2)
                pe.wait_ge(S("z_copied"), NCUT * min(t + 2, NT))
                for c in range(2):
                    for k in range(KD):
                        last = mmul(Z[c][0:n, :], yT[:, k, 0:n], w_out[:, k, 512 * c:512 * c + 512], start=(k == 0), stop=(k == KD - 1))
                    last.then_inc(S("wo_ps"), 1)
                features(x1[0:n], n, "x1_ready", t + 1, "yT_ready", 2 * t + 2, "x1T_ps")
                pe.wait_ge(S("x1T_ready"), 2 * t + 2)
                pe.wait_ge(S("ya_ready"), t + 1)
                for k in range(KD):
                    last = mmul(M[0:n, 0:NE], yT[:, k, 0:n], wr[:, k, :], start=(k == 0), stop=(k == KD - 1))
                last.then_inc(S("route_ps"), 1)
                pe.wait_ge(S("chosen"), t + 1)
                mmul(M[0:n, 16:32], ones[:, 0:n], chosen_sum[:], start=True, stop=False)
                mmul(M[0:n, 16:32], upper_x[0:n, 0:n], sm(n, RSUM, NE), start=False, stop=True).then_inc(S("pos_ps"), 1)

            def recur(t):
                n = tokens(t)
                g = grp(t)
                mid, half = (mid_p, half_p) if t < NPT else (mid_s, half_s)
                if t == 0:
                    pe.wait_ge(S("vec_loaded"), 16 * N_VEC)
                if t == NPT:
                    pe.wait_ge(S("states_loaded"), 16 * N_STATE)
                pe.wait_ge(S("aT_ready"), 2 * t + 2)
                if t:
                    pe.wait_ge(S("x1T_ready"), 2 * t)
                    pe.wait_ge(S("residual_done"), 2 * t)
                pe.wait_ge(S("z_copied"), NCUT * (t + 1))
                for h in range(H):
                    last = tr(T[1][0:HC, 128 * h:128 * h + n], zc[0:n, HC * h:HC * h + HC])
                last.then_inc(S("ccT_ps"), 1)
                tr(T[0][0:RANK + 1, 0:n], zr[0:n, WB:WB + RANK + 1]).then_inc(S("glrT_ps"), 1)
                pe.wait_ge(S("glrT_ready"), t + 1)
                if t:
                    pe.wait_ge(S("slots_ready"), t)
                mmul(M[0:n, 0:H * DK], glrT[:, 0:n], a2b[:], start=True, stop=True).then_inc(S("lgpre_ps"), 1)
                pe.wait_ge(S("ccx_ready"), t + 1)
                for h in range(H):
                    last = tr(T[1][0:HC, 128 * h:128 * h + n], zm[0:n, h, 0:HC])
                last.then_inc(S("vT_ps"), 1)
                pe.wait_ge(S("lg_ready"), t + 1)
                if t:
                    pe.wait_ge(S("yb_normed"), t)
                lgf = lg[0:n].rearrange("p h d -> p (h d)")
                mmul(O[0:n, 0:256], mid[0:n, 0:n], lgf, start=True, stop=True)
                for p in range(2):
                    last = mmul(O[:, 256 + 2 * p:258 + 2 * p], lgf[:, 128 * p:128 * p + 128], half[0:n, :], start=True, stop=True)
                last.then_inc(S("cum_ps"), 1)
                pe.wait_ge(S("u_ready"), t + 1)
                if t:
                    pe.wait_ge(S("lm_ready"), H * t)
                if units_before(t + 1):
                    pe.wait_ge(S("rel_ready"), units_before(t + 1))
                for h in range(H):
                    last = mmul(SC[0:HC, 512 + 128 * h:512 + 128 * h + n], wmq[:, h, :], uT[:, h, 0:n], start=True, stop=True)
                last.then_inc(S("qc_ps"), 1)
                for h in range(H):
                    last = mmul(SC[0:HC, 128 * h:128 * h + n], wmk[:, h, :], uT[:, h, 0:n], start=True, stop=True)
                last.then_inc(S("kcT_ps"), 1)
                for h in range(H):
                    last = mmul(Z[0][0:n, HC * h:HC * h + HC], uT[:, h, 0:n], wmk[:, h, :], start=True, stop=True)
                last.then_inc(S("kc_ps"), 1)
                pe.wait_ge(S("qk_ready"), t + 1)
                qkf = qk[0:n].rearrange("p a h d -> p (a h d)")
                for b in range(4):
                    last = tr(T[0][:, 128 * b:128 * b + n], qkf[:, 128 * b:128 * b + 128])
                last.then_inc(S("qkT_ps"), 1)
                pe.wait_ge(S("qkT_ready"), t + 1)
                for h in (0, 2, 1, 3):
                    b = 64 * (h % 2)
                    if h == 1:
                        step(last)
                    last = mmul(M[0:n, 128 * h:128 * h + n], qkT[b:b + 64, 2 + h // 2, 0:n], qkT[b:b + 64, h // 2, 0:n], start=True, stop=True)
                last.then_inc(S("att_ps"), 1)
                pe.wait_ge(S("qc_ready"), t + 1)
                pe.wait_ge(S("kcT_ready"), t + 1)
                pe.wait_ge(S("vT_ready"), t + 1)
                srcs = [qcT, kcT, mp]
                for b in range(3 * H):
                    last = mmul(Z[1][0:n, 0:8], srcs[b // H][0:HC, b % H, 0:n], wif[:, b, :], start=(b == 0), stop=(b == 3 * H - 1))
                last.then_inc(S("gates_ps"), 1)
                pe.wait_ge(S("att_ready"), t + 1)
                pe.wait_ge(S("gS2_ready"), t + 1)
                for h in (0, 2, 1, 3):
                    b = 64 * (h % 2)
                    if h == 1 or (n < 128 and h):
                        step(last)
                    last = mmul(O[0:n, DV * h:DV * h + DV], att[0:n, h, 0:n], zv[0:n, DV * h:DV * h + DV], start=True, stop=False)
                    if n < 128 and b:
                        step(last)
                    last = mmul(O[0:n, DV * h:DV * h + DV], qkT[b:b + 64, h // 2, 0:n], gS2[b:b + 64, h // 2, :], start=False, stop=True)
                last.then_inc(S("gla_o_ps"), 1)
                pe.wait_ge(S("ml_nabs"), t + 1)
                for h in range(H):
                    b = 64 * (h % 2)
                    last = mmul(Z[1][b:b + 64, 128 + DV * (h // 2):128 + DV * (h // 2) + DV], qk[0:n, 1, h, :], zv[0:n, DV * h:DV * h + DV],
                                start=True, stop=True)
                last.then_inc(S("gla_s_ps"), 1)
                for h in range(H):
                    last = mmul(SC[0:n, 128 * h:128 * h + n], kcT[:, h, 0:n], qcT[:, h, 0:n], start=True, stop=True)
                last.then_inc(S("qk2_ps"), 1)
                pe.wait_ge(S("lf_ready"), t + 1)
                pe.wait_ge(S("kc_ready"), t + 1)
                pe.wait_ge(S("gla_state"), t + 1)
                for h in range(H):
                    lf, ig = (sm(n, c + h).to_broadcast([n, 128]) for c in (LF, GATES))
                    cs = slice(128 * h, 128 * h + n)
                    mmul(Z[0][:, cs], lf, ident[0:n, 0:n], start=True, stop=True)
                    mmul(T[1][:, cs], ig, ident[0:n, 0:n], start=True, stop=True)
                    mmul(T[0][:, cs], lf, upper[0:n, 0:n], start=True, stop=True)
                mmul(Z[1][0:n, 8:12], upper[0:n, 0:n], sm(n, LF, H), start=True, stop=True).then_inc(S("rows_ps"), 1)
                pe.wait_ge(S("mm_ready"), t + 1)
                for h in range(H):
                    last = mmul(Z[1][0:n, 16 + h:17 + h], mm[0:1, h, 0:n], ones[0:1, 0:1], start=True, stop=True)
                last.then_inc(S("mcol_ps"), 1)
                pe.wait_ge(S("p_ready"), t + 1)
                pe.wait_ge(S("qs_ready"), t + 1)
                for h in range(H):
                    o_ = SC[0:n, 512 + (HC + 1) * h:512 + (HC + 1) * (h + 1)]
                    mmul(o_, mp[0:n, h, 0:n], zm[0:n, h, :], start=True, stop=False)
                    last = mmul(o_, qcT[:, h, 0:n], cS[g][:, h, :], start=False, stop=True)
                last.then_inc(S("num_ps"), 1)
                for h in range(H):
                    last = mmul(M[0:HC, (HC + 1) * h:(HC + 1) * (h + 1)], kc[0:n, h, :], zm[0:n, h, :], start=True, stop=True)
                last.then_inc(S("ml_s_ps"), 1)

            for t in range(NT + 1):
                if t < NT:
                    project(t)
                if t >= 1:
                    output(t - 1)
                if t < NT:
                    recur(t)


def experts(nc, a, o, ident, ones, chosen_sum, expert, before, gatew, ps, x1_d, slot_d, eo_d, em_d):
    outer = ExitStack()
    with outer:
        at_i = outer.enter_context(nc.sbuf_tensor("at_i", [128, NT, 2], I32))
        more_i = outer.enter_context(nc.sbuf_tensor("more_i", [128, NT, 2], I32))
        w_at = outer.enter_context(nc.sbuf_tensor("w_at", [128, NT, 2], F32))
        w_more = outer.enter_context(nc.sbuf_tensor("w_more", [128, NT, 2], F32))
        mlps(nc, a, ident, ones, chosen_sum, expert, before, gatew, at_i, more_i, w_at, w_more, ps, x1_d, slot_d, eo_d, em_d)
        combine(nc, a, o, at_i, w_at, x1_d, eo_d)


def mlps(nc, a, ident, ones, chosen_sum, expert, before, gatew, at_i, more_i, w_at, w_more, ps, x1_d, slot_d, eo_d, em_d):
    ctx = ExitStack()
    S = semaphores(nc, ctx)
    with ctx:
        def sb(name, shape, dt=F32):
            return ctx.enter_context(nc.sbuf_tensor(name, shape, dt))

        wg = [sb(f"wg{j}", [128, KD, FF]) for j in range(NW)]
        wu = [sb(f"wu{j}", [128, KD, FF]) for j in range(NW)]
        wd = [sb(f"wd{j}", [128, FF // 128, D]) for j in range(NW)]
        ids = sb("ids", [128, NW, 2], I32)
        xg = [sb(f"xg{j}", [128, 2, D]) for j in range(2)]
        xgT = sb("xgT", [128, KD, CAP])
        gate = sb("gate", [128, CAP])
        hT = sb("hT", [128, 2, CAP])
        rows = [sb(f"rows{j}", [128, 2, D]) for j in range(2)]
        most = sb("most", [128, NE])
        in_cap = sb("in_cap", [128, NT, 2])
        pos_f = sb("pos_f", [128, NT, 2])
        most_i = sb("most_i", [128, 1], I32)
        T = [ps[1][:, 0:512], ps[1][:, 512:1024]]
        GU = [ps[0][:, 0:512], ps[0][:, 512:1024]]
        OA, OB = ps[2], ps[3]
        wsrc = {n: a[f"w_exp_{n}"][0].rearrange("e (k p) f -> p e k f", p=128) for n in ("gate", "up", "down")}
        slots_e = slot_d.rearrange("(e s) one -> s e one", e=NE)
        rows_e = eo_d.rearrange("(e s) d -> s e d", e=NE)
        more_e = em_d.rearrange("(e s) d -> s e d", e=NE)

        with nc.Block() as block:
            @block.sync
            def _(sp):
                sp.sem_inc(S("ob_ps"), NW)
                with sp.Fori(0, NE // NW) as i:
                    for j in range(NW):
                        e = i * NW + j
                        sp.wait_ge(S("ob_ps"), e + 1)
                        with nc.allow_non_contiguous_dma("slot ids"):
                            sp.dma_start(ids[:, j, 0:1], slots_e[0:128, bass.ds(e, 1), 0]).then_inc(S(f"ids_loaded{j}"), 16)
                            sp.dma_start(ids[0:CB, j, 1:2], slots_e[128:CAP, bass.ds(e, 1), 0]).then_inc(S(f"ids_loaded{j}"), 16)
                        sp.dma_start(wg[j][:], wsrc["gate"][:, bass.ds(e, 1)].rearrange("p one k f -> p (one k) f")).then_inc(S(f"w_loaded{j}"), 16)
                        sp.dma_start(wu[j][:], wsrc["up"][:, bass.ds(e, 1)].rearrange("p one k f -> p (one k) f")).then_inc(S(f"w_loaded{j}"), 16)
                        sp.dma_start(wd[j][:], wsrc["down"][:, bass.ds(e, 1)].rearrange("p one k f -> p (one k) f")).then_inc(S(f"w_loaded{j}"), 16)

            @block.gpsimd
            def _(pool):
                pool.sem_inc(S("xgT_ps"), 8)
                with pool.Fori(0, NE // NW) as i:
                    for j in range(NW):
                        e = i * NW + j
                        pool.wait_ge(S(f"ids_loaded{j}"), i * 32 + 32)
                        pool.sem_inc(S("pool_passed"), 1)
                        pool.wait_ge(S("xgT_ps"), e * 4 + 4)
                        pool.sem_inc(S("pool_passed"), 1)
                        for b, nb in ((0, 128), (1, CB)):
                            pool.indirect_dma_start(
                                out=xg[j % 2][0:nb, b, :], out_offset=None, in_=x1_d,
                                in_offset=bass.IndirectOffsetOnAxis(ap=ids[0:nb, j, b:b + 1], axis=0)).then_inc(S(f"xg_loaded{j % 2}"), 16)

            @block.scalar
            def _(act):
                A = nc.scalar
                act.sem_inc(S("xgT_copied"), 2)
                act.sem_inc(S("gu_ps"), 2)
                for p in range(2):
                    act.sem_inc(S(f"rows_stored{p}"), 32)
                act.sem_inc(S("oa_copied"), 1)
                with act.Fori(0, NE // NW) as i:
                    for j in range(NW):
                        e = i * NW + j
                        for u in range(4):
                            act.wait_ge(S("xgT_ps"), e * 4 + (u + 9))
                            if u == 0:
                                act.wait_ge(S("gu_ps"), e * 2 + 2)
                            A.activation(xgT[:, 2 * u:2 * u + 2, :], T[u % 2][:, 0:2 * CAP].rearrange("p (k n) -> p k n", k=2),
                                         ACT.Copy).then_inc(S("xgT_copied"), 1)
                        for f in range(2):
                            act.wait_ge(S("gu_ps"), e * 2 + (f + 3))
                            act.wait_ge(S("h_ready"), e * 2 + (f + 2))
                            A.activation(gate[:], GU[f][:, 0:CAP], ACT.Silu).then_inc(S("gate_ready"), 1)
                        act.wait_ge(S("oa_ps"), e + 1)
                        act.wait_ge(S(f"rows_stored{j % 2}"), i * (16 * NW) + 32 * (j // 2 + 1))
                        A.activation(rows[j % 2][:, 0, :], OA[:], ACT.Copy).then_inc(S("oa_copied"), 1)
                        act.wait_ge(S("oa_copied"), e + 2)
                        act.dma_start(rows_e[0:128, bass.ds(e, 1), :].rearrange("s one d -> s (one d)"), rows[j % 2][:, 0, :]).then_inc(S(f"rows_stored{j % 2}"), 16)
                        act.wait_ge(S("ob_copied"), e + 2)
                        act.dma_start(rows_e[128:CAP, bass.ds(e, 1), :].rearrange("s one d -> s (one d)"), rows[j % 2][0:CB, 1, :]).then_inc(S(f"rows_stored{j % 2}"), 16)
                for p in range(2):
                    act.wait_ge(S(f"rows_stored{p}"), 32 + 32 * NE // 2)

            @block.vector
            def _(dve):
                V = nc.vector
                dve.sem_inc(S("h_ready"), 2)
                dve.sem_inc(S("ob_copied"), 1)
                dve.wait_ge(S("counts_ps"), 1)
                V.tensor_reduce(most[:, 0:1], OB[:, 0:NE], AX.X, ALU.max).then_inc(S("most_ready"), 1)
                dve.wait_ge(S("most_ready"), 1)
                V.tensor_copy(most_i[:], most[:, 0:1]).then_inc(S("most_ready"), 1)
                n_step = [0]

                def step(ins):
                    n_step[0] += 1
                    ins.then_inc(S("place_step"), 1)
                    dve.wait_ge(S("place_step"), n_step[0])

                step(V.tensor_scalar(in_cap[:], before[:], float(CAP), None, ALU.is_lt))
                step(V.scalar_tensor_tensor(out=pos_f[:], in0=expert[:], scalar=float(CAP), in1=before[:], op0=ALU.mult, op1=ALU.add))
                step(V.tensor_tensor(pos_f[:], pos_f[:], in_cap[:], ALU.mult))
                step(V.tensor_copy(at_i[:], pos_f[:]))
                step(V.tensor_tensor(w_at[:], gatew[:], in_cap[:], ALU.mult))
                V.tensor_tensor(w_more[:], gatew[:], w_at[:], ALU.subtract)
                step(V.tensor_scalar(in_cap[:], before[:], float(CAP), None, ALU.is_ge))
                step(V.scalar_tensor_tensor(out=pos_f[:], in0=expert[:], scalar=float(128 * MORE), in1=before[:], op0=ALU.mult, op1=ALU.add))
                step(V.tensor_scalar(pos_f[:], pos_f[:], -float(CAP), None, ALU.add))
                step(V.tensor_tensor(pos_f[:], pos_f[:], in_cap[:], ALU.mult))
                step(V.tensor_copy(more_i[:], pos_f[:]))
                with dve.Fori(0, NE // NW) as i:
                    for j in range(NW):
                        e = i * NW + j
                        for f in range(2):
                            dve.wait_ge(S("gate_ready"), e * 2 + (f + 1))
                            if f == 0:
                                dve.wait_ge(S("ob_ps"), e + NW)
                            V.tensor_tensor(hT[:, f, :], gate[:], GU[f][:, CAP:2 * CAP], ALU.mult).then_inc(S("h_ready"), 1)
                        dve.wait_ge(S("ob_ps"), e + (NW + 1))
                        dve.wait_ge(S(f"rows_stored{j % 2}"), i * (16 * NW) + 32 * (j // 2 + 1))
                        V.tensor_copy(rows[j % 2][0:CB, 1, :], OB[0:CB, :]).then_inc(S("ob_copied"), 1)

            @block.tensor
            def _(pe):
                E = nc.tensor
                E.matmul(OB[:, 0:NE], ones[:], chosen_sum[:], start=True, stop=True).then_inc(S("counts_ps"), 1)
                pe.wait_ge(S("most_ready"), 2)
                with pe.Fori(0, NE // NW) as i:
                    for j in range(NW):
                        e = i * NW + j
                        pe.wait_ge(S(f"xg_loaded{j % 2}"), i * (32 * NW // 2) + 32 * (j // 2 + 1))
                        for u in range(4):
                            pe.wait_ge(S("xgT_copied"), e * 4 + (u + 1))
                            for k in (2 * u, 2 * u + 1):
                                c = CAP * (k % 2)
                                E.transpose(T[u % 2][:, c:c + 128], xg[j % 2][:, 0, 128 * k:128 * k + 128], ident[:])
                                last = E.transpose(T[u % 2][:, c + 128:c + CAP], xg[j % 2][0:CB, 1, 128 * k:128 * k + 128], ident[0:CB, 0:CB])
                            last.then_inc(S("xgT_ps"), 1)
                        pe.wait_ge(S(f"w_loaded{j}"), i * 48 + 48)
                        pe.wait_ge(S("xgT_copied"), e * 4 + 6)
                        for f in range(2):
                            pe.wait_ge(S("h_ready"), e * 2 + (f + 1))
                            for m, w in ((0, wg[j]), (1, wu[j])):
                                for k in range(KD):
                                    last = E.matmul(GU[f][:, CAP * m:CAP * m + CAP], w[:, k, 128 * f:128 * f + 128], xgT[:, k, :],
                                                    start=(k == 0), stop=(k == KD - 1))
                            last.then_inc(S("gu_ps"), 1)
                        for f in range(2):
                            pe.wait_ge(S("h_ready"), e * 2 + (f + 3))
                            for out, c0, nb, sem in ((OA, 0, 128, "oa"), (OB, 128, CB, "ob")):
                                if f == 0:
                                    pe.wait_ge(S(sem + "_copied"), e + 1)
                                for c in range(2):
                                    last = E.matmul(out[0:nb, 512 * c:512 * c + 512], hT[:, f, c0:c0 + nb], wd[j][:, f, 512 * c:512 * c + 512],
                                                    start=(f == 0), stop=(f == 1))
                                if f == 1:
                                    last.then_inc(S(sem + "_ps"), 1)

        with nc.Block() as block:
            F = lambda name: S("more_" + name)

            @block.sync
            def _(sp):
                sp.sem_inc(F("o_ps"), 1)
                n_most = sp.value_load(most_i[0:1, 0:1])
                with sp.If(n_most > CAP):
                    with sp.Fori(0, NE) as e:
                        sp.wait_ge(F("o_ps"), e * MORE + 1)
                        for w, src in ((wg, "gate"), (wu, "up"), (wd, "down")):
                            sp.dma_start(w[0][:], wsrc[src][:, bass.ds(e, 1)].rearrange("p one k f -> p (one k) f")).then_inc(F("w_loaded"), 16)
                        with sp.Fori(0, MORE) as b:
                            q = e * MORE + b
                            sp.wait_ge(F("o_ps"), q + 1)
                            with nc.allow_non_contiguous_dma("slot ids"):
                                sp.dma_start(ids[:, 0, 0:1], slots_e[bass.ds(b * 128 + CAP, 128), bass.ds(e, 1), 0]).then_inc(F("ids_loaded"), 16)
                            sp.wait_ge(F("rows_ready"), q * 2 + 2)
                            sp.dma_start(more_e[bass.ds(b * 128, 128), bass.ds(e, 1), :].rearrange("s one d -> s (one d)"),
                                         rows[0][:, 0, :]).then_inc(F("stored"), 16)
                    sp.wait_ge(F("stored"), 16 * (NE * MORE + 1))
                    sp.sem_inc(F("all_stored"), 1)
                    for t in range(NT):
                        n = tokens(t)
                        sp.dma_start(rows[0][0:n, 0, :], x1_d[128 * t:128 * t + n]).then_inc(F("x1_loaded"), 16)
                        sp.wait_ge(F("x1_added"), 2 * (t + 1))
                        sp.dma_start(x1_d[128 * t:128 * t + n], rows[0][0:n, 0, :]).then_inc(F("x1_stored"), 16)
                        sp.wait_ge(F("x1_stored"), 16 * (t + 1))

            @block.gpsimd
            def _(pool):
                n_most = pool.value_load(most_i[0:1, 0:1])
                with pool.If(n_most > CAP):
                    with pool.Fori(0, NE * MORE) as q:
                        pool.wait_ge(F("ids_loaded"), q * 16 + 16)
                        pool.sem_inc(S("pool_passed"), 1)
                        pool.indirect_dma_start(out=xg[0][:, 0, :], out_offset=None, in_=x1_d,
                                                in_offset=bass.IndirectOffsetOnAxis(ap=ids[:, 0, 0:1], axis=0)).then_inc(F("xg_loaded"), 16)
                    pool.wait_ge(F("all_stored"), 1)
                    for t in range(NT):
                        n = tokens(t)
                        if t:
                            pool.wait_ge(F("x1_added"), 2 * t)
                        for k in range(2):
                            pool.indirect_dma_start(out=xg[k][0:n, 0, :], out_offset=None, in_=em_d,
                                                    in_offset=bass.IndirectOffsetOnAxis(ap=more_i[0:n, t, k:k + 1], axis=0)).then_inc(
                                                        F("r_loaded"), 16)

            @block.scalar
            def _(act):
                A = nc.scalar
                n_most = act.value_load(most_i[0:1, 0:1])
                with act.If(n_most > CAP):
                    with act.Fori(0, NE * MORE) as q:
                        for u in range(2):
                            act.wait_ge(F("xgT_ps"), q * 2 + (u + 1))
                            A.activation(xgT[:, 4 * u:4 * u + 4, 0:128], T[u].rearrange("p (k n) -> p k n", k=4), ACT.Copy).then_inc(F("xgT_copied"), 1)
                        act.wait_ge(F("gu_ps"), q + 1)
                        for f in range(2):
                            A.activation(hT[:, f, 0:128], GU[f][:, 0:128], ACT.Silu).then_inc(F("gate_ready"), 1)

            @block.vector
            def _(dve):
                V = nc.vector
                dve.sem_inc(F("stored"), 16)
                n_most = dve.value_load(most_i[0:1, 0:1])
                with dve.If(n_most > CAP):
                    with dve.Fori(0, NE * MORE) as q:
                        dve.wait_ge(F("gate_ready"), q * 2 + 2)
                        for f in range(2):
                            V.tensor_tensor(hT[:, f, 0:128], hT[:, f, 0:128], GU[f][:, 128:256], ALU.mult).then_inc(F("h_ready"), 1)
                        dve.wait_ge(F("o_ps"), q + 2)
                        dve.wait_ge(F("stored"), q * 16 + 16)
                        for c in range(2):
                            V.tensor_copy(rows[0][:, 0, 512 * c:512 * c + 512], OA[:, 512 * c:512 * c + 512]).then_inc(F("rows_ready"), 1)
                    V.tensor_scalar(w_more[:], w_more[:], 1 / ALPHA, None, ALU.mult).then_inc(F("w_scaled"), 1)
                    dve.wait_ge(F("w_scaled"), 1)
                    for t in range(NT):
                        n = tokens(t)
                        dve.wait_ge(F("x1_loaded"), 16 * (t + 1))
                        dve.wait_ge(F("r_loaded"), 32 * (t + 1))
                        for k in range(2):
                            x = rows[0][0:n, 0, :]
                            V.scalar_tensor_tensor(out=x, in0=xg[k][0:n, 0, :], scalar=w_more[0:n, t, k:k + 1], in1=x, op0=ALU.mult,
                                                   op1=ALU.add).then_inc(F("x1_added"), 1)
                            dve.wait_ge(F("x1_added"), 2 * t + k + 1)

            @block.tensor
            def _(pe):
                E = nc.tensor
                n_most = pe.value_load(most_i[0:1, 0:1])
                with pe.If(n_most > CAP):
                    with pe.Fori(0, NE) as e:
                        pe.wait_ge(F("w_loaded"), e * 48 + 48)
                        pe.sem_inc(S("pe_passed"), 1)
                        with pe.Fori(0, MORE) as b:
                            q = e * MORE + b
                            pe.wait_ge(F("xg_loaded"), q * 16 + 16)
                            for u in range(2):
                                for k in range(4 * u, 4 * u + 4):
                                    last = E.transpose(T[u][:, 128 * (k % 4):128 * (k % 4) + 128], xg[0][:, 0, 128 * k:128 * k + 128], ident[:])
                                last.then_inc(F("xgT_ps"), 1)
                            pe.wait_ge(F("xgT_copied"), q * 2 + 2)
                            for f in range(2):
                                for m, w in ((0, wg[0]), (1, wu[0])):
                                    for k in range(KD):
                                        last = E.matmul(GU[f][:, 128 * m:128 * m + 128], w[:, k, 128 * f:128 * f + 128], xgT[:, k, 0:128],
                                                        start=(k == 0), stop=(k == KD - 1))
                            last.then_inc(F("gu_ps"), 1)
                            pe.wait_ge(F("h_ready"), q * 2 + 2)
                            for c in range(2):
                                for f in range(2):
                                    last = E.matmul(OA[:, 512 * c:512 * c + 512], hT[:, f, 0:128], wd[0][:, f, 512 * c:512 * c + 512],
                                                    start=(f == 0), stop=(f == 1))
                            last.then_inc(F("o_ps"), 1)
                            pe.wait_ge(F("rows_ready"), q * 2 + 2)
                            pe.sem_inc(S("pe_passed"), 1)


def combine(nc, a, o, at_i, w_at, x1_d, eo_d):
    ctx = ExitStack()
    S = semaphores(nc, ctx)
    NB = 3
    with ctx:
        def sb(name, shape, dt=F32):
            return ctx.enter_context(nc.sbuf_tensor(name, shape, dt))

        xr = sb("xr", [128, NB, D])
        r0 = sb("r0", [128, NB, D])
        r1 = sb("r1", [128, NB, D])
        g2, b2 = sb("g2", [128, D]), sb("b2", [128, D])
        st = sb("st", [128, NB, 24])
        half = sb("half", [128, 1])
        block = ctx.enter_context(nc.Block())

        def store(sp, t):
            n = tokens(t)
            sp.wait_ge(S("y_ready"), t + 1)
            dst = o["y_p"][0, 128 * t:128 * t + n] if t < NPT else o["y_s"][0]
            sp.dma_start(dst, xr[0:n, t % NB, :]).then_inc(S(f"y_stored{t % NB}"), 16)

        @block.sync
        def _(sp):
            for t in range(NT):
                n = tokens(t)
                if t >= NB:
                    sp.wait_ge(S(f"y_stored{t % NB}"), 16 * (t // NB))
                sp.dma_start(xr[0:n, t % NB, :], x1_d[128 * t:128 * t + n]).then_inc(S(f"xr_loaded{t % NB}"), 16)
                if t == 0:
                    sp.dma_start(g2[:], a["ln2_g"][0].partition_broadcast(128)).then_inc(S("ln2_loaded"), 16)
                    sp.dma_start(b2[:], a["ln2_b"][0].partition_broadcast(128)).then_inc(S("ln2_loaded"), 16)
                if t >= 1:
                    store(sp, t - 1)
            store(sp, NT - 1)
            for j in range(NB):
                sp.wait_ge(S(f"y_stored{j}"), 16 * len(range(j, NT, NB)))

        @block.gpsimd
        def _(pool):
            G = nc.gpsimd
            G.memset(half[:], -0.5).then_inc(S("half_ready"), 1)
            pool.wait_ge(S("half_ready"), 1)

            def gather(t):
                n = tokens(t)
                if t >= NB:
                    pool.wait_ge(S("summed"), 3 * (t - NB + 1))
                for k, r in ((0, r0), (1, r1)):
                    pool.indirect_dma_start(out=r[0:n, t % NB, :], out_offset=None, in_=eo_d,
                                            in_offset=bass.IndirectOffsetOnAxis(ap=at_i[0:n, t, k:k + 1], axis=0)).then_inc(
                                                S(f"r_loaded{t % NB}"), 16)

            for t in range(min(2, NT)):
                gather(t)
            for t in range(NT):
                n, b = tokens(t), t % NB
                if t + 2 < NT:
                    gather(t + 2)
                pool.wait_ge(S("ln2_stats"), t + 1)
                G.tensor_tensor(st[0:n, b, 14:15], st[0:n, b, 13:14], half[0:n], ALU.pow).then_inc(S("pool2_step"), 1)
                pool.wait_ge(S("pool2_step"), t + 1)
                G.tensor_scalar(st[0:n, b, 15:16], st[0:n, b, 12:13], st[0:n, b, 14:15], -1.0, ALU.mult, ALU.mult).then_inc(S("ln2_scale"), 1)

        @block.scalar
        def _(act):
            A = nc.scalar
            for t in range(NT):
                n, b = tokens(t), t % NB
                act.wait_ge(S("ln2_scale"), t + 1)
                A.activation(xr[0:n, b, :], xr[0:n, b, :], ACT.Identity, bias=st[0:n, b, 15:16], scale=st[0:n, b, 14:15]).then_inc(S("y_normed"), 1)

        @block.vector
        def _(dve):
            V = nc.vector
            n_step = [0]

            def step(ins):
                n_step[0] += 1
                ins.then_inc(S("dve2_step"), 1)
                dve.wait_ge(S("dve2_step"), n_step[0])

            def add_norm(t):
                n, b = tokens(t), t % NB
                dve.wait_ge(S(f"xr_loaded{b}"), 16 * (t // NB + 1))
                dve.wait_ge(S(f"r_loaded{b}"), 32 * (t // NB + 1))
                x = xr[0:n, b, :]
                V.tensor_scalar(x, x, ALPHA, None, ALU.mult).then_inc(S("summed"), 1)
                dve.wait_ge(S("summed"), 3 * t + 1)
                for k, r in ((0, r0), (1, r1)):
                    V.scalar_tensor_tensor(out=x, in0=r[0:n, b, :], scalar=w_at[0:n, t, k:k + 1], in1=x, op0=ALU.mult,
                                           op1=ALU.add).then_inc(S("summed"), 1)
                    dve.wait_ge(S("summed"), 3 * t + 2 + k)
                V.bn_stats(st[0:n, b, 0:6], x[:, 0:512])
                step(V.bn_stats(st[0:n, b, 6:12], x[:, 512:1024]))
                step(V.bn_aggr(st[0:n, b, 12:14], st[0:n, b, 0:12].rearrange("p (a b) -> p a b", a=2)))
                V.tensor_scalar(st[0:n, b, 13:14], st[0:n, b, 13:14], EPS, None, ALU.add).then_inc(S("ln2_stats"), 1)

            def gain(t):
                n, b = tokens(t), t % NB
                x = xr[0:n, b, :]
                if t == 0:
                    dve.wait_ge(S("ln2_loaded"), 32)
                dve.wait_ge(S("y_normed"), t + 1)
                step(V.tensor_tensor(x, x, g2[0:n], ALU.mult))
                V.tensor_tensor(x, x, b2[0:n], ALU.add).then_inc(S("y_ready"), 1)

            for t in range(NT + 1):
                if t < NT:
                    add_norm(t)
                if t >= 1:
                    gain(t - 1)

        @block.tensor
        def _(pe):
            pass



INS = ['x_prompt', 'x_sample', 'cache_k', 'cache_v', 'cache_kidx', 'state_gla', 'state_mlstm_C', 'state_mlstm_n',
       'state_mlstm_m', 'state_conv', 'ln0_g', 'ln0_b', 'w_in', 'w_gla_a2', 'b_gla_a', 'g_gla', 'conv_w', 'conv_b',
       'w_mq', 'w_mk', 'w_if', 'b_if', 'g_mlstm', 'w_out', 'ln1_g', 'ln1_b', 'w_router', 'b_router', 'w_exp_gate',
       'w_exp_up', 'w_exp_down', 'ln2_g', 'ln2_b']


def _group(g, b, s):
    return [(f"k_{g}", (1, b, s, H, HA)), (f"v_{g}", (1, b, s, H, HA)), (f"kidx_{g}", (1, b, s, DI)),
            (f"gla_{g}", (1, b, H, DK, DV)), (f"mC_{g}", (1, b, H, HC, HC)), (f"mn_{g}", (1, b, H, HC)),
            (f"mm_{g}", (1, b, H)), (f"conv_{g}", (1, b, CW - 1, WC))]


OUTS = [("y_p", (1, SEQ, D)), ("y_s", (1, SMP, D))] + _group("p", 1, SEQ) + _group("s", 1, SMP)


def kernel(**inputs):
    import numpy as np
    import concourse.bacc as bacc
    from concourse.bass_utils import run_bass_kernel_spmd

    nc = bacc.Bacc("TRN2", target_bir_lowering=False, num_devices=1)
    arrays, ins, outs = {}, {}, {}
    for name in INS:
        arr = np.ascontiguousarray(inputs[name])
        arrays[f"in_{name}"] = arr
        ins[name] = nc.dram_tensor(f"in_{name}", arr.shape, mybir.dt.from_np(arr.dtype), kind="ExternalInput").ap()
    for name, shape in OUTS:
        outs[name] = nc.dram_tensor(f"out_{name}", shape, F32, kind="ExternalOutput").ap()
    build(nc, ins, outs)
    r = run_bass_kernel_spmd(nc, [arrays], core_ids=[0])
    return tuple(r.results[0][f"out_{name}"] for name, _ in OUTS)
```

```python
import concourse.bass as bass
from concourse import mybir
from contextlib import ExitStack
import math

F32 = mybir.dt.float32
U32 = mybir.dt.uint32
I32 = mybir.dt.int32
ALU = mybir.AluOpType
ACT = mybir.ActivationFunctionType
AX = mybir.AxisListType

D = 1024
KD = D // 128
SEQ, SMP, PAST = 1024, 32, 256
NPT = SEQ // 128
NT = NPT + 1
CHUNK = 64
H = 4
HA, WA = 64, 256
DI = 32
TOPK_P = min(256, SEQ // 4)
TOPK_S = min(256, (PAST + SMP) // 4)
DK, DV, WB = 48, 96, 384
RANK, TAU = 16, 16.0
HC, WC, CW = 96, 384, 4
P_IN = 3 * WA + H * DI + DI + H + 2 * H * DK + 2 * WB + RANK + 3 * WC
NE, NG, EPG, FF = 16, 4, 4, 256
ALPHA = 2.0 ** 0.25
EPS = 1e-5
CAP = 160
TOKENS = SEQ + SMP
MORE = -(-(TOKENS - CAP) // 128)
SLOTS = CAP + 128 * MORE
CB = CAP - 128
NW = 4
NEG = -1.0e30
OUTSIDE = -3.0e38

CUTS = [0, 512, 932, 1316, 1700, 2100, 2484, 2868, P_IN]
NCUT = len(CUTS) - 1
WCUT = max(b - a for a, b in zip(CUTS, CUTS[1:]))


def tokens(t):
    return 128 if t < NPT else SMP


def keys(t):
    return 128 * (t + 1) if t < NPT else PAST + SMP


def selects(t):
    return keys(t) > (TOPK_P if t < NPT else TOPK_S)


def score_units(t):
    if not selects(t):
        return []
    return [(h, a, min(512, keys(t) - a)) for a in range(0, keys(t), 512) for h in range(H)]


def units_before(t):
    return sum(len(score_units(u)) for u in range(t))


def key_blocks(t):
    return -(-keys(t) // 128)


def block_groups(t):
    return [(b, min(4, key_blocks(t) - b)) for b in range(0, key_blocks(t), 4)]


def groups_before(t):
    return sum(len(block_groups(u)) for u in range(t)) * H


def semaphores(nc, ctx):
    sems = {}

    def S(name):
        if name not in sems:
            sems[name] = nc.alloc_semaphore(name)
        return sems[name]

    def give_back():
        nc.clear_and_free_semaphores(list(sems.values()))
        nc.all_engine_barrier()

    ctx.callback(give_back)

    return S


def build(nc, a, o):
    ctx = ExitStack()
    with ctx:
        x1_d = nc.dram_tensor("x1_rows", [TOKENS, D], F32, kind="Internal").ap()
        slot_d = nc.dram_tensor("slot_tokens", [NE * SLOTS, 1], I32, kind="Internal").ap()
        eo_d = nc.dram_tensor("expert_rows", [NE * CAP, D], F32, kind="Internal").ap()
        em_d = nc.dram_tensor("expert_rows_more", [NE * 128 * MORE, D], F32, kind="Internal").ap()

        def keep(name, shape, dt=F32):
            return ctx.enter_context(nc.sbuf_tensor(name, shape, dt))

        ident = keep("ident", [128, 128])
        expert = keep("expert", [128, NT, 2])
        before = keep("before", [128, NT, 2])
        gatew = keep("gatew", [128, NT, 2])
        ps = [ctx.enter_context(nc.psum_tensor(f"bank_pair{i}", [128, 1024], F32)) for i in range(4)]
        ones = keep("ones", [128, 128])
        chosen_sum = keep("chosen_sum", [128, NE])
        win = keep("win", [128, NWIN, KD // 2, WCUT])
        trunk(nc, a, o, win, ident, ones, chosen_sum, expert, before, gatew, ps, x1_d, slot_d)
        experts(nc, a, o, win, ident, ones, chosen_sum, expert, before, gatew, ps, x1_d, slot_d, eo_d, em_d)


SLOTS_T = 18
ORDER = [0, 1, 7, 4, 5, 2, 3, 6]


def weave(strands):
    for _ in range(SLOTS_T):
        for strand in strands:
            next(strand, None)
    for strand in strands:
        assert next(strand, "over") == "over"


CUT_SLOT = [2 * c + 2 for c in range(NCUT)]
LN0_SLOT = 11
CHOOSE_SLOT = 2
PLACE_SLOT = 3
TURN_SLOT = [6, 8]
SCORE_SLOT = [10, 10, 12, 12, 14, 14, 16, 16]
ROUNDS = [0, 1, 1, 2, 2, 3, 2, 3, 2, 3, 2, 2, 4, 2, 2, 1, 0, 0]
NWIN = 3


def prob_slot(h, v):
    return 2 * h + 1 + v


def bank_uses(t):
    uses = [("x", 0), ("x", 1)]
    for s in range(1, SLOTS_T):
        if s in CUT_SLOT:
            uses.append(("cut", CUT_SLOT.index(s)))
        if s in TURN_SLOT:
            uses.append(("turn", TURN_SLOT.index(s)))
        uses += [("score", v) for v in range(len(score_units(t))) if SCORE_SLOT[v] == s]
    return uses


def use(t, what, which):
    return 2 + sum(len(bank_uses(u)) for u in range(t)) + bank_uses(t).index((what, which))


def trunk(nc, a, o, win, ident, ones, chosen_sum, expert, before, gatew, ps, x1_d, slot_d):
    ctx = ExitStack()
    S = semaphores(nc, ctx)
    x0_d = nc.dram_tensor("x0_rows", [TOKENS, D], F32, kind="Internal").ap()
    with ctx:
        def sb(name, shape, dt=F32):
            return ctx.enter_context(nc.sbuf_tensor(name, shape, dt))

        upper = sb("upper", [128, 128])
        upper_x = sb("upper_x", [128, 128])
        mid_p = sb("mid_p", [128, 128])
        mid_s = sb("mid_s", [SMP, SMP])
        half_p = sb("half_p", [128, 2])
        half_s = sb("half_s", [SMP, 2])
        minmask = sb("minmask", [128, 128])
        iota16 = sb("iota16", [128, NE])
        group16 = sb("group16", [128, NE])
        tok_id = sb("tok_id", [128, NT], I32)
        pexp = sb("pexp", [128, 4])
        w_out = sb("w_out", [128, KD, D])
        ln0g, ln0b = sb("ln0g", [128, D]), sb("ln0b", [128, D])
        ln1g, ln1b = sb("ln1g", [128, D]), sb("ln1b", [128, D])
        ggla, gml = sb("ggla", [128, WB]), sb("gml", [128, WC])
        a2b = sb("a2b", [RANK + 1, H * DK])
        cw, cb = sb("cw", [HC, H, CW]), sb("cb", [HC, H])
        wmq, wmk = sb("wmq", [HC, H, HC]), sb("wmk", [HC, H, HC])
        wif = sb("wif", [HC, 3 * H, 2 * H])
        bif = sb("bif", [128, 2 * H])
        wr, br = sb("wr", [128, KD, NE]), sb("br", [128, NE])
        x0 = sb("x0", [128, 2, D])
        xT = sb("xT", [128, KD, 128])
        zqk = sb("zqk", [128, 2 * WA])
        zix = sb("zix", [128, 2 * H * DI])
        zw = sb("zw", [128, 2, H])
        zg = sb("zg", [128, 2, H, 64])
        zv = sb("zv", [128, 2, WB])
        zr = sb("zr", [128, WB + RANK + 1])
        zc = sb("zc", [128, WC])
        zm = sb("zm", [128, 2, H, HC + 1])
        zo = sb("zo", [128, WC])
        kT = sb("kT", [128, 2, SEQ])
        kiT = sb("kiT", [128, SEQ])
        va = sb("va", [128, NT, WA])
        kTs = sb("kTs", [128, 2, PAST + SMP])
        kiTs = sb("kiTs", [128, PAST + SMP])
        vc = sb("vc", [128, 2, WA])
        qT = sb("qT", [128, 2, 2, 128])
        qiT = sb("qiT", [128, 128])
        rel = sb("rel", [128, 2, 512])
        score = sb("score", [128, 2, SEQ])
        top8 = sb("top8", [128, 8])
        zeros_i = score[:, 0, 0:NE * SLOTS // 128].bitcast(I32)
        lm = sb("lm", [128, SEQ])
        cach = lm[:, 0:2 * (WA + H * DI)].rearrange("p (b w) -> p b w", b=2)
        x1 = lm
        pT = sb("pT", [128, 2, 4, 128])
        y = sb("y", [128, D])
        yT = sb("yT", [128, KD, 128])
        idx8 = sb("idx8", [128, 8], U32)
        slots_i = sb("slots_i", [128, NT, 2], I32)
        small = sb("small", [128, 288])
        glrT = sb("glrT", [RANK + 1, 128])
        lg = sb("lg", [128, H, 64])
        gtmp = sb("gtmp", [128, 2, H * DK])
        dec = sb("dec", [128, 2, H * 64])
        ecol = sb("ecol", [128, 2, 2])
        qk = sb("qk", [128, 2, H, 64])
        qkT = sb("qkT", [128, 4, 128])
        att = sb("att", [128, H, 128])
        gS = {g: sb(f"gS_{g}", [128, 2, DV]) for g in "ps"}
        gS2 = sb("gS2", [128, 2, DV])
        yb = sb("yb", [128, WB])
        eg, eo = sb("eg", [128, WB]), sb("eo", [128, WC])
        ccx = sb("ccx", [HC, H, CW - 1 + 128])
        xconv = att[0:HC]
        H_DVE = 3
        conv_tmp = yb[0:HC, 0:128 * (H - H_DVE)].rearrange("p (h n) -> p h n", n=128)
        uT = sb("uT", [HC, H, 128])
        qcT, kcT = sb("qcT", [HC, H, 128]), sb("kcT", [HC, H, 128])
        kc = sb("kc", [128, H, HC])
        mi = sb("mi", [128, H, 128])
        mm = sb("mm", [128, H, 128])
        mw = sb("mw", [128, H, 128])
        mp = sb("mp", [128, H, 128])
        cS = {g: sb(f"cS_{g}", [HC, H, HC + 1]) for g in "ps"}
        m0 = {g: sb(f"m0_{g}", [128, H]) for g in "ps"}
        scv = small[0:HC, 100:100 + H * (CW - 1)].rearrange("p (h j) -> p h j", h=H)

        Z = [ps[0][:, 0:512], ps[0][:, 512:1024]]
        RA, RB = ps[1][:, 0:512], ps[1][:, 512:1024]
        SC = ps[2]
        TA, MA = ps[3][:, 0:512], ps[3][:, 512:1024]

        bc = lambda v: v.partition_broadcast(128)
        cache_loads = [(cach[:, :, 0:WA], a["cache_k"][0, 0].rearrange("(b p) h d -> p b (h d)", p=128))]
        cache_loads += [(cach[:, :, WA + DI * h:WA + DI * h + DI], a["cache_kidx"][0, 0].rearrange("(b p) d -> p b d", p=128)) for h in range(H)]
        vec_loads = [
            (a2b[0:RANK, :], a["w_gla_a2"][0]), (a2b[RANK:RANK + 1, :], a["b_gla_a"]),
            (wmq[:], a["w_mq"][0].rearrange("h d e -> d h e")), (wmk[:], a["w_mk"][0].rearrange("h d e -> d h e")),
            (wif[:], a["w_if"][0].rearrange("(b d) g -> d b g", d=HC)), (bif[:], bc(a["b_if"][0])),
            (ggla[:], bc(a["g_gla"][0])), (gml[:], bc(a["g_mlstm"][0])),
            (wr[:], a["w_router"].rearrange("(k p) e -> p k e", p=128)), (br[:], bc(a["b_router"])),
            (vc[:], a["cache_v"][0, 0].rearrange("(b p) h d -> p b (h d)", p=128)),
            (ln1g[:], bc(a["ln1_g"][0])), (ln1b[:], bc(a["ln1_b"][0])),
        ]
        vec_loads += [(cw[:, h, :], a["conv_w"][0][:, HC * h:HC * h + HC].rearrange("j d -> d j")) for h in range(H)]
        N_VEC = len(vec_loads)
        N_STATE = 1 + H + 2 + H
        grp = lambda t: "p" if t < NPT else "s"
        STAT0, MV0, RSTD0, NB0 = 0, 12, 14, 15
        STAT1, MV1, RSTD1, NB1 = 16, 28, 30, 31
        AMAX, ANEG, ASUM, AINV = 32, 36, 40, 44
        GMS, GRSTD = 52, 56
        GATES, LF, LNT, GI, DEN, EM, REC, MMS, MRSTD = 60, 68, 72, 76, 80, 84, 88, 92, 96
        RS, RSEL, RPAIR, RGS, RTOP, RF = 112, 128, 144, 168, 176, 184
        RIN, RSELM, RO, RSUM, RSCR = 192, 208, 224, 256, 272
        sm = lambda n, i, w=1: small[0:n, i:i + w]
        h4 = lambda bank, p, n: bank[0:p, :].rearrange("p (h n) -> p h n", h=H)[:, :, 0:n]
        zbank = lambda i: Z[i % 2]

        def tile_strands(f_attend, f_route, f_recur, f_project, f_select):
            weave([f_project(0)])
            for t in range(NT + 2):
                weave([strand(u) for strand, u in ((f_attend, t - 1), (f_route, t - 2), (f_recur, t), (f_project, t + 1),
                                                   (f_select, t)) if 0 <= u < NT])

        def nothing(t):
            return iter(())

        block = ctx.enter_context(nc.Block())

        @block.sync
        def _(sp):
            def load_x(t):
                n = tokens(t)
                if t >= 2:
                    sp.wait_ge(S(f"x0_stored{t % 2}"), 16 * (t // 2))
                    sp.wait_ge(S("p_ps"), use(t - 2, "x", 1) + 1)
                src = a["x_prompt"][0, 128 * t:128 * t + n] if t < NPT else a["x_sample"][0]
                sp.dma_start(x0[0:n, t % 2, :], src).then_inc(S(f"x_loaded{t % 2}"), 16)

            def project(t):
                n = tokens(t)
                kout, vout, iout, cout = (o["k_p"], o["v_p"], o["kidx_p"], o["conv_p"]) if t < NPT else (
                    o["k_s"], o["v_s"], o["kidx_s"], o["conv_s"])
                r0 = 128 * t if t < NPT else 0
                half = 0
                for s in range(SLOTS_T):
                    if half < 2 * NCUT:
                        i, j = 2 * NCUT * t + half, ORDER[half // 2]
                        k0, c0, c1 = KD // 2 * (half % 2), CUTS[j], CUTS[j + 1]
                        if i >= NWIN:
                            before_t, before_half = divmod(i - NWIN, 2 * NCUT)
                            if before_half % 2:
                                sp.wait_ge(S("p_ps"), use(before_t, "cut", before_half // 2) + 1)
                            else:
                                sp.wait_ge(S("half_cuts"), (i - NWIN) // 2 + 1)
                        sp.dma_start(win[:, i % NWIN, :, 0:c1 - c0],
                                     a["w_in"][0, 128 * k0:128 * k0 + 512, c0:c1].rearrange("(k p) n -> p k n", p=128)).then_inc(
                                         S(f"win_loaded{i % NWIN}"), 16)
                        half += 1
                    if t == 0:
                        with nc.allow_non_contiguous_dma("small vectors"):
                            for dst, src in vec_loads[2 * s:2 * s + 2]:
                                sp.dma_start(dst, src).then_inc(S("vec_loaded"), 16)
                    if s == 2:
                        sp.wait_ge(S("x0_ready"), t + 1)
                        sp.dma_start(x0_d[128 * t:128 * t + n], x0[0:n, t % 2, :]).then_inc(S(f"x0_stored{t % 2}"), 16)
                    if s == 8:
                        sp.wait_ge(S("p_copied"), use(t, "cut", 1) + 1)
                        sp.dma_start(kout[0, 0, r0:r0 + n].rearrange("s h d -> s (h d)"), zqk[0:n, WA:2 * WA]).then_inc(S("kv_stored"), 16)
                        sp.dma_start(vout[0, 0, r0:r0 + n].rearrange("s h d -> s (h d)"), va[0:n, t, :]).then_inc(S("kv_stored"), 16)
                        sp.dma_start(iout[0, 0, r0:r0 + n], zix[0:n, H * DI:H * DI + DI]).then_inc(S("kv_stored"), 16)
                    if s == 15 and t >= NPT - 1:
                        sp.wait_ge(S("p_copied"), use(t, "cut", ORDER.index(5)) + 1)
                        sp.dma_start(cout[0, 0], zc[n - 3:n, :]).then_inc(S("conv_stored"), 16)
                    if s == 4 and t + 2 < NT:
                        load_x(t + 2)
                    yield

            def attend(t):
                n = tokens(t)
                for s in range(SLOTS_T):
                    if s == 10:
                        sp.wait_ge(S("pT_ps"), groups_before(t + 1))
                        if t + 2 >= NT:
                            sp.wait_ge(S(f"x0_stored{t % 2}"), 16 * (t // 2 + 1))
                        sp.dma_start(x1[0:n], x0_d[128 * t:128 * t + n]).then_inc(S("x0_back"), 16)
                    yield

            load_x(0)
            sp.dma_start(ln0g[:], a["ln0_g"].partition_broadcast(128)).then_inc(S("ln0_loaded"), 16)
            sp.dma_start(ln0b[:], a["ln0_b"].partition_broadcast(128)).then_inc(S("ln0_loaded"), 16)
            load_x(1)
            weave([project(0)])
            for t in range(NT + 1):
                if t == NT - 1:
                    sp.wait_ge(S("half_cuts"), NT * NCUT)
                    sp.wait_ge(S("p_ps"), use(NT - 1, "cut", NCUT - 1) + 1)
                    for w, src in zip(first_weights(win), ("gate", "up", "down")):
                        sp.dma_start(w, a[f"w_exp_{src}"][0, 0].rearrange("(k p) f -> p k f", p=128)).then_inc(S("first_loaded"), 16)
                if t == 1:
                    sp.dma_start(w_out[:], a["w_out"][0].rearrange("(k p) n -> p k n", p=128)).then_inc(S("w_out_loaded"), 16)
                weave([g for g in ([attend(t - 1)] if t >= 1 else []) + ([project(t + 1)] if t + 1 < NT else [])])
            for done, g in ((NPT, "p"), (NT, "s")):
                q = S(f"state_stored_{g}")
                sp.wait_ge(S("gla_state"), done)
                for h in range(H):
                    sp.dma_start(o[f"gla_{g}"][0, 0, h], gS[g][64 * (h % 2):64 * (h % 2) + DK, h // 2, :]).then_inc(q, 16)
                sp.wait_ge(S("mlstm_state"), done)
                sp.dma_start(o[f"mC_{g}"][0, 0].rearrange("h d e -> d h e"), cS[g][:, :, 0:HC]).then_inc(q, 16)
                with nc.allow_non_contiguous_dma("a column of the state"):
                    sp.dma_start(o[f"mn_{g}"][0, 0].rearrange("h d -> d h"), cS[g][:, :, HC]).then_inc(q, 16)
                sp.dma_start(o[f"mm_{g}"][0, 0:1], m0[g][0:1, :]).then_inc(q, 16)
            sp.wait_ge(S("first_loaded"), 48)
            sp.wait_ge(S("kv_stored"), 48 * NT)
            sp.wait_ge(S("conv_stored"), 32)
            sp.wait_ge(S("state_stored_p"), 16 * 7)
            sp.wait_ge(S("state_stored_s"), 16 * 7)

        @block.gpsimd
        def _(pool):
            G = nc.gpsimd
            n_step = [0]

            def step(ins):
                n_step[0] += 1
                ins.then_inc(S("pool_step"), 1)
                pool.wait_ge(S("pool_step"), n_step[0])

            def keep_where(out, base, pattern, mult, fill, op=ALU.is_ge):
                return G.affine_select(out=out, in_=out, compare_op=op, fill=fill, base=base,
                                       pattern=pattern, channel_multiplier=mult)

            G.memset(pexp[:], -0.5)
            G.memset(ident[:], 0.0)
            G.memset(ones[:], 1.0)
            G.memset(upper[:], 1.0)
            G.memset(upper_x[:], 1.0)
            G.memset(half_p[:], 1.0)
            G.memset(half_s[:], 1.0)
            G.memset(small[:], 0.0)
            step(G.memset(minmask[:], 0.0))
            keep_where(ident[:], 0, [[-1, 128]], 1, 1.0, ALU.not_equal).then_inc(S("ident_ready"), 1)

            def norm_scale(n, mv, rstd, nb, out_sem):
                step(G.tensor_tensor(sm(n, rstd), sm(n, mv + 1), pexp[0:n, 0:1], ALU.pow))
                G.tensor_scalar(sm(n, nb), sm(n, mv), sm(n, rstd), -1.0, ALU.mult, ALU.mult).then_inc(S(out_sem), 1)

            def ln0(t):
                n = tokens(t)
                xt = x0[0:n, t % 2, :]
                pool.wait_ge(S("ln0_stats"), t + 1)
                norm_scale(n, MV0, RSTD0, NB0, "ln0_scale")
                pool.wait_ge(S("x_normed"), t + 1)
                if t == 0:
                    pool.wait_ge(S("ln0_loaded"), 32)
                step(G.tensor_tensor(xt, xt, ln0g[0:n], ALU.mult))
                G.tensor_tensor(xt, xt, ln0b[0:n], ALU.add).then_inc(S("x0_ready"), 1)

            def constants():
                keep_where(upper[:], 0, [[1, 128]], -1, 0.0)
                keep_where(upper_x[:], -1, [[1, 128]], -1, 0.0)
                keep_where(minmask[:], 0, [[1, 128]], -1, NEG)
                for hf, L in ((half_p, 128), (half_s, SMP)):
                    keep_where(hf[:, 0:1], L // 2 - 1, [[0, 1]], -1, 0.0)
                    keep_where(hf[:, 1:2], -(L // 2), [[0, 1]], 1, 0.0)
                G.iota(tok_id[:], [[128, NT]], base=0, channel_multiplier=1)
                G.iota(iota16[:], [[1, NE]], base=0, channel_multiplier=0, allow_small_or_imprecise_dtypes=True)
                G.iota(group16[:], [[1, NG], [0, EPG]], base=0, channel_multiplier=0, allow_small_or_imprecise_dtypes=True)
                G.memset(zeros_i, 0)
                G.memset(zg[:], 0.0)
                G.memset(lg[:], 0.0)
                for g in "ps":
                    G.memset(gS[g][:], 0.0)
                G.memset(cS["p"][:], 0.0)
                G.memset(m0["p"][:], 0.0)
                G.memset(ccx[:], 0.0)
                G.memset(zr[:, WB + RANK:], 1.0)
                for kept in (chosen_sum, expert, before, gatew):
                    G.memset(kept[:], 0.0)
                step(G.memset(zm[:], 1.0))
                G.memset(small[:, RGS + 4:RGS + 8], NEG)
                G.tensor_scalar(mid_p[:], upper[:], half_p[:, 0:1], None, ALU.subtract)
                G.tensor_scalar(mid_s[:], upper[0:SMP, 0:SMP], half_s[:, 0:1], None, ALU.subtract).then_inc(S("consts"), 1)
                pool.wait_ge(S("consts"), 1)
                pool.dma_start(m0["s"][:], a["state_mlstm_m"][0, 0].partition_broadcast(128)).then_inc(S("states_loaded"), 16)
                for h in range(H):
                    pool.dma_start(gS["s"][64 * (h % 2):64 * (h % 2) + DK, h // 2, :], a["state_gla"][0, 0, h]).then_inc(S("states_loaded"), 16)
                pool.dma_start(cS["s"][:, :, 0:HC], a["state_mlstm_C"][0, 0].rearrange("h d e -> d h e")).then_inc(S("states_loaded"), 16)
                with nc.allow_non_contiguous_dma("a column of the state"):
                    pool.dma_start(cS["s"][:, :, HC], a["state_mlstm_n"][0, 0].rearrange("h d -> d h")).then_inc(S("states_loaded"), 16)
                    for h in range(H):
                        pool.dma_start(scv[:, h, :], a["state_conv"][0, 0][:, HC * h:HC * h + HC].rearrange("j d -> d j")).then_inc(S("states_loaded"), 16)
                pool.dma_start(slot_d.rearrange("(p n) one -> p (n one)", p=128), zeros_i).then_inc(S("slots_cleared"), 16)

            def attend(t):
                n = tokens(t)
                for s in range(SLOTS_T):
                    if s == 13:
                        if t == 0:
                            pool.wait_ge(S("vec_loaded"), 16 * N_VEC)
                        pool.wait_ge(S("ln1_stats"), t + 1)
                        norm_scale(n, MV1, RSTD1, NB1, "ln1_scale")
                        pool.wait_ge(S("x1_normed"), t + 1)
                        step(G.tensor_tensor(x1[0:n, 0:D // 2], x1[0:n, 0:D // 2], ln1g[0:n, 0:D // 2], ALU.mult))
                        G.tensor_tensor(x1[0:n, 0:D // 2], x1[0:n, 0:D // 2], ln1b[0:n, 0:D // 2], ALU.add).then_inc(S("x1_left"), 1)
                    if s == 14:
                        pool.wait_ge(S("x1_left"), t + 1)
                        pool.wait_ge(S("x1_right"), t + 1)
                        pool.dma_start(x1_d[128 * t:128 * t + n], x1[0:n]).then_inc(S("x1_stored"), 16)
                    yield

            def route(t):
                n = tokens(t)
                for s in range(SLOTS_T):
                    if s == PLACE_SLOT:
                        pool.wait_ge(S("slots_ready"), t + 1)
                        if t == 0:
                            pool.wait_ge(S("slots_cleared"), 16)
                        for k in range(2):
                            pool.indirect_dma_start(
                                out=slot_d, out_offset=bass.IndirectOffsetOnAxis(ap=slots_i[0:n, t, k:k + 1], axis=0),
                                in_=tok_id[0:n, t:t + 1], in_offset=None).then_inc(S("ids_stored"), 16)
                            pool.wait_ge(S("ids_stored"), 16 * (2 * t + k + 1))
                    yield

            def recur(t):
                n = tokens(t)
                for s in range(SLOTS_T):
                    if s == 1:
                        if t == 0:
                            pool.wait_ge(S("vec_loaded"), 16 * N_VEC)
                            pool.wait_ge(S("cb_loaded"), 16)
                        pool.wait_ge(S("ccx_ready"), t + 1)
                        if t:
                            pool.wait_ge(S("gla_o_ps"), t)
                        for j in range(CW):
                            for h in range(H_DVE, H):
                                out = xconv[:, h, 0:n] if j == 0 else conv_tmp[:, h - H_DVE, 0:n]
                                ins = G.tensor_scalar(out, ccx[:, h, j:j + n], cw[:, h, j:j + 1], cb[:, h:h + 1] if j == 0 else None,
                                                      ALU.mult, *((ALU.add,) if j == 0 else ()))
                            if j:
                                step(ins)
                                for h in range(H_DVE, H):
                                    ins = G.tensor_tensor(xconv[:, h, 0:n], xconv[:, h, 0:n], conv_tmp[:, h - H_DVE, 0:n], ALU.add)
                            if j < CW - 1:
                                step(ins)
                        ins.then_inc(S("conv_done_pool"), 1)
                    if s == 2:
                        if t == 0:
                            pool.wait_ge(S("vec_loaded"), 16 * N_VEC)
                        pool.wait_ge(S("eg_ready"), t + 1)
                        G.tensor_tensor(eg[0:n], eg[0:n], ggla[0:n], ALU.mult).then_inc(S("eg_gained"), 1)
                    if s == 9:
                        pool.wait_ge(S("gla_ms"), t + 1)
                        G.tensor_tensor(sm(n, GRSTD, H), sm(n, GMS, H), pexp[0:n, :], ALU.pow).then_inc(S("gla_scale"), 1)
                    if s == 13:
                        pool.wait_ge(S("yb_normed"), t + 1)
                        pool.wait_ge(S("eg_gained"), t + 1)
                        if t:
                            pool.wait_ge(S("yT_ps"), 2 * t)
                        G.tensor_tensor(y[0:n, WA:WA + WB], yb[0:n], eg[0:n], ALU.mult).then_inc(S("yb_ready"), 1)
                    if s == 14:
                        pool.wait_ge(S("ml_ms"), t + 1)
                        G.tensor_tensor(sm(n, MRSTD, H), sm(n, MMS, H), pexp[0:n, :], ALU.pow).then_inc(S("ml_scale"), 1)
                    if s == 15:
                        pool.wait_ge(S("yc_normed"), t + 1)
                        G.tensor_tensor(y[0:n, WA + WB:], y[0:n, WA + WB:], gml[0:n], ALU.mult).then_inc(S("yc_ready"), 1)
                    yield

            def project(t):
                n = tokens(t)
                units = score_units(t)
                for s in range(SLOTS_T):
                    if s == 0 and t == 0:
                        ln0(0)
                        constants()
                    for v in range(len(units)):
                        if SCORE_SLOT[v] == s:
                            h, k0, w = units[v]
                            u = units_before(t) + v
                            pool.wait_ge(S("p_copied"), use(t, "score", v) + 1)
                            r, sc = rel[0:n, u % 2, 0:w], score[0:n, t % 2, k0:k0 + w]
                            if h == 0:
                                pool.wait_ge(S("lm_ready"), H * (t - 1))
                            ins = G.tensor_scalar(r if h else sc, r, zw[0:n, t % 2, h:h + 1], None, ALU.mult)
                            if h:
                                step(ins)
                                ins = G.tensor_tensor(sc, sc, r, ALU.add)
                            ins.then_inc(S("rel_used"), 1)
                            pool.wait_ge(S("rel_used"), u + 1)
                    if s == LN0_SLOT and t + 1 < NT:
                        ln0(t + 1)
                    yield

            tile_strands(attend, route, recur, project, nothing)
            pool.wait_ge(S("x1_stored"), 16 * NT)
            pool.wait_ge(S("ids_stored"), 32 * NT)

        @block.scalar
        def _(act):
            A = nc.scalar
            n_step = [0]

            def step(ins):
                n_step[0] += 1
                ins.then_inc(S("act_step"), 1)
                act.wait_ge(S("act_step"), n_step[0])

            copy = lambda out, in_: A.activation(out, in_, ACT.Copy)
            with nc.allow_non_contiguous_dma("the cache's heads"):
                for dst, src in cache_loads:
                    act.dma_start(dst, src).then_inc(S("cache_loaded"), 16)
                act.dma_start(cb[:], a["conv_b"][0].rearrange("(h d) -> d h", d=HC)).then_inc(S("cb_loaded"), 16)

            def evacuate(i, copies):
                act.wait_ge(S("p_ps"), i + 1)
                for out, in_ in copies:
                    last = copy(out, in_)
                last.then_inc(S("p_copied"), 1)

            def ln0(t):
                xt = x0[0:tokens(t), t % 2, :]
                act.wait_ge(S("ln0_scale"), t + 1)
                A.activation(xt, xt, ACT.Identity, bias=sm(tokens(t), NB0), scale=sm(tokens(t), RSTD0)).then_inc(S("x_normed"), 1)

            def cut(t, c):
                n, j, i = tokens(t), ORDER[c], use(t, "cut", c)
                w = CUTS[j + 1] - CUTS[j]
                zp = zbank(i)[0:n, 0:w]
                if t == 0 and c == 0:
                    act.wait_ge(S("consts"), 1)
                if t:
                    for name, v in {0: [("kv_stored", 48 * t)], 7: [("eo_ready", t)], 4: [("eg_ready", t), ("glrT_ps", t)],
                                    5: [("ccT_ps", t)] + ([("conv_stored", 16)] if t == NPT else []),
                                    2: [("qk_ready", t)], 3: [("gla_o_ps", t - 1)] if t > 1 else [],
                                    6: [("ml_s_ps", t - 1)] if t > 1 else []}.get(j, []):
                        act.wait_ge(S(name), v)
                evacuate(i, {
                    0: lambda: [(zqk[0:n], zp)],
                    1: lambda: [(va[0:n, t, :], zp[:, 0:WA]), (zix[0:n, 0:128], zp[:, WA:WA + 128]),
                                (zix[0:n, 128:256].rearrange("p (h d) -> p h d", h=H),
                                 zp[:, WA + 128:WA + 128 + DI].unsqueeze(1).to_broadcast([n, H, DI])),
                                (zw[0:n, t % 2, :], zp[:, w - H:w])],
                    2: lambda: [(zg[0:n, :, :, 0:DK], zp.rearrange("p (a h d) -> p a h d", a=2, h=H))],
                    3: lambda: [(zv[0:n, t % 2, :], zp)],
                    4: lambda: [(zr[0:n, 0:w], zp)],
                    5: lambda: [(zc[0:n], zp)],
                    6: lambda: [(zm[0:n, t % 2, :, 0:HC], zp.rearrange("p (h d) -> p h d", h=H))],
                    7: lambda: [(zo[0:n], zp)],
                }[j]())

            def project(t):
                n = tokens(t)
                kdst, kidst, r0 = (kT, kiT, 128 * t) if t < NPT else (kTs, kiTs, PAST)
                units = score_units(t)
                for s in range(SLOTS_T):
                    if s == 0:
                        if t == 0:
                            ln0(0)
                            for b in range(2):
                                zb = zbank(b)
                                evacuate(b, [(kTs[:, :, 128 * b:128 * b + 128], h4(zb, 128, 128)[:, 0:2]),
                                             (kiTs[:, 128 * b:128 * b + 128], zb[:, 256:384])])
                        for g in range(2):
                            i = use(t, "x", g)
                            evacuate(i, [(xT[:, 4 * g:4 * g + 4, 0:n], h4(zbank(i), 128, n))])
                    if s in CUT_SLOT:
                        cut(t, CUT_SLOT.index(s))
                    if s == TURN_SLOT[0]:
                        i = use(t, "turn", 0)
                        zb = h4(zbank(i), 128, n)
                        if t >= 2:
                            act.wait_ge(S("logits_ps"), H * (t - 1))
                        evacuate(i, [(qT[:, t % 2, :, 0:n], zb[:, 0:2]), (kdst[:, :, r0:r0 + n], zb[:, 2:4])])
                    if s == TURN_SLOT[1]:
                        i = use(t, "turn", 1)
                        zb = zbank(i)
                        evacuate(i, [(qiT[:, 0:n], zb[:, 0:n]), (kidst[:, r0:r0 + n], zb[:, 128:128 + n])])
                    for v in range(len(units)):
                        if SCORE_SLOT[v] == s:
                            h, k0, w = units[v]
                            u, i = units_before(t) + v, use(t, "score", v)
                            act.wait_ge(S("p_ps"), i + 1)
                            if u >= 2:
                                act.wait_ge(S("rel_used"), u - 1)
                            A.activation(rel[0:n, u % 2, 0:w], zbank(i)[0:n, 0:w], ACT.Relu, scale=DI ** -0.5).then_inc(S("p_copied"), 1)
                    if s == LN0_SLOT and t + 1 < NT:
                        ln0(t + 1)
                    yield

            def attend(t):
                n, K = tokens(t), keys(t)
                gb, groups = groups_before(t), block_groups(t)

                def spread(h, v):
                    b0, nb = groups[v]
                    g = gb + len(groups) * h + v
                    act.wait_ge(S("pT_ps"), g + 1)
                    if g >= 2:
                        act.wait_ge(S("pv_done"), g - 1)
                    full = [b for b in range(b0, b0 + nb) if K - 128 * b >= 128]
                    if full:
                        last = copy(pT[:, g % 2, 0:len(full), 0:n], h4(TA, 128, n)[:, 0:len(full)])
                    if len(full) < nb:
                        kb, b = K % 128, len(full)
                        last = copy(pT[0:kb, g % 2, b, 0:n], TA[0:kb, 128 * b:128 * b + n])
                    last.then_inc(S("pT_ready"), 1)

                for s in range(SLOTS_T):
                    if s < 10:
                        for h, v in [(h, v) for h in range(H) for v in range(len(groups)) if prob_slot(h, v) == s]:
                            spread(h, v)
                    if s in (0, 2, 4, 6):
                        h = s // 2
                        act.wait_ge(S("lm_ready"), H * t + h + 1)
                        A.activation(lm[0:n, 0:K], lm[0:n, 0:K], ACT.Exp, bias=sm(n, ANEG + h), scale=HA ** -0.5,
                                     accum_out=sm(n, ASUM + h)).then_inc(S("probs_ready"), 1)
                    for g in (0, 1) if s == 10 else ():
                        act.wait_ge(S("yT_ps"), 2 * t + g + 1)
                        if t:
                            act.wait_ge(S("route_ps"), t)
                        copy(yT[:, 4 * g:4 * g + 4, 0:n], h4((TA, MA)[g], 128, n)).then_inc(S("yT_ready"), 1)
                    if s == 13:
                        act.wait_ge(S("ln1_scale"), t + 1)
                        A.activation(x1[0:n], x1[0:n], ACT.Identity, bias=sm(n, NB1), scale=sm(n, RSTD1)).then_inc(S("x1_normed"), 1)
                    for g in (0, 1) if s == 17 else ():
                        act.wait_ge(S("x1T_ps"), 2 * t + g + 1)
                        copy(yT[:, 4 * g:4 * g + 4, 0:n], h4((TA, MA)[g], 128, n)).then_inc(S("x1T_ready"), 1)
                    yield

            def route(t):
                n = tokens(t)
                for s in range(SLOTS_T):
                    if s == 0:
                        act.wait_ge(S("route_ps"), t + 1)
                        A.activation(sm(n, RS, NE), MA[0:n, 0:NE], ACT.Exp, scale=-1.0).then_inc(S("route_exp"), 1)
                    yield

            def recur(t):
                n = tokens(t)
                m0t = m0[grp(t)]
                for s in range(SLOTS_T):
                    if s == 0:
                        act.wait_ge(S("ccT_ps"), t + 1)
                        if t == 0:
                            act.wait_ge(S("consts"), 1)
                        else:
                            act.wait_ge(S("carry_done"), t)
                        copy(ccx[:, :, CW - 1:CW - 1 + n], h4(RA, HC, n)).then_inc(S("ccx_ready"), 1)
                        act.wait_ge(S("glrT_ps"), t + 1)
                        copy(glrT[:, 0:n], RB[0:RANK + 1, 0:n]).then_inc(S("glrT_ready"), 1)
                    if s == 1:
                        act.wait_ge(S("vT_ps"), t + 1)
                        copy(mp[0:HC, :, 0:n], h4(RB, HC, n)).then_inc(S("vT_ready"), 1)
                        act.wait_ge(S("lg_in"), t + 1)
                        step(A.activation(gtmp[0:n, 0, :], gtmp[0:n, 0, :], ACT.Exp))
                        A.activation(gtmp[0:n, 0, :], gtmp[0:n, 0, :], ACT.Ln, bias=1.0).then_inc(S("gla_ln"), 1)
                        act.wait_ge(S("p_copied"), use(t, "cut", NCUT - 1) + 1)
                        if t:
                            act.wait_ge(S("yb_ready"), t)
                        A.activation(eg[0:n], zr[0:n, 0:WB], ACT.Silu).then_inc(S("eg_ready"), 1)
                        act.wait_ge(S("conv_done"), t + 1)
                        act.wait_ge(S("conv_done_pool"), t + 1)
                        A.activation(uT[:, :, 0:n], xconv[:, :, 0:n], ACT.Silu).then_inc(S("u_ready"), 1)
                        if t:
                            act.wait_ge(S("hs_ready"), t)
                        A.activation(eo[0:n], zo[0:n], ACT.Sigmoid).then_inc(S("eo_ready"), 1)
                    if s == 4:
                        act.wait_ge(S("cum_ps"), t + 1)
                        A.activation(dec[0:n, 0, :], RA[0:n, 0:256], ACT.Exp, scale=1 / TAU)
                        A.activation(dec[0:n, 1, :], RA[0:n, 0:256], ACT.Exp, scale=-1 / TAU)
                        A.activation(ecol[:], RA[:, 256:260].rearrange("p (a b) -> p a b", a=2), ACT.Exp, scale=1 / TAU).then_inc(S("dec_ready"), 1)
                        act.wait_ge(S("qc_ps"), t + 1)
                        copy(qcT[:, :, 0:n], h4(RB, HC, n)).then_inc(S("qc_ready"), 1)
                    if s == 5:
                        act.wait_ge(S("kcT_ps"), t + 1)
                        A.mul(kcT[:, :, 0:n], h4(RA, HC, n), HC ** -0.5).then_inc(S("kcT_ready"), 1)
                        act.wait_ge(S("kc_ps"), t + 1)
                        A.mul(kc[0:n], RB[0:n, 0:WC].rearrange("p (h d) -> p h d", h=H), HC ** -0.5).then_inc(S("kc_ready"), 1)
                    if s == 6:
                        act.wait_ge(S("qkT_ps"), t + 1)
                        copy(qkT[:, :, 0:n], h4(RA, 128, n)).then_inc(S("qkT_ready"), 1)
                        act.wait_ge(S("ml_nabs"), t + 1)
                        step(A.activation(sm(n, LNT, H), sm(n, LNT, H), ACT.Exp))
                        A.activation(sm(n, LNT, H), sm(n, LNT, H), ACT.Ln, bias=1.0).then_inc(S("ml_ln"), 1)
                    if s == 7:
                        act.wait_ge(S("irow_ps"), t + 1)
                        copy(mi[:, :, 0:n], h4(RB, 128, n)).then_inc(S("irow_ready"), 1)
                    if s == 9:
                        act.wait_ge(S("gla_o_ps"), t + 1)
                        A.activation(gtmp[0:n].rearrange("p a b -> p (a b)"), RA[0:n, 0:WB], ACT.Square).then_inc(S("gla_sq"), 1)
                        act.wait_ge(S("fm_ready"), t + 1)
                        if t == NPT:
                            act.wait_ge(S("states_loaded"), 16 * N_STATE)
                        for h in range(H):
                            last = A.activation(mi[:, h, 0:n], mw[:, h, 0:n], ACT.Exp, bias=m0t[:, h:h + 1])
                        last.then_inc(S("wst_ready"), 1)
                    if s == 11:
                        act.wait_ge(S("cols_ps"), t + 1)
                        act.wait_ge(S("gi_ready"), t + 1)
                        A.activation(sm(n, EM, H), RA[0:n, 4:8], ACT.Exp, scale=-1.0).then_inc(S("mcol_exp"), 1)
                        act.wait_ge(S("arg_ready"), t + 1)
                        A.activation(mw[0:n, :, 0:n], mw[0:n, :, 0:n], ACT.Exp).then_inc(S("w_ready"), 1)
                    if s == 13:
                        act.wait_ge(S("hs_ready"), t + 1)
                        A.activation(gtmp[0:n].rearrange("p a b -> p (a b)"), y[0:n, WA + WB:], ACT.Square).then_inc(S("ml_sq"), 1)
                    yield

            tile_strands(attend, route, recur, project, nothing)

        @block.vector
        def _(dve):
            V = nc.vector
            n_step = [0]

            def step(ins):
                n_step[0] += 1
                ins.then_inc(S("dve_step"), 1)
                dve.wait_ge(S("dve_step"), n_step[0])

            def tell(ins, name, value):
                ins.then_inc(S(name), 1)
                dve.wait_ge(S(name), value)

            TT, TS, STT = V.tensor_tensor, V.tensor_scalar, V.scalar_tensor_tensor

            def stats(src, n, stat, mv, out_sem):
                V.bn_stats(sm(n, stat, 6), src[:, 0:512])
                step(V.bn_stats(sm(n, stat + 6, 6), src[:, 512:1024]))
                step(V.bn_aggr(sm(n, mv, 2), sm(n, stat, 12).rearrange("p (a b) -> p a b", a=2)))
                TS(sm(n, mv + 1), sm(n, mv + 1), EPS, None, ALU.add).then_inc(S(out_sem), 1)

            def ln0(t):
                if t == 0:
                    dve.wait_ge(S("ident_ready"), 1)
                dve.wait_ge(S(f"x_loaded{t % 2}"), 16 * (t // 2 + 1))
                if t:
                    dve.wait_ge(S("x_normed"), t)
                stats(x0[0:tokens(t), t % 2, :], tokens(t), STAT0, MV0, "ln0_stats")

            def project(t):
                for s in range(SLOTS_T):
                    if s == 0 and t == 0:
                        ln0(0)
                    if s == LN0_SLOT - 1 and t + 1 < NT:
                        ln0(t + 1)
                    yield

            def select(t):
                n, K = tokens(t), keys(t)
                sc = score[0:n, t % 2, 0:K]
                if t < NPT:
                    corner = score[0:CHUNK, t % 2, K - CHUNK:K]
                rounds = (TOPK_P if t < NPT else TOPK_S) // 8 if selects(t) else 0
                for s in range(SLOTS_T):
                    if s == 0:
                        if t == 0:
                            dve.wait_ge(S("slots_cleared"), 16)
                        if selects(t):
                            dve.wait_ge(S("rel_used"), units_before(t + 1))
                        if t < NPT and not selects(t):
                            step(V.memset(sc, 0.0))
                        if t < NPT:
                            step(V.memset(corner, OUTSIDE if selects(t) else NEG))
                    for _ in range(rounds * sum(ROUNDS[:s + 1]) // sum(ROUNDS) - rounds * sum(ROUNDS[:s]) // sum(ROUNDS)):
                        step(V.max(top8[0:n], sc))
                        step(V.match_replace(sc, top8[0:n], sc, NEG))
                    if s == SLOTS_T - 1 and selects(t):
                        step(TS(sc, sc, NEG, NEG, ALU.not_equal, ALU.mult))
                    yield

            def attend(t):
                n, K = tokens(t), keys(t)
                ng = len(block_groups(t))
                for s in range(SLOTS_T):
                    if s in (0, 2, 4, 6):
                        h = s // 2
                        dve.wait_ge(S("logits_ps"), H * t + h + 1)
                        if t and h == 0:
                            dve.wait_ge(S("x1_stored"), 16 * t)
                            dve.wait_ge(S("x1T_ps"), 2 * t)
                        if h:
                            dve.wait_ge(S("pT_ps"), groups_before(t) + ng * h)
                        if t == 0 and h == 0:
                            dve.wait_ge(S("p_ps"), 2)
                        step(V.tensor_tensor_reduce(lm[0:n, 0:K], SC[0:n, 0:K], score[0:n, t % 2, 0:K], 1.0, -3.0e38,
                                                    ALU.add, ALU.max, sm(n, AMAX + h)))
                        TS(sm(n, ANEG + h), sm(n, AMAX + h), -HA ** -0.5, None, ALU.mult).then_inc(S("lm_ready"), 1)
                    if s == 9:
                        dve.wait_ge(S("probs_ready"), H * (t + 1))
                        step(V.reciprocal(sm(n, AINV, H), sm(n, ASUM, H)))
                        dve.wait_ge(S("pv_done"), groups_before(t + 1))
                        TT(y[0:n, 0:WA].rearrange("p (h d) -> p h d", h=H), MA[0:n, 0:WA].rearrange("p (h d) -> p h d", h=H),
                           sm(n, AINV, H).unsqueeze(2).to_broadcast([n, H, HA]), ALU.mult).then_inc(S("ya_ready"), 1)
                    if s == 13:
                        dve.wait_ge(S("x0_back"), 16 * (t + 1))
                        for c in range(2):
                            dve.wait_ge(S("wo_ps"), 2 * t + c + 1)
                            cs = slice(512 * c, 512 * c + 512)
                            tell(STT(out=x1[0:n, cs], in0=x1[0:n, cs], scalar=ALPHA, in1=SC[0:n, cs],
                                     op0=ALU.mult, op1=ALU.add), "residual_done", 2 * t + c + 1)
                        stats(x1[0:n], n, STAT1, MV1, "ln1_stats")
                    if s == 14:
                        dve.wait_ge(S("x1_normed"), t + 1)
                        step(TT(x1[0:n, D // 2:], x1[0:n, D // 2:], ln1g[0:n, D // 2:], ALU.mult))
                        TT(x1[0:n, D // 2:], x1[0:n, D // 2:], ln1b[0:n, D // 2:], ALU.add).then_inc(S("x1_right"), 1)
                    yield

            def route(t):
                for s in range(SLOTS_T):
                    if s == CHOOSE_SLOT:
                        choose(t)
                    if s == PLACE_SLOT:
                        place(t)
                    yield

            def choose(t):
                n = tokens(t)
                sg, sel = sm(n, RS, NE), sm(n, RSEL, NE)
                g4 = lambda v: v.rearrange("p (g e) -> p g e", g=NG)
                dve.wait_ge(S("route_exp"), t + 1)
                step(TS(sg, sg, 1.0, None, ALU.add))
                step(V.reciprocal(sg, sg))
                step(TT(sel, sg, br[0:n], ALU.add))
                pair, at = sm(n, RPAIR, 24).rearrange("p (g e) -> p g e", g=NG), 0
                for d in (1, 2, 3):
                    ins = TT(pair[:, :, at:at + 4 - d], g4(sel)[:, :, 0:4 - d], g4(sel)[:, :, d:4], ALU.add)
                    at += 4 - d
                step(ins)
                step(V.tensor_reduce(sm(n, RGS, NG), pair, AX.X, ALU.max))
                step(V.max(sm(n, RTOP, 8), sm(n, RGS, 8)))
                step(V.max_index(idx8[0:n], sm(n, RTOP, 8), sm(n, RGS, 8)))
                step(V.tensor_copy(sm(n, RF), idx8[0:n, 0:1]))
                step(TS(sm(n, RIN, NE), group16[0:n], sm(n, RF), None, ALU.is_equal))
                step(TT(sm(n, RSELM, NE), sel, sm(n, RIN, NE), ALU.mult))
                step(TS(sm(n, RIN, NE), sm(n, RIN, NE), -NEG, NEG, ALU.mult, ALU.add))
                step(TT(sm(n, RSELM, NE), sm(n, RSELM, NE), sm(n, RIN, NE), ALU.add))
                step(V.max(sm(n, RTOP, 8), sm(n, RSELM, NE)))
                step(V.max_index(idx8[0:n], sm(n, RTOP, 8), sm(n, RSELM, NE)))
                step(V.tensor_copy(expert[0:n, t, :], idx8[0:n, 0:2]))
                for k in range(2):
                    ins = TS(sm(n, RO + NE * k, NE), iota16[0:n], expert[0:n, t, k:k + 1], None, ALU.is_equal)
                step(ins)
                tell(TT(sm(n, RSUM, NE), sm(n, RO, NE), sm(n, RO + NE, NE), ALU.add), "chosen", t + 1)
                for k in range(2):
                    ins = V.tensor_tensor_reduce(sm(n, RSCR, NE), sm(n, RO + NE * k, NE), sg, 1.0, 0.0, ALU.mult, ALU.add,
                                                 gatew[0:n, t, k:k + 1])
                    step(ins)
                step(TT(sm(n, RF + 2), gatew[0:n, t, 0:1], gatew[0:n, t, 1:2], ALU.add))
                step(V.reciprocal(sm(n, RF + 3), sm(n, RF + 2)))
                step(TS(gatew[0:n, t, :], gatew[0:n, t, :], sm(n, RF + 3), None, ALU.mult))

            def place(t):
                n = tokens(t)
                dve.wait_ge(S("pos_ps"), t + 1)
                for k in range(2):
                    step(V.tensor_tensor_reduce(sm(n, RSCR, NE), RB[0:n, 0:NE], sm(n, RO + NE * k, NE), 1.0, 0.0,
                                                ALU.mult, ALU.add, before[0:n, t, k:k + 1]))
                step(STT(out=sm(n, RF + 6, 2), in0=expert[0:n, t, :], scalar=float(SLOTS), in1=before[0:n, t, :], op0=ALU.mult, op1=ALU.add))
                step(V.tensor_copy(slots_i[0:n, t, :], sm(n, RF + 6, 2)))
                TT(chosen_sum[0:n], chosen_sum[0:n], sm(n, RSUM, NE), ALU.add).then_inc(S("slots_ready"), 1)

            def recur(t):
                n = tokens(t)
                g = grp(t)
                hd = lambda v: v.rearrange("p (h d) -> p h d", h=H)
                wide = lambda v, w: v.unsqueeze(2).to_broadcast([v.shape[0], H, w])
                for s in range(SLOTS_T):
                    if s == 0 and t == 0:
                        dve.wait_ge(S("consts"), 1)
                        dve.wait_ge(S("vec_loaded"), 16 * N_VEC)
                        dve.wait_ge(S("cb_loaded"), 16)
                    if s == 1:
                        dve.wait_ge(S("lgpre_ps"), t + 1)
                        step(TS(gtmp[0:n, 1, :], RA[0:n, 0:H * DK], 0.0, None, ALU.min))
                        STT(out=gtmp[0:n, 0, :], in0=gtmp[0:n, 1, :], scalar=2.0, in1=RA[0:n, 0:H * DK], op0=ALU.mult,
                            op1=ALU.subtract).then_inc(S("lg_in"), 1)
                        dve.wait_ge(S("ccx_ready"), t + 1)
                        if t:
                            dve.wait_ge(S("gla_o_ps"), t)
                        for j in range(CW):
                            for h in range(H_DVE):
                                if j == 0:
                                    ins = TS(xconv[:, h, 0:n], ccx[:, h, 0:n], cw[:, h, 0:1], cb[:, h:h + 1], ALU.mult, ALU.add)
                                else:
                                    ins = STT(out=xconv[:, h, 0:n], in0=ccx[:, h, j:j + n], scalar=cw[:, h, j:j + 1],
                                              in1=xconv[:, h, 0:n], op0=ALU.mult, op1=ALU.add)
                            if j < CW - 1:
                                step(ins)
                        tell(ins, "conv_done", t + 1)
                    if s == 2:
                        dve.wait_ge(S("gla_ln"), t + 1)
                        TT(lg[0:n, :, 0:DK], hd(gtmp[0:n, 1, :]), hd(gtmp[0:n, 0, :]), ALU.subtract).then_inc(S("lg_ready"), 1)
                        if t + 1 == NPT:
                            dve.wait_ge(S("states_loaded"), 16 * N_STATE)
                        dve.wait_ge(S("conv_done_pool"), t + 1)
                        if t + 1 < NT:
                            V.tensor_copy(ccx[:, :, 0:CW - 1], scv[:] if t + 1 == NPT else ccx[:, :, 128:128 + CW - 1]).then_inc(S("carry_done"), 1)
                    if s == 5:
                        dve.wait_ge(S("dec_ready"), t + 1)
                        v4 = lambda v: v.rearrange("p (h d) -> p h d", h=H)
                        STT(out=qk[0:n, 0], in0=zg[0:n, 0], scalar=DK ** -0.5, in1=v4(dec[0:n, 0, :]), op0=ALU.mult, op1=ALU.mult)
                        TT(qk[0:n, 1], zg[0:n, 1], v4(dec[0:n, 1, :]), ALU.mult).then_inc(S("qk_ready"), 1)
                        TT(gS2[:], gS[g][:], ecol[:, :, 0:1].to_broadcast([128, 2, DV]), ALU.mult).then_inc(S("gS2_ready"), 1)
                    if s == 6:
                        dve.wait_ge(S("gates_ps"), t + 1)
                        step(TT(sm(n, GATES, 8), RB[0:n, 0:8], bif[0:n], ALU.add))
                        step(TS(sm(n, LF, H), sm(n, GATES + H, H), 0.0, None, ALU.min))
                        STT(out=sm(n, LNT, H), in0=sm(n, LF, H), scalar=2.0, in1=sm(n, GATES + H, H), op0=ALU.mult,
                            op1=ALU.subtract).then_inc(S("ml_nabs"), 1)
                        dve.wait_ge(S("ml_ln"), t + 1)
                        TT(sm(n, LF, H), sm(n, LF, H), sm(n, LNT, H), ALU.subtract).then_inc(S("lf_ready"), 1)
                    if s == 7:
                        dve.wait_ge(S("att_ps"), t + 1)
                        TT(att[0:n, :, 0:n], h4(RA, n, n), upper[0:n, 0:n].unsqueeze(1).to_broadcast([n, H, n]), ALU.mult).then_inc(S("att_ready"), 1)
                    if s == 8:
                        dve.wait_ge(S("gla_s_ps"), t + 1)
                        gps = RA[:, 0:2 * DV].rearrange("p (a v) -> p a v", a=2)
                        step(TT(gS[g][:], gps, gS2[:], ALU.add))
                        TT(gS[g][:], gS[g][:], ecol[:, :, 1:2].to_broadcast([128, 2, DV]), ALU.mult).then_inc(S("gla_state"), 1)
                        dve.wait_ge(S("irow_ready"), t + 1)
                        dve.wait_ge(S("lfrow_ps"), t + 1)
                        for h in range(H):
                            ins = V.tensor_tensor_scan(mm[:, h, 0:n], h4(RB, 128, n)[:, h], mi[:, h, 0:n], m0[g][:, h:h + 1], ALU.add, ALU.max)
                        tell(ins, "mm_ready", t + 1)
                    if s == 9:
                        dve.wait_ge(S("frow_ps"), t + 1)
                        tell(TT(mw[:, :, 0:n], h4(RB, 128, n), mm[:, :, 0:n], ALU.subtract), "fm_ready", t + 1)
                        dve.wait_ge(S("gla_sq"), t + 1)
                        step(V.tensor_reduce(sm(n, GMS, H), hd(gtmp[0:n].rearrange("p a b -> p (a b)")), AX.X, ALU.add))
                        TS(sm(n, GMS, H), sm(n, GMS, H), 1.0 / DV, EPS, ALU.mult, ALU.add).then_inc(S("gla_ms"), 1)
                        dve.wait_ge(S("gla_scale"), t + 1)
                        if t:
                            dve.wait_ge(S("yb_ready"), t)
                        TT(hd(yb[0:n]), hd(RA[0:n, 0:WB]), wide(sm(n, GRSTD, H), DV), ALU.mult).then_inc(S("yb_normed"), 1)
                    if s == 11:
                        dve.wait_ge(S("cols_ps"), t + 1)
                        tell(TT(sm(n, GI, H), sm(n, GATES, H), RA[0:n, 0:4], ALU.subtract), "gi_ready", t + 1)
                        dve.wait_ge(S("wst_ready"), t + 1)
                        for h in range(H):
                            ins = STT(out=mw[0:n, h, 0:n], in0=mw[0:n, h, 0:n], scalar=sm(n, GI + h), in1=minmask[0:n, 0:n],
                                      op0=ALU.add, op1=ALU.min)
                        ins.then_inc(S("arg_ready"), 1)
                    if s == 12:
                        dve.wait_ge(S("qk2_ps"), t + 1)
                        TT(qcT[:, :, 0:n], qcT[:, :, 0:n], mi[0:HC, :, 0:n], ALU.mult).then_inc(S("qs_ready"), 1)
                        dve.wait_ge(S("w_ready"), t + 1)
                        TT(mp[0:n, :, 0:n], mw[0:n, :, 0:n], h4(RB, n, n), ALU.mult)
                        TT(kc[0:n], kc[0:n], mw[0:n, :, n - 1:n].to_broadcast([n, H, HC]), ALU.mult).then_inc(S("p_ready"), 1)
                    if s == 13:
                        num = RA[0:n, 0:H * (HC + 1)].rearrange("p (h d) -> p h d", h=H)
                        yc = y[0:n, WA + WB:]
                        dve.wait_ge(S("num_ps"), t + 1)
                        dve.wait_ge(S("mcol_exp"), t + 1)
                        if t:
                            dve.wait_ge(S("yT_ps"), 2 * t)
                        step(TS(sm(n, DEN, H), num[:, :, HC], -1.0, None, ALU.mult))
                        step(TT(sm(n, DEN, H), sm(n, DEN, H), num[:, :, HC], ALU.max))
                        step(TT(sm(n, DEN, H), sm(n, DEN, H), sm(n, EM, H), ALU.max))
                        step(V.reciprocal(sm(n, REC, H), sm(n, DEN, H)))
                        step(TT(hd(yc), num[:, :, 0:HC], wide(sm(n, REC, H), HC), ALU.mult))
                        dve.wait_ge(S("eo_ready"), t + 1)
                        tell(TT(yc, yc, eo[0:n], ALU.mult), "hs_ready", t + 1)
                        step(TT(cS[g][:], cS[g][:], mi[0:HC, :, n - 1:n].to_broadcast([HC, H, HC + 1]), ALU.mult))
                        V.tensor_copy(m0[g][:], mm[:, :, n - 1])
                        dve.wait_ge(S("ml_s_ps"), t + 1)
                        TT(cS[g][:], cS[g][:], RB[0:HC, 0:H * (HC + 1)].rearrange("p (h d) -> p h d", h=H), ALU.add).then_inc(S("mlstm_state"), 1)
                    if s == 14:
                        dve.wait_ge(S("ml_sq"), t + 1)
                        step(V.tensor_reduce(sm(n, MMS, H), hd(gtmp[0:n].rearrange("p a b -> p (a b)")), AX.X, ALU.add))
                        TS(sm(n, MMS, H), sm(n, MMS, H), 1.0 / HC, EPS, ALU.mult, ALU.add).then_inc(S("ml_ms"), 1)
                    if s == 15:
                        dve.wait_ge(S("ml_scale"), t + 1)
                        TT(hd(y[0:n, WA + WB:]), hd(y[0:n, WA + WB:]), wide(sm(n, MRSTD, H), HC), ALU.mult).then_inc(S("yc_normed"), 1)
                    yield

            tile_strands(attend, route, recur, project, select)

        @block.tensor
        def _(pe):
            E = nc.tensor
            mmul = E.matmul
            n_step = [0]

            def step(ins):
                n_step[0] += 1
                ins.then_inc(S("pe_step"), 1)
                pe.wait_ge(S("pe_step"), n_step[0])

            tr = lambda out, in_: E.transpose(out, in_, ident[0:in_.shape[0], 0:in_.shape[0]])

            def four(src, n, g):
                bank = (TA, MA)[g]
                for k in range(4):
                    last = tr(bank[:, 128 * k:128 * k + n], src[:, 512 * g + 128 * k:512 * g + 128 * k + 128])
                return last

            def bank(i):
                if i >= 2:
                    pe.wait_ge(S("p_copied"), i - 1)
                return zbank(i)

            def project(t):
                n = tokens(t)
                units = score_units(t)
                ki = kiT if t < NPT else kiTs
                half = 0
                for s in range(SLOTS_T):
                    if s == 0:
                        if t == 0:
                            pe.wait_ge(S("ident_ready"), 1)
                            pe.wait_ge(S("cache_loaded"), 16 * len(cache_loads))
                            for b in range(2):
                                zb = bank(b)
                                for c in range(2):
                                    tr(zb[:, 128 * c:128 * c + 128], cach[:, b, 128 * c:128 * c + 128])
                                tr(zb[:, 256:384], cach[:, b, WA:]).then_inc(S("p_ps"), 1)
                        pe.wait_ge(S("x0_ready"), t + 1)
                        for g in range(2):
                            zb = bank(use(t, "x", g))
                            for k in range(4):
                                last = tr(zb[:, 128 * k:128 * k + n], x0[0:n, t % 2, 512 * g + 128 * k:512 * g + 128 * k + 128])
                            last.then_inc(S("p_ps"), 1)
                    elif half < 2 * NCUT:
                        i, c = 2 * NCUT * t + half, half // 2
                        w = CUTS[ORDER[c] + 1] - CUTS[ORDER[c]]
                        if half == 0:
                            pe.wait_ge(S("p_copied"), use(t, "x", 1) + 1)
                        u = use(t, "cut", c)
                        zb = zbank(u) if half % 2 else bank(u)
                        pe.wait_ge(S(f"win_loaded{i % NWIN}"), 16 * (i // NWIN + 1))
                        for k in range(4):
                            kk = 4 * (half % 2) + k
                            last = mmul(zb[0:n, 0:w], xT[:, kk, 0:n], win[:, i % NWIN, k, 0:w], start=(kk == 0), stop=(kk == KD - 1))
                        last.then_inc(S("p_ps") if half % 2 else S("half_cuts"), 1)
                        half += 1
                    if s == TURN_SLOT[0]:
                        zb = bank(use(t, "turn", 0))
                        pe.wait_ge(S("p_copied"), use(t, "cut", ORDER.index(0)) + 1)
                        for b in range(4):
                            last = tr(zb[:, 128 * b:128 * b + n], zqk[0:n, 128 * b:128 * b + 128])
                        last.then_inc(S("p_ps"), 1)
                    if s == TURN_SLOT[1]:
                        zb = bank(use(t, "turn", 1))
                        pe.wait_ge(S("p_copied"), use(t, "cut", ORDER.index(1)) + 1)
                        tr(zb[:, 0:n], zix[0:n, 0:128])
                        tr(zb[:, 128:128 + n], zix[0:n, 128:256]).then_inc(S("p_ps"), 1)
                    for v in range(len(units)):
                        if SCORE_SLOT[v] == s:
                            h, k0, w = units[v]
                            zb = bank(use(t, "score", v))
                            if v == 0:
                                pe.wait_ge(S("p_copied"), use(t, "turn", 1) + 1)
                            mmul(zb[0:n, 0:w], qiT[DI * h:DI * h + DI, 0:n], ki[DI * h:DI * h + DI, k0:k0 + w],
                                 start=True, stop=True).then_inc(S("p_ps"), 1)
                    yield

            def attend(t):
                n, K = tokens(t), keys(t)
                kt = kT if t < NPT else kTs
                gb, groups = groups_before(t), block_groups(t)

                def logits(h):
                    if t or h:
                        pe.wait_ge(S("lm_ready"), H * t + h)
                    if t and h == 0:
                        pe.wait_ge(S("residual_done"), 2 * t)
                    b = HA * (h % 2)
                    for c in range(0, K, 512):
                        w = min(512, K - c)
                        last = mmul(SC[0:n, c:c + w], qT[b:b + HA, t % 2, h // 2, 0:n], kt[b:b + HA, h // 2, c:c + w], start=True, stop=True)
                    last.then_inc(S("logits_ps"), 1)

                def turn(h, v):
                    b0, nb = groups[v]
                    g = gb + len(groups) * h + v
                    if v == 0:
                        pe.wait_ge(S("probs_ready"), H * t + h + 1)
                    if g:
                        pe.wait_ge(S("pT_ready"), g)
                    if g == gb and t:
                        pe.wait_ge(S("x1T_ready"), 2 * t)
                    for b in range(b0, b0 + nb):
                        kb = min(128, K - 128 * b)
                        last = tr(TA[0:kb, 128 * (b - b0):128 * (b - b0) + n], lm[0:n, 128 * b:128 * b + kb])
                    last.then_inc(S("pT_ps"), 1)

                def values(h, v):
                    b0, nb = groups[v]
                    g = gb + len(groups) * h + v
                    pe.wait_ge(S("pT_ready"), g + 1)
                    if g == gb and t:
                        pe.wait_ge(S("route_exp"), t)
                    for b in range(b0, b0 + nb):
                        kb = min(128, K - 128 * b)
                        vv = va[0:kb, b, :] if t < NPT else (vc[0:kb, b, :] if b < 2 else va[0:kb, t, :])
                        last = mmul(MA[0:n, HA * h:HA * h + HA], pT[0:kb, g % 2, b - b0, 0:n], vv[:, HA * h:HA * h + HA],
                                    start=(b == 0), stop=(128 * b + kb == K))
                    last.then_inc(S("pv_done"), 1)

                for s in range(SLOTS_T):
                    if s < 11:
                        for h in range(H):
                            for v in range(len(groups)):
                                if prob_slot(h, v) + 1 == s:
                                    values(h, v)
                        for h in range(H):
                            for v in range(len(groups)):
                                if prob_slot(h, v) == s:
                                    turn(h, v)
                    if s in (0, 2, 4, 6):
                        logits(s // 2)
                    if s == 10:
                        pe.wait_ge(S("ya_ready"), t + 1)
                        pe.wait_ge(S("yb_ready"), t + 1)
                        pe.wait_ge(S("yc_ready"), t + 1)
                        pe.wait_ge(S("pT_ready"), groups_before(t + 1))
                        four(y[0:n], n, 0).then_inc(S("yT_ps"), 1)
                        four(y[0:n], n, 1).then_inc(S("yT_ps"), 1)
                    if s in (12, 13):
                        c = s - 12
                        if c == 0:
                            if t == 0:
                                pe.wait_ge(S("w_out_loaded"), 16)
                            pe.wait_ge(S("yT_ready"), 2 * t + 2)
                            pe.wait_ge(S("lm_ready"), H * (t + 1))
                        for k in range(KD):
                            last = mmul(SC[0:n, 512 * c:512 * c + 512], yT[:, k, 0:n], w_out[:, k, 512 * c:512 * c + 512],
                                        start=(k == 0), stop=(k == KD - 1))
                        last.then_inc(S("wo_ps"), 1)
                    if s == 17:
                        pe.wait_ge(S("wo_ps"), 2 * t + 2)
                        for g in range(2):
                            pe.wait_ge(S(("x1_left", "x1_right")[g]), t + 1)
                            four(x1[0:n], n, g).then_inc(S("x1T_ps"), 1)
                    yield

            def route(t):
                n = tokens(t)
                for s in range(SLOTS_T):
                    if s == 0:
                        pe.wait_ge(S("x1T_ready"), 2 * t + 2)
                        for k in range(KD):
                            last = mmul(MA[0:n, 0:NE], yT[:, k, 0:n], wr[:, k, :], start=(k == 0), stop=(k == KD - 1))
                        last.then_inc(S("route_ps"), 1)
                    if s == PLACE_SLOT:
                        pe.wait_ge(S("chosen"), t + 1)
                        if t + 2 < NT:
                            pe.wait_ge(S("vT_ready"), t + 3)
                        else:
                            pe.wait_ge(S("mlstm_state"), NT)
                        mmul(RB[0:n, 0:NE], ones[:, 0:n], chosen_sum[:], start=True, stop=False)
                        mmul(RB[0:n, 0:NE], upper_x[0:n, 0:n], sm(n, RSUM, NE), start=False, stop=True).then_inc(S("pos_ps"), 1)
                    yield

            def recur(t):
                n = tokens(t)
                g = grp(t)
                mid, half = (mid_p, half_p) if t < NPT else (mid_s, half_s)
                zvt, zmt = zv[0:n, t % 2, :], zm[0:n, t % 2]
                done = lambda name: pe.wait_ge(S(name), t + 1)
                for s in range(SLOTS_T):
                    if s == 0:
                        if t == 0:
                            done("consts")
                            pe.wait_ge(S("vec_loaded"), 16 * N_VEC)
                        if t == NPT:
                            pe.wait_ge(S("states_loaded"), 16 * N_STATE)
                        pe.wait_ge(S("p_copied"), use(t, "cut", NCUT - 1) + 1)
                        if t:
                            pe.wait_ge(S("hs_ready"), t)
                            pe.wait_ge(S("mlstm_state"), t)
                        for h in range(H):
                            last = tr(RA[0:HC, 128 * h:128 * h + n], zc[0:n, HC * h:HC * h + HC])
                        last.then_inc(S("ccT_ps"), 1)
                        tr(RB[0:RANK + 1, 0:n], zr[0:n, WB:WB + RANK + 1]).then_inc(S("glrT_ps"), 1)
                    if s == 1:
                        done("glrT_ready")
                        done("ccx_ready")
                        mmul(RA[0:n, 0:H * DK], glrT[:, 0:n], a2b[:], start=True, stop=True).then_inc(S("lgpre_ps"), 1)
                        for h in range(H):
                            last = tr(RB[0:HC, 128 * h:128 * h + n], zmt[:, h, 0:HC])
                        last.then_inc(S("vT_ps"), 1)
                    if s == 4:
                        done("lg_ready")
                        lgf = lg[0:n].rearrange("p h d -> p (h d)")
                        mmul(RA[0:n, 0:256], mid[0:n, 0:n], lgf, start=True, stop=True)
                        for p in range(2):
                            last = mmul(RA[:, 256 + 2 * p:258 + 2 * p], lgf[:, 128 * p:128 * p + 128], half[0:n, :], start=True, stop=True)
                        last.then_inc(S("cum_ps"), 1)
                        done("u_ready")
                        done("vT_ready")
                        if t >= 2:
                            pe.wait_ge(S("slots_ready"), t - 1)
                        for h in range(H):
                            last = mmul(RB[0:HC, 128 * h:128 * h + n], wmq[:, h, :], uT[:, h, 0:n], start=True, stop=True)
                        last.then_inc(S("qc_ps"), 1)
                    if s == 5:
                        done("dec_ready")
                        for h in range(H):
                            last = mmul(RA[0:HC, 128 * h:128 * h + n], wmk[:, h, :], uT[:, h, 0:n], start=True, stop=True)
                        last.then_inc(S("kcT_ps"), 1)
                        done("qc_ready")
                        for h in range(H):
                            last = mmul(RB[0:n, HC * h:HC * h + HC], uT[:, h, 0:n], wmk[:, h, :], start=True, stop=True)
                        last.then_inc(S("kc_ps"), 1)
                    if s == 6:
                        done("qk_ready")
                        done("kcT_ready")
                        qkf = qk[0:n].rearrange("p a h d -> p (a h d)")
                        for b in range(4):
                            last = tr(RA[:, 128 * b:128 * b + n], qkf[:, 128 * b:128 * b + 128])
                        last.then_inc(S("qkT_ps"), 1)
                        done("kc_ready")
                        srcs = [qcT, kcT, mp]
                        for b in range(3 * H):
                            last = mmul(RB[0:n, 0:8], srcs[b // H][0:HC, b % H, 0:n], wif[:, b, :], start=(b == 0), stop=(b == 3 * H - 1))
                        last.then_inc(S("gates_ps"), 1)
                    if s == 7:
                        done("qkT_ready")
                        for h in (0, 2, 1, 3):
                            b = 64 * (h % 2)
                            if h == 1:
                                step(last)
                            last = mmul(RA[0:n, 128 * h:128 * h + n], qkT[b:b + 64, 2 + h // 2, 0:n], qkT[b:b + 64, h // 2, 0:n], start=True, stop=True)
                        last.then_inc(S("att_ps"), 1)
                        done("ml_nabs")
                        for h in range(H):
                            last = mmul(RB[:, 128 * h:128 * h + n], sm(n, GATES + h).to_broadcast([n, 128]), ident[0:n, 0:n], start=True, stop=True)
                        last.then_inc(S("irow_ps"), 1)
                    if s == 8:
                        done("att_ready")
                        for h in range(H):
                            b = 64 * (h % 2)
                            last = mmul(RA[b:b + 64, DV * (h // 2):DV * (h // 2) + DV], qk[0:n, 1, h, :], zvt[:, DV * h:DV * h + DV],
                                        start=True, stop=True)
                        last.then_inc(S("gla_s_ps"), 1)
                        done("lf_ready")
                        done("irow_ready")
                        for h in range(H):
                            last = mmul(RB[:, 128 * h:128 * h + n], sm(n, LF + h).to_broadcast([n, 128]), ident[0:n, 0:n], start=True, stop=True)
                        last.then_inc(S("lfrow_ps"), 1)
                    if s == 9:
                        done("mm_ready")
                        for h in range(H):
                            last = mmul(RB[:, 128 * h:128 * h + n], sm(n, LF + h).to_broadcast([n, 128]), upper[0:n, 0:n], start=True, stop=True)
                        last.then_inc(S("frow_ps"), 1)
                        done("gS2_ready")
                        done("gla_state")
                        for h in (0, 2, 1, 3):
                            b = 64 * (h % 2)
                            if h == 1 or (n < 128 and h):
                                step(last)
                            last = mmul(RA[0:n, DV * h:DV * h + DV], att[0:n, h, 0:n], zvt[:, DV * h:DV * h + DV], start=True, stop=False)
                            if n < 128 and b:
                                step(last)
                            last = mmul(RA[0:n, DV * h:DV * h + DV], qkT[b:b + 64, h // 2, 0:n], gS2[b:b + 64, h // 2, :], start=False, stop=True)
                        last.then_inc(S("gla_o_ps"), 1)
                    if s == 11:
                        done("yb_normed")
                        mmul(RA[0:n, 0:4], upper[0:n, 0:n], sm(n, LF, H), start=True, stop=True)
                        for h in range(H):
                            last = mmul(RA[0:n, 4 + h:5 + h], mm[0:1, h, 0:n], ones[0:1, 0:1], start=True, stop=True)
                        last.then_inc(S("cols_ps"), 1)
                    if s == 12:
                        done("fm_ready")
                        for h in range(H):
                            last = mmul(RB[0:n, 128 * h:128 * h + n], kcT[:, h, 0:n], qcT[:, h, 0:n], start=True, stop=True)
                        last.then_inc(S("qk2_ps"), 1)
                    if s == 13:
                        done("p_ready")
                        done("qs_ready")
                        done("arg_ready")
                        done("mcol_exp")
                        for h in range(H):
                            o_ = RA[0:n, (HC + 1) * h:(HC + 1) * (h + 1)]
                            mmul(o_, mp[0:n, h, 0:n], zmt[:, h, :], start=True, stop=False)
                            last = mmul(o_, qcT[:, h, 0:n], cS[g][:, h, :], start=False, stop=True)
                        last.then_inc(S("num_ps"), 1)
                        for h in range(H):
                            last = mmul(RB[0:HC, (HC + 1) * h:(HC + 1) * (h + 1)], kc[0:n, h, :], zmt[:, h, :], start=True, stop=True)
                        last.then_inc(S("ml_s_ps"), 1)
                    yield

            tile_strands(attend, route, recur, project, nothing)




def first_weights(win):
    flat = [win[:, i].rearrange("p k n -> p (k n)") for i in range(3)]
    return [flat[0].rearrange("p (k f) -> p k f", k=KD), flat[1].rearrange("p (k f) -> p k f", k=KD),
            flat[2].rearrange("p (k d) -> p k d", k=FF // 128)]


def experts(nc, a, o, win, ident, ones, chosen_sum, expert, before, gatew, ps, x1_d, slot_d, eo_d, em_d):
    outer = ExitStack()
    with outer:
        at_i = outer.enter_context(nc.sbuf_tensor("at_i", [128, NT, 2], I32))
        more_i = outer.enter_context(nc.sbuf_tensor("more_i", [128, NT, 2], I32))
        w_at = outer.enter_context(nc.sbuf_tensor("w_at", [128, NT, 2], F32))
        w_more = outer.enter_context(nc.sbuf_tensor("w_more", [128, NT, 2], F32))
        xr = outer.enter_context(nc.sbuf_tensor("xr", [128, NT, D], F32))
        g2 = outer.enter_context(nc.sbuf_tensor("g2", [128, D], F32))
        b2 = outer.enter_context(nc.sbuf_tensor("b2", [128, D], F32))
        mlps(nc, a, win, ident, ones, chosen_sum, expert, before, gatew, at_i, more_i, w_at, w_more, xr, g2, b2, ps, x1_d, slot_d, eo_d, em_d)
        combine(nc, o, at_i, w_at, xr, g2, b2, eo_d)


def mlps(nc, a, win, ident, ones, chosen_sum, expert, before, gatew, at_i, more_i, w_at, w_more, xr, g2, b2, ps, x1_d, slot_d, eo_d, em_d):
    ctx = ExitStack()
    S = semaphores(nc, ctx)
    with ctx:
        def sb(name, shape, dt=F32):
            return ctx.enter_context(nc.sbuf_tensor(name, shape, dt))

        first = first_weights(win)
        wg = [first[0]] + [sb(f"wg{j}", [128, KD, FF])[:] for j in range(1, NW)]
        wu = [first[1]] + [sb(f"wu{j}", [128, KD, FF])[:] for j in range(1, NW)]
        wd = [first[2]] + [sb(f"wd{j}", [128, FF // 128, D])[:] for j in range(1, NW)]
        ids = sb("ids", [128, NW, 2], I32)
        xg = [sb(f"xg{j}", [128, 2, D]) for j in range(2)]
        xgT = sb("xgT", [128, 2, KD, CAP])
        gate = sb("gate", [128, 2, CAP])
        hT = sb("hT", [128, 2, CAP])
        rows = [sb(f"rows{j}", [128, 2, D]) for j in range(2)]
        most = sb("most", [128, NE])
        in_cap = sb("in_cap", [128, NT, 2])
        pos_f = sb("pos_f", [128, NT, 2])
        most_i = sb("most_i", [128, 1], I32)
        T = [ps[1][:, 0:512], ps[1][:, 512:1024]]
        GU = [ps[0][:, 0:512], ps[0][:, 512:1024]]
        OA, OB = ps[2], ps[3]
        wsrc = {n: a[f"w_exp_{n}"][0].rearrange("e (k p) f -> p e k f", p=128) for n in ("gate", "up", "down")}
        slots_e = slot_d.rearrange("(e s) one -> s e one", e=NE)
        rows_e = eo_d.rearrange("(e s) d -> s e d", e=NE)
        more_e = em_d.rearrange("(e s) d -> s e d", e=NE)

        def each_expert(engine, body):
            with engine.Fori(0, NE // NW - 1) as i:
                for j in range(NW):
                    body(i, j, i * NW + j, False)
            for j in range(NW):
                body(NE // NW - 1, j, NE - NW + j, j == NW - 1)

        with nc.Block() as block:
            @block.sync
            def _(sp):
                sp.sem_inc(S("ob_ps"), 1)
                sp.sem_inc(S("w_loaded0"), 48)

                def load(e, j):
                    sp.wait_ge(S("ob_ps"), e + 1)
                    for w, src in ((wg, "gate"), (wu, "up"), (wd, "down")):
                        sp.dma_start(w[j], wsrc[src][:, bass.ds(e, 1)].rearrange("p one k f -> p (one k) f")).then_inc(S(f"w_loaded{j}"), 16)

                for j in range(1, NW):
                    load(j, j)
                with sp.Fori(0, NE // NW - 1) as i:
                    for j in range(NW):
                        load(i * NW + (NW + j), j)

            @block.gpsimd
            def _(pool):
                pool.sem_inc(S("xgT_ps"), 8)
                with pool.Fori(0, NE // NW) as i:
                    for j in range(NW):
                        e = i * NW + j
                        with nc.allow_non_contiguous_dma("slot ids"):
                            pool.dma_start(ids[:, j, 0:1], slots_e[0:128, bass.ds(e, 1), 0]).then_inc(S(f"ids_loaded{j}"), 16)
                            pool.dma_start(ids[0:CB, j, 1:2], slots_e[128:CAP, bass.ds(e, 1), 0]).then_inc(S(f"ids_loaded{j}"), 16)
                        pool.wait_ge(S(f"ids_loaded{j}"), i * 32 + 32)
                        pool.sem_inc(S("pool_passed"), 1)
                        pool.wait_ge(S("xgT_ps"), e * 4 + 4)
                        pool.sem_inc(S("pool_passed"), 1)
                        for b, nb in ((0, 128), (1, CB)):
                            pool.indirect_dma_start(
                                out=xg[j % 2][0:nb, b, :], out_offset=None, in_=x1_d,
                                in_offset=bass.IndirectOffsetOnAxis(ap=ids[0:nb, j, b:b + 1], axis=0)).then_inc(S(f"xg_loaded{j % 2}"), 16)
                pool.dma_start(xr[:, 0:NPT, :], x1_d[0:SEQ].rearrange("(t p) d -> p t d", p=128)).then_inc(S("xr_loaded"), 16)
                pool.dma_start(xr[0:SMP, NPT, :], x1_d[SEQ:TOKENS]).then_inc(S("xr_loaded"), 16)
                pool.dma_start(g2[:], a["ln2_g"][0].partition_broadcast(128)).then_inc(S("xr_loaded"), 16)
                pool.dma_start(b2[:], a["ln2_b"][0].partition_broadcast(128)).then_inc(S("xr_loaded"), 16)
                pool.wait_ge(S("xr_loaded"), 64)
                for t in range(NT):
                    x = xr[0:tokens(t), t, :]
                    nc.gpsimd.tensor_scalar(x, x, ALPHA, None, ALU.mult)

            @block.scalar
            def _(act):
                A = nc.scalar
                act.sem_inc(S("xgT_copied"), 2)
                act.sem_inc(S("gu_ps"), 2)
                for p in range(2):
                    act.sem_inc(S(f"rows_stored{p}"), 32)
                act.sem_inc(S("oa_copied"), 1)
                def turned(e, j):
                    for u in range(4):
                        act.wait_ge(S("xgT_ps"), e * 4 + (u + 9))
                        A.activation(xgT[:, j % 2, 2 * u:2 * u + 2, :], T[u % 2][:, 0:2 * CAP].rearrange("p (k n) -> p k n", k=2),
                                     ACT.Copy).then_inc(S("xgT_copied"), 1)

                def body(i, j, e, last):
                    for f in range(2):
                        act.wait_ge(S("gu_ps"), e * 2 + (f + 3))
                        act.wait_ge(S("h_ready"), e * 2 + (f + 1))
                        A.activation(gate[:, f, :], GU[f][:, 0:CAP], ACT.Silu).then_inc(S("gate_ready"), 1)
                    if not last:
                        turned(e + 1, j + 1)
                    act.wait_ge(S("oa_ps"), e + 1)
                    act.wait_ge(S(f"rows_stored{j % 2}"), i * (16 * NW) + 32 * (j // 2 + 1))
                    A.activation(rows[j % 2][:, 0, :], OA[:], ACT.Copy).then_inc(S("oa_copied"), 1)
                    act.wait_ge(S("oa_copied"), e + 2)
                    act.dma_start(rows_e[0:128, bass.ds(e, 1), :].rearrange("s one d -> s (one d)"), rows[j % 2][:, 0, :]).then_inc(S(f"rows_stored{j % 2}"), 16)
                    act.wait_ge(S("ob_copied"), e + 2)
                    act.dma_start(rows_e[128:CAP, bass.ds(e, 1), :].rearrange("s one d -> s (one d)"), rows[j % 2][0:CB, 1, :]).then_inc(S(f"rows_stored{j % 2}"), 16)

                turned(0, 0)
                act.wait_ge(S("xg_loaded1"), 32)
                act.sem_inc(S("ob_ps"), NW - 1)
                each_expert(act, body)
                for p in range(2):
                    act.wait_ge(S(f"rows_stored{p}"), 32 + 32 * NE // 2)

            @block.vector
            def _(dve):
                V = nc.vector
                dve.sem_inc(S("h_ready"), 2)
                dve.sem_inc(S("ob_copied"), 1)
                dve.wait_ge(S("counts_ps"), 1)
                V.tensor_reduce(most[:, 0:1], OB[:, 0:NE], AX.X, ALU.max).then_inc(S("most_ready"), 1)
                dve.wait_ge(S("most_ready"), 1)
                V.tensor_copy(most_i[:], most[:, 0:1]).then_inc(S("most_ready"), 1)
                n_step = [0]

                def step(ins):
                    n_step[0] += 1
                    ins.then_inc(S("place_step"), 1)
                    dve.wait_ge(S("place_step"), n_step[0])

                step(V.tensor_scalar(in_cap[:], before[:], float(CAP), None, ALU.is_lt))
                step(V.scalar_tensor_tensor(out=pos_f[:], in0=expert[:], scalar=float(CAP), in1=before[:], op0=ALU.mult, op1=ALU.add))
                step(V.tensor_tensor(pos_f[:], pos_f[:], in_cap[:], ALU.mult))
                step(V.tensor_copy(at_i[:], pos_f[:]))
                step(V.tensor_tensor(w_at[:], gatew[:], in_cap[:], ALU.mult))
                V.tensor_tensor(w_more[:], gatew[:], w_at[:], ALU.subtract)
                step(V.tensor_scalar(in_cap[:], before[:], float(CAP), None, ALU.is_ge))
                step(V.scalar_tensor_tensor(out=pos_f[:], in0=expert[:], scalar=float(128 * MORE), in1=before[:], op0=ALU.mult, op1=ALU.add))
                step(V.tensor_scalar(pos_f[:], pos_f[:], -float(CAP), None, ALU.add))
                step(V.tensor_tensor(pos_f[:], pos_f[:], in_cap[:], ALU.mult))
                step(V.tensor_copy(more_i[:], pos_f[:]))
                with dve.Fori(0, NE // NW) as i:
                    for j in range(NW):
                        e = i * NW + j
                        for f in range(2):
                            dve.wait_ge(S("gate_ready"), e * 2 + (f + 1))
                            if f == 0:
                                dve.wait_ge(S("ob_ps"), e + NW)
                            V.tensor_tensor(hT[:, f, :], gate[:, f, :], GU[f][:, CAP:2 * CAP], ALU.mult).then_inc(S("h_ready"), 1)
                        dve.wait_ge(S("ob_ps"), e + (NW + 1))
                        dve.wait_ge(S(f"rows_stored{j % 2}"), i * (16 * NW) + 32 * (j // 2 + 1))
                        V.tensor_copy(rows[j % 2][0:CB, 1, :], OB[0:CB, :]).then_inc(S("ob_copied"), 1)

            @block.tensor
            def _(pe):
                E = nc.tensor
                E.matmul(OB[:, 0:NE], ones[:], chosen_sum[:], start=True, stop=True).then_inc(S("counts_ps"), 1)
                pe.wait_ge(S("most_ready"), 2)

                def turn(e, j, loaded):
                    pe.wait_ge(S(f"xg_loaded{j % 2}"), loaded)
                    for u in range(4):
                        pe.wait_ge(S("xgT_copied"), e * 4 + (u + 1))
                        for k in (2 * u, 2 * u + 1):
                            c = CAP * (k % 2)
                            E.transpose(T[u % 2][:, c:c + 128], xg[j % 2][:, 0, 128 * k:128 * k + 128], ident[:])
                            last = E.transpose(T[u % 2][:, c + 128:c + CAP], xg[j % 2][0:CB, 1, 128 * k:128 * k + 128], ident[0:CB, 0:CB])
                        last.then_inc(S("xgT_ps"), 1)

                def body(i, j, e, last_one):
                    pe.wait_ge(S(f"w_loaded{j}"), i * 48 + 48)
                    pe.wait_ge(S("xgT_copied"), e * 4 + 6)
                    for f in range(2):
                        pe.wait_ge(S("h_ready"), e * 2 + (f + 1))
                        for m, w in ((0, wg[j]), (1, wu[j])):
                            for k in range(KD):
                                last = E.matmul(GU[f][:, CAP * m:CAP * m + CAP], w[:, k, 128 * f:128 * f + 128], xgT[:, j % 2, k, :],
                                                start=(k == 0), stop=(k == KD - 1))
                        last.then_inc(S("gu_ps"), 1)
                    if not last_one:
                        turn(e + 1, j + 1, i * (16 * NW) + 32 * ((j + 1) // 2 + 1))
                    for f in range(2):
                        pe.wait_ge(S("h_ready"), e * 2 + (f + 3))
                        for out, c0, nb, sem in ((OA, 0, 128, "oa"), (OB, 128, CB, "ob")):
                            if f == 0:
                                pe.wait_ge(S(sem + "_copied"), e + 1)
                            for c in range(2):
                                last = E.matmul(out[0:nb, 512 * c:512 * c + 512], hT[:, f, c0:c0 + nb], wd[j][:, f, 512 * c:512 * c + 512],
                                                start=(f == 0), stop=(f == 1))
                            if f == 1:
                                last.then_inc(S(sem + "_ps"), 1)

                turn(0, 0, 32)
                each_expert(pe, body)

        with nc.Block() as block:
            F = lambda name: S("more_" + name)

            @block.sync
            def _(sp):
                sp.sem_inc(F("o_ps"), 1)
                n_most = sp.value_load(most_i[0:1, 0:1])
                with sp.If(n_most > CAP):
                    with sp.Fori(0, NE) as e:
                        sp.wait_ge(F("o_ps"), e * MORE + 1)
                        for w, src in ((wg, "gate"), (wu, "up"), (wd, "down")):
                            sp.dma_start(w[0], wsrc[src][:, bass.ds(e, 1)].rearrange("p one k f -> p (one k) f")).then_inc(F("w_loaded"), 16)
                        with sp.Fori(0, MORE) as b:
                            q = e * MORE + b
                            sp.wait_ge(F("o_ps"), q + 1)
                            with nc.allow_non_contiguous_dma("slot ids"):
                                sp.dma_start(ids[:, 0, 0:1], slots_e[bass.ds(b * 128 + CAP, 128), bass.ds(e, 1), 0]).then_inc(F("ids_loaded"), 16)
                            sp.wait_ge(F("rows_ready"), q * 2 + 2)
                            sp.dma_start(more_e[bass.ds(b * 128, 128), bass.ds(e, 1), :].rearrange("s one d -> s (one d)"),
                                         rows[0][:, 0, :]).then_inc(F("stored"), 16)
                    sp.wait_ge(F("stored"), 16 * (NE * MORE + 1))
                    sp.sem_inc(F("all_stored"), 1)

            @block.gpsimd
            def _(pool):
                n_most = pool.value_load(most_i[0:1, 0:1])
                with pool.If(n_most > CAP):
                    with pool.Fori(0, NE * MORE) as q:
                        pool.wait_ge(F("ids_loaded"), q * 16 + 16)
                        pool.sem_inc(S("pool_passed"), 1)
                        pool.indirect_dma_start(out=xg[0][:, 0, :], out_offset=None, in_=x1_d,
                                                in_offset=bass.IndirectOffsetOnAxis(ap=ids[:, 0, 0:1], axis=0)).then_inc(F("xg_loaded"), 16)
                    pool.wait_ge(F("all_stored"), 1)
                    for t in range(NT):
                        n = tokens(t)
                        if t:
                            pool.wait_ge(F("x1_added"), 2 * t)
                        for k in range(2):
                            pool.indirect_dma_start(out=xg[k][0:n, 0, :], out_offset=None, in_=em_d,
                                                    in_offset=bass.IndirectOffsetOnAxis(ap=more_i[0:n, t, k:k + 1], axis=0)).then_inc(
                                                        F("r_loaded"), 16)

            @block.scalar
            def _(act):
                A = nc.scalar
                n_most = act.value_load(most_i[0:1, 0:1])
                with act.If(n_most > CAP):
                    with act.Fori(0, NE * MORE) as q:
                        for u in range(2):
                            act.wait_ge(F("xgT_ps"), q * 2 + (u + 1))
                            A.activation(xgT[:, 0, 4 * u:4 * u + 4, 0:128], T[u].rearrange("p (k n) -> p k n", k=4), ACT.Copy).then_inc(F("xgT_copied"), 1)
                        act.wait_ge(F("gu_ps"), q + 1)
                        for f in range(2):
                            A.activation(hT[:, f, 0:128], GU[f][:, 0:128], ACT.Silu).then_inc(F("gate_ready"), 1)

            @block.vector
            def _(dve):
                V = nc.vector
                dve.sem_inc(F("stored"), 16)
                n_most = dve.value_load(most_i[0:1, 0:1])
                with dve.If(n_most > CAP):
                    with dve.Fori(0, NE * MORE) as q:
                        dve.wait_ge(F("gate_ready"), q * 2 + 2)
                        for f in range(2):
                            V.tensor_tensor(hT[:, f, 0:128], hT[:, f, 0:128], GU[f][:, 128:256], ALU.mult).then_inc(F("h_ready"), 1)
                        dve.wait_ge(F("o_ps"), q + 2)
                        dve.wait_ge(F("stored"), q * 16 + 16)
                        for c in range(2):
                            V.tensor_copy(rows[0][:, 0, 512 * c:512 * c + 512], OA[:, 512 * c:512 * c + 512]).then_inc(F("rows_ready"), 1)
                    for t in range(NT):
                        n = tokens(t)
                        dve.wait_ge(F("r_loaded"), 32 * (t + 1))
                        for k in range(2):
                            x = xr[0:n, t, :]
                            V.scalar_tensor_tensor(out=x, in0=xg[k][0:n, 0, :], scalar=w_more[0:n, t, k:k + 1], in1=x, op0=ALU.mult,
                                                   op1=ALU.add).then_inc(F("x1_added"), 1)
                            dve.wait_ge(F("x1_added"), 2 * t + k + 1)

            @block.tensor
            def _(pe):
                E = nc.tensor
                n_most = pe.value_load(most_i[0:1, 0:1])
                with pe.If(n_most > CAP):
                    with pe.Fori(0, NE) as e:
                        pe.wait_ge(F("w_loaded"), e * 48 + 48)
                        pe.sem_inc(S("pe_passed"), 1)
                        with pe.Fori(0, MORE) as b:
                            q = e * MORE + b
                            pe.wait_ge(F("xg_loaded"), q * 16 + 16)
                            for u in range(2):
                                for k in range(4 * u, 4 * u + 4):
                                    last = E.transpose(T[u][:, 128 * (k % 4):128 * (k % 4) + 128], xg[0][:, 0, 128 * k:128 * k + 128], ident[:])
                                last.then_inc(F("xgT_ps"), 1)
                            pe.wait_ge(F("xgT_copied"), q * 2 + 2)
                            for f in range(2):
                                for m, w in ((0, wg[0]), (1, wu[0])):
                                    for k in range(KD):
                                        last = E.matmul(GU[f][:, 128 * m:128 * m + 128], w[:, k, 128 * f:128 * f + 128], xgT[:, 0, k, 0:128],
                                                        start=(k == 0), stop=(k == KD - 1))
                            last.then_inc(F("gu_ps"), 1)
                            pe.wait_ge(F("h_ready"), q * 2 + 2)
                            for c in range(2):
                                for f in range(2):
                                    last = E.matmul(OA[:, 512 * c:512 * c + 512], hT[:, f, 0:128], wd[0][:, f, 512 * c:512 * c + 512],
                                                    start=(f == 0), stop=(f == 1))
                            last.then_inc(F("o_ps"), 1)
                            pe.wait_ge(F("rows_ready"), q * 2 + 2)
                            pe.sem_inc(S("pe_passed"), 1)


def combine(nc, o, at_i, w_at, xr, g2, b2, eo_d):
    ctx = ExitStack()
    S = semaphores(nc, ctx)
    AHEAD = 3
    LAG = 3
    with ctx:
        def sb(name, shape, dt=F32):
            return ctx.enter_context(nc.sbuf_tensor(name, shape, dt))

        r = [sb(f"r{k}", [128, NT, D]) for k in range(2)]
        st = sb("st", [128, NT, 16])
        half = sb("half", [128, 1])
        block = ctx.enter_context(nc.Block())

        @block.sync
        def _(sp):
            for t in range(NT):
                n = tokens(t)
                sp.wait_ge(S("y_ready"), t + 1)
                dst = o["y_p"][0, 128 * t:128 * t + n] if t < NPT else o["y_s"][0]
                sp.dma_start(dst, xr[0:n, t, :]).then_inc(S("y_stored"), 16)
            sp.wait_ge(S("y_stored"), 16 * NT)

        @block.gpsimd
        def _(pool):
            G = nc.gpsimd
            n_step = [0]

            def step(ins):
                n_step[0] += 1
                ins.then_inc(S("pool2_step"), 1)
                pool.wait_ge(S("pool2_step"), n_step[0])

            def gather(t):
                n = tokens(t)
                for k in range(2):
                    pool.indirect_dma_start(out=r[k][0:n, t, :], out_offset=None, in_=eo_d,
                                            in_offset=bass.IndirectOffsetOnAxis(ap=at_i[0:n, t, k:k + 1], axis=0)).then_inc(
                                                S(f"r_loaded{t}_{k}"), 16)

            for t in range(AHEAD):
                gather(t)
            step(G.memset(half[:], -0.5))
            for t in range(NT + 1):
                if t + AHEAD < NT:
                    gather(t + AHEAD)
                if t < NT:
                    n = tokens(t)
                    pool.wait_ge(S("ln2_stats"), t + 1)
                    step(G.tensor_tensor(st[0:n, t, 14:15], st[0:n, t, 13:14], half[0:n], ALU.pow))
                    G.tensor_scalar(st[0:n, t, 15:16], st[0:n, t, 12:13], st[0:n, t, 14:15], -1.0, ALU.mult, ALU.mult).then_inc(S("ln2_scale"), 1)
                if t >= 1:
                    x = xr[0:tokens(t - 1), t - 1, :]
                    pool.wait_ge(S("y_normed"), t)
                    G.tensor_tensor(x, x, g2[0:tokens(t - 1)], ALU.mult).then_inc(S("y_gained"), 1)

        @block.scalar
        def _(act):
            for t in range(NT):
                n = tokens(t)
                x = xr[0:n, t, :]
                act.wait_ge(S("ln2_scale"), t + 1)
                nc.scalar.activation(x, x, ACT.Identity, bias=st[0:n, t, 15:16], scale=st[0:n, t, 14:15]).then_inc(S("y_normed"), 1)

        @block.vector
        def _(dve):
            V = nc.vector
            n_step = [0]

            def step(ins):
                n_step[0] += 1
                ins.then_inc(S("dve2_step"), 1)
                dve.wait_ge(S("dve2_step"), n_step[0])

            for t in range(NT + LAG):
                if t < NT:
                    n = tokens(t)
                    x = xr[0:n, t, :]
                    for k in range(2):
                        dve.wait_ge(S(f"r_loaded{t}_{k}"), 16)
                        step(V.scalar_tensor_tensor(out=x, in0=r[k][0:n, t, :], scalar=w_at[0:n, t, k:k + 1], in1=x, op0=ALU.mult, op1=ALU.add))
                    V.bn_stats(st[0:n, t, 0:6], x[:, 0:512])
                    step(V.bn_stats(st[0:n, t, 6:12], x[:, 512:1024]))
                    step(V.bn_aggr(st[0:n, t, 12:14], st[0:n, t, 0:12].rearrange("p (a b) -> p a b", a=2)))
                    V.tensor_scalar(st[0:n, t, 13:14], st[0:n, t, 13:14], EPS, None, ALU.add).then_inc(S("ln2_stats"), 1)
                if t >= LAG:
                    x = xr[0:tokens(t - LAG), t - LAG, :]
                    dve.wait_ge(S("y_gained"), t - LAG + 1)
                    V.tensor_tensor(x, x, b2[0:tokens(t - LAG)], ALU.add).then_inc(S("y_ready"), 1)

        @block.tensor
        def _(pe):
            pass


INS = ['x_prompt', 'x_sample', 'cache_k', 'cache_v', 'cache_kidx', 'state_gla', 'state_mlstm_C', 'state_mlstm_n',
       'state_mlstm_m', 'state_conv', 'ln0_g', 'ln0_b', 'w_in', 'w_gla_a2', 'b_gla_a', 'g_gla', 'conv_w', 'conv_b',
       'w_mq', 'w_mk', 'w_if', 'b_if', 'g_mlstm', 'w_out', 'ln1_g', 'ln1_b', 'w_router', 'b_router', 'w_exp_gate',
       'w_exp_up', 'w_exp_down', 'ln2_g', 'ln2_b']


def _group(g, b, s):
    return [(f"k_{g}", (1, b, s, H, HA)), (f"v_{g}", (1, b, s, H, HA)), (f"kidx_{g}", (1, b, s, DI)),
            (f"gla_{g}", (1, b, H, DK, DV)), (f"mC_{g}", (1, b, H, HC, HC)), (f"mn_{g}", (1, b, H, HC)),
            (f"mm_{g}", (1, b, H)), (f"conv_{g}", (1, b, CW - 1, WC))]


OUTS = [("y_p", (1, SEQ, D)), ("y_s", (1, SMP, D))] + _group("p", 1, SEQ) + _group("s", 1, SMP)


def kernel(**inputs):
    import numpy as np
    import concourse.bacc as bacc
    from concourse.bass_utils import run_bass_kernel_spmd

    nc = bacc.Bacc("TRN2", target_bir_lowering=False, num_devices=1)
    arrays, ins, outs = {}, {}, {}
    for name in INS:
        arr = np.ascontiguousarray(inputs[name])
        arrays[f"in_{name}"] = arr
        ins[name] = nc.dram_tensor(f"in_{name}", arr.shape, mybir.dt.from_np(arr.dtype), kind="ExternalInput").ap()
    for name, shape in OUTS:
        outs[name] = nc.dram_tensor(f"out_{name}", shape, F32, kind="ExternalOutput").ap()
    build(nc, ins, outs)
    r = run_bass_kernel_spmd(nc, [arrays], core_ids=[0])
    return tuple(r.results[0][f"out_{name}"] for name, _ in OUTS)
```
